# Optimizing a Trainium2 kernel written in Bass

```python
import math
import jax, jax.numpy as jnp
from jax import lax
import numpy as np

D_MODEL = 1024
BATCH = 1
SEQ = 512
DEPTH = 2

M_HEADS = 4
M_QK_DIM = 128
M_V_DIM = 256
M_QK_WIDTH = M_HEADS * M_QK_DIM
M_V_WIDTH = M_HEADS * M_V_DIM
M_CHUNK = 64
CONV_K = 4
A_Q_HEADS = 16
A_KV_HEADS = 4
A_HEAD_DIM = 64
A_GROUP = A_Q_HEADS // A_KV_HEADS
A_Q_WIDTH = A_Q_HEADS * A_HEAD_DIM
A_KV_WIDTH = A_KV_HEADS * A_HEAD_DIM
WINDOW = 128
N_BUCKETS = 32
MAX_DISTANCE = 128
D_FF = 4 * D_MODEL
EPS = 1e-6

IN_SIZES = (2 * M_QK_WIDTH, M_V_WIDTH, M_V_WIDTH, M_HEADS, M_HEADS,
            A_Q_WIDTH, A_KV_WIDTH, A_KV_WIDTH, D_MODEL, D_MODEL)
N_IN = sum(IN_SIZES)


def rmsnorm(x, g):
    xf = x.astype(jnp.float32)
    y = xf * lax.rsqrt(jnp.mean(xf * xf, axis=-1, keepdims=True) + EPS)
    return (y * g.astype(jnp.float32)).astype(x.dtype)

def t5_bucket(n):
    max_exact = N_BUCKETS // 2
    n = np.maximum(n, 0)
    large = max_exact + (np.log(np.maximum(n, 1) / max_exact)
                         / np.log(MAX_DISTANCE / max_exact)
                         * (N_BUCKETS - max_exact)).astype(np.int32)
    large = np.minimum(large, N_BUCKETS - 1)
    return np.where(n < max_exact, n, large).astype(np.int32)

def causal_conv(x, w, b):
    S = x.shape[1]
    xp = jnp.pad(x, ((0, 0), (CONV_K - 1, 0), (0, 0)))
    y = b
    for j in range(CONV_K):
        y = y + xp[:, j:j + S] * w[j]
    return y

def mlstm_chunkwise(q, k, v, ig, logf):
    B, S, H, dk = q.shape
    dv = v.shape[-1]
    L = M_CHUNK
    NC = S // L

    def chunks4(t):
        return t.reshape(B, NC, L, H, t.shape[-1]).transpose(1, 0, 3, 2, 4)

    def chunks3(t):
        return t.reshape(B, NC, L, H).transpose(1, 0, 3, 2)

    tril = jnp.tril(jnp.ones((L, L), dtype=bool))

    def step(carry, xs):
        C, n, m = carry
        qc, kc, vc, ic, fc = xs
        b = jnp.cumsum(fc, axis=-1)
        dmat = jnp.where(tril, b[..., :, None] - b[..., None, :] + ic[..., None, :], -jnp.inf)
        m_inter = b + m[..., None]
        m_comb = jnp.maximum(m_inter, jnp.max(dmat, axis=-1))
        w_intra = jnp.exp(dmat - m_comb[..., None])
        w_inter = jnp.exp(m_inter - m_comb)
        s = jnp.einsum('bhld,bhsd->bhls', qc, kc) * w_intra
        num = (jnp.einsum('bhls,bhsv->bhlv', s, vc)
               + w_inter[..., None] * jnp.einsum('bhld,bhdv->bhlv', qc, C))
        den = jnp.sum(s, axis=-1) + w_inter * jnp.einsum('bhld,bhd->bhl', qc, n)
        h = num / jnp.maximum(jnp.abs(den), jnp.exp(-m_comb))[..., None]
        bL = b[..., -1]
        g = bL[..., None] - b + ic
        m_new = jnp.maximum(bL + m, jnp.max(g, axis=-1))
        decay = jnp.exp(bL + m - m_new)
        wk = jnp.exp(g - m_new[..., None])
        C_new = decay[..., None, None] * C + jnp.einsum('bhl,bhld,bhlv->bhdv', wk, kc, vc)
        n_new = decay[..., None] * n + jnp.einsum('bhl,bhld->bhd', wk, kc)
        return (C_new, n_new, m_new), h

    init = (jnp.zeros((B, H, dk, dv), jnp.float32),
            jnp.zeros((B, H, dk), jnp.float32),
            jnp.zeros((B, H), jnp.float32))
    _, hs = lax.scan(step, init, (chunks4(q), chunks4(k), chunks4(v), chunks3(ig), chunks3(logf)))
    return hs.transpose(1, 0, 3, 2, 4).reshape(B, S, H, dv)

def sliding_window_attention(q, k, v, sinks, rel_bias):
    B, S = q.shape[:2]
    W = WINDOW
    NB = S // W
    qb = q.astype(jnp.float32).reshape(B, NB, W, A_KV_HEADS, A_GROUP, A_HEAD_DIM)
    kb = k.astype(jnp.float32).reshape(B, NB, W, A_KV_HEADS, A_HEAD_DIM)
    vb = v.astype(jnp.float32).reshape(B, NB, W, A_KV_HEADS, A_HEAD_DIM)

    def with_prev(t):
        prev = jnp.concatenate([jnp.zeros_like(t[:, :1]), t[:, :-1]], axis=1)
        return jnp.concatenate([prev, t], axis=2)

    k_ctx, v_ctx = with_prev(kb), with_prev(vb)
    scores = jnp.einsum('bnqhgd,bnkhd->bnhgqk', qb, k_ctx) * (A_HEAD_DIM ** -0.5)

    dist = np.arange(W)[:, None] + W - np.arange(2 * W)[None, :]
    bias = rel_bias.astype(jnp.float32)[t5_bucket(dist)]
    bias = bias.transpose(2, 0, 1).reshape(A_KV_HEADS, A_GROUP, W, 2 * W)
    valid_rel = jnp.asarray((dist >= 0) & (dist < W))
    kpos = jnp.arange(NB)[:, None, None] * W - W + jnp.arange(2 * W)[None, None, :]
    valid = valid_rel[None] & (kpos >= 0)
    logits = jnp.where(valid[None, :, None, None], scores + bias, -jnp.inf)

    sink = sinks.astype(jnp.float32).reshape(A_KV_HEADS, A_GROUP, 1)
    m = jnp.maximum(jnp.max(logits, axis=-1), sink)
    p = jnp.exp(logits - m[..., None])
    denom = jnp.sum(p, axis=-1) + jnp.exp(sink - m)
    out = jnp.einsum('bnhgqk,bnkhd->bnqhgd', p / denom[..., None], v_ctx)
    return out.reshape(B, S, A_Q_WIDTH).astype(q.dtype)

def mixer_block(h, w_in, conv_w, conv_b, b_igate, b_fgate, mlstm_norm_g, sinks,
                rel_bias, w_branch_m, w_branch_a, w_out):
    B, S, _ = h.shape
    proj = h @ w_in
    offsets = [int(o) for o in np.cumsum(IN_SIZES)[:-1]]
    mqk, mv, mo, mi, mf, aq, ak, av, ga, gb = jnp.split(proj, offsets, axis=-1)

    mqk = jax.nn.silu(causal_conv(mqk, conv_w, conv_b))
    mq, mk = jnp.split(mqk.astype(jnp.float32), 2, axis=-1)
    mq = mq.reshape(B, S, M_HEADS, M_QK_DIM) * (M_QK_DIM ** -0.5)
    mk = mk.reshape(B, S, M_HEADS, M_QK_DIM)
    mvf = mv.astype(jnp.float32).reshape(B, S, M_HEADS, M_V_DIM)
    ig = mi.astype(jnp.float32) + b_igate.astype(jnp.float32)
    logf = jax.nn.log_sigmoid(mf.astype(jnp.float32) + b_fgate.astype(jnp.float32))
    hm = mlstm_chunkwise(mq, mk, mvf, ig, logf)
    hm = hm * lax.rsqrt(jnp.mean(hm * hm, axis=-1, keepdims=True) + EPS)
    hm = hm * mlstm_norm_g.astype(jnp.float32).reshape(M_HEADS, M_V_DIM)
    hm = (hm.reshape(B, S, M_V_WIDTH) * jax.nn.sigmoid(mo.astype(jnp.float32))).astype(h.dtype)

    ha = sliding_window_attention(aq.reshape(B, S, A_Q_HEADS, A_HEAD_DIM),
                                  ak.reshape(B, S, A_KV_HEADS, A_HEAD_DIM),
                                  av.reshape(B, S, A_KV_HEADS, A_HEAD_DIM),
                                  sinks, rel_bias)

    y = jax.nn.sigmoid(ga) * (hm @ w_branch_m) + jax.nn.sigmoid(gb) * (ha @ w_branch_a)
    return y @ w_out

def sqrelu_mlp(h, w_up, w_down):
    return jnp.square(jax.nn.relu(h @ w_up)) @ w_down

def first_inputs(seed: int = 0) -> dict:
    key = jax.random.key(seed)
    ks = jax.random.split(key, 20)
    f32 = jnp.float32
    nrm = lambda k, shape, s: jax.random.normal(k, shape, f32) * s
    return {
        "x": nrm(ks[0], (BATCH, SEQ, D_MODEL), 1.0),
        "norm_mix_g": 1.0 + nrm(ks[1], (DEPTH, D_MODEL), 0.05),
        "w_in": nrm(ks[2], (DEPTH, D_MODEL, N_IN), D_MODEL ** -0.5),
        "conv_w": nrm(ks[3], (DEPTH, CONV_K, 2 * M_QK_WIDTH), CONV_K ** -0.5),
        "conv_b": nrm(ks[4], (DEPTH, 2 * M_QK_WIDTH), 0.02),
        "b_igate": nrm(ks[5], (DEPTH, M_HEADS), 0.1),
        "b_fgate": jnp.linspace(3.0, 6.0, M_HEADS, dtype=f32)[None] + nrm(ks[6], (DEPTH, M_HEADS), 0.1),
        "mlstm_norm_g": 1.0 + nrm(ks[7], (DEPTH, M_V_WIDTH), 0.05),
        "attn_sinks": nrm(ks[8], (DEPTH, A_Q_HEADS), 0.5),
        "rel_bias": nrm(ks[9], (N_BUCKETS, A_Q_HEADS), 0.5),
        "w_branch_m": nrm(ks[10], (DEPTH, M_V_WIDTH, D_MODEL), M_V_WIDTH ** -0.5),
        "w_branch_a": nrm(ks[11], (DEPTH, A_Q_WIDTH, D_MODEL), A_Q_WIDTH ** -0.5),
        "w_out": nrm(ks[12], (DEPTH, D_MODEL, D_MODEL), D_MODEL ** -0.5),
        "norm_mlp_g": 1.0 + nrm(ks[13], (DEPTH, D_MODEL), 0.05),
        "w_up": nrm(ks[14], (DEPTH, D_MODEL, D_FF), D_MODEL ** -0.5),
        "w_down": nrm(ks[15], (DEPTH, D_FF, D_MODEL), D_FF ** -0.5),
        "final_norm_g": 1.0 + nrm(ks[16], (D_MODEL,), 0.05),
    }

def first_block(x, norm_mix_g, w_in, conv_w, conv_b, b_igate, b_fgate, mlstm_norm_g,
              attn_sinks, rel_bias, w_branch_m, w_branch_a, w_out, norm_mlp_g,
              w_up, w_down, final_norm_g):
    for l in range(DEPTH):
        h = rmsnorm(x, norm_mix_g[l])
        x = x + mixer_block(h, w_in[l], conv_w[l], conv_b[l], b_igate[l], b_fgate[l],
                            mlstm_norm_g[l], attn_sinks[l], rel_bias,
                            w_branch_m[l], w_branch_a[l], w_out[l])
        h = rmsnorm(x, norm_mlp_g[l])
        x = x + sqrelu_mlp(h, w_up[l], w_down[l])
    return rmsnorm(x, final_norm_g)


DEPTH_2 = 1

N_MIXERS = 2
RMS_EPS = 1e-6
GN_EPS = 1e-6
NEG_INF = -1e30

NSA_HEADS = 16
NSA_HEAD_DIM = 64
NSA_KV_GROUPS = 4
NSA_Q_PER_GROUP = NSA_HEADS // NSA_KV_GROUPS
NSA_WIDTH = NSA_HEADS * NSA_HEAD_DIM
NSA_KV_WIDTH = NSA_KV_GROUPS * NSA_HEAD_DIM
CMP_BLOCK = 32
CMP_STRIDE = 16
CMP_HIDDEN = 256
SLC_BLOCK = 64
SLC_TOPN = 16
SLC_Q_BLOCK = 32
WIN_SIZE = 512
WIN_Q_BLOCK = 128
FORCED_SCORE = 1e3
NSA_PROJ = NSA_WIDTH + 6 * NSA_KV_WIDTH + 3 * NSA_HEADS + 3 * NSA_WIDTH

REL_BUCKETS = 32
REL_MAX_DIST = 128

RET_HEADS = 4
RET_QK_DIM = 256
RET_V_DIM = 512
RET_QK_WIDTH = RET_HEADS * RET_QK_DIM
RET_WIDTH = RET_HEADS * RET_V_DIM
RET_CHUNK = 128
ROPE_BASE = 10000.0
RET_PROJ = 2 * RET_QK_WIDTH + 2 * RET_WIDTH


def rms_norm(x, gain):
    xf = x.astype(jnp.float32)
    y = xf * lax.rsqrt(jnp.mean(xf * xf, axis=-1, keepdims=True) + RMS_EPS)
    return (y * gain.astype(jnp.float32)).astype(x.dtype)

def split_cols(a, sizes):
    return jnp.split(a, list(np.cumsum(sizes)[:-1]), axis=-1)

def masked_softmax(logits, mask):
    p = jax.nn.softmax(jnp.where(mask, logits, NEG_INF), axis=-1)
    return jnp.where(mask, p, 0.0)

def t5_bucket_2(dist):
    n = jnp.maximum(dist, 0)
    max_exact = REL_BUCKETS // 2
    nf = jnp.maximum(n, 1).astype(jnp.float32)
    large = max_exact + (jnp.log(nf / max_exact) / math.log(REL_MAX_DIST / max_exact)
                         * (REL_BUCKETS - max_exact)).astype(jnp.int32)
    large = jnp.minimum(large, REL_BUCKETS - 1)
    return jnp.where(n < max_exact, n, large)

def compress_kv(kv, pos, w1, w2):
    B, S, G, dh = kv.shape
    n_cmp = (S - CMP_BLOCK) // CMP_STRIDE + 1
    idx = jnp.arange(n_cmp)[:, None] * CMP_STRIDE + jnp.arange(CMP_BLOCK)[None, :]
    blocks = kv[:, idx] + pos[None, None, :, None, :].astype(kv.dtype)
    flat = blocks.transpose(0, 1, 3, 2, 4).reshape(B, n_cmp, G, CMP_BLOCK * dh)
    return jax.nn.silu(flat @ w1) @ w2

def nsa_compressed(q, kc, vc, table):
    B, S, H, dh = q.shape
    n_cmp = kc.shape[1]
    qg = q.reshape(B, S, NSA_KV_GROUPS, NSA_Q_PER_GROUP, dh)
    logits = jnp.einsum('bsgrd,bcgd->bgrsc', qg, kc).astype(jnp.float32) * (dh ** -0.5)
    t = jnp.arange(S)
    end = jnp.arange(n_cmp) * CMP_STRIDE + CMP_BLOCK - 1
    dist = t[:, None] - end[None, :]
    bias = table[t5_bucket_2(dist)].astype(jnp.float32)
    bias = bias.reshape(S, n_cmp, NSA_KV_GROUPS, NSA_Q_PER_GROUP).transpose(2, 3, 0, 1)
    p = masked_softmax(logits + bias, dist >= 0)
    o = jnp.einsum('bgrsc,bcgd->bsgrd', p.astype(vc.dtype), vc).reshape(B, S, H, dh)
    return o, p

def select_blocks(p_cmp, S):
    n_cmp = p_cmp.shape[-1]
    n_sel = S // SLC_BLOCK
    cs = jnp.arange(n_cmp) * CMP_STRIDE
    j = jnp.arange(n_sel)
    overlap = ((cs[:, None] < (j[None, :] + 1) * SLC_BLOCK)
               & (cs[:, None] + CMP_BLOCK > j[None, :] * SLC_BLOCK)).astype(jnp.float32)
    imp = jnp.einsum('bgrsc,cj->bgsj', p_cmp, overlap)
    t = jnp.arange(S)
    cur = t // SLC_BLOCK
    valid = j[None, :] * SLC_BLOCK <= t[:, None]
    forced = (j[None, :] == 0) | (j[None, :] == cur[:, None]) | (j[None, :] == cur[:, None] - 1)
    score = jnp.where(valid, imp + jnp.where(forced, FORCED_SCORE, 0.0), NEG_INF)
    _, sel = lax.top_k(score, min(SLC_TOPN, n_sel))
    return sel

def nsa_selected(q, k, v, sel, table):
    B, S, H, dh = q.shape
    G, R = NSA_KV_GROUPS, NSA_Q_PER_GROUP
    n_sel = S // SLC_BLOCK
    n_top = sel.shape[-1]
    n_keys = n_top * SLC_BLOCK
    kb = k.reshape(B, n_sel, SLC_BLOCK, G, dh).transpose(0, 3, 1, 2, 4)
    vb = v.reshape(B, n_sel, SLC_BLOCK, G, dh).transpose(0, 3, 1, 2, 4)
    nq = S // SLC_Q_BLOCK
    q_blk = q.reshape(B, nq, SLC_Q_BLOCK, G, R, dh).transpose(1, 0, 2, 3, 4, 5)
    sel_blk = sel.reshape(B, G, nq, SLC_Q_BLOCK, n_top).transpose(2, 0, 1, 3, 4)
    bi = jnp.arange(B)[:, None, None, None]
    gi = jnp.arange(G)[None, :, None, None]
    tbl = table.reshape(REL_BUCKETS, G, R)

    def one(args):
        qb, sb, blk = args
        t = blk * SLC_Q_BLOCK + jnp.arange(SLC_Q_BLOCK)
        kg = kb[bi, gi, sb].reshape(B, G, SLC_Q_BLOCK, n_keys, dh)
        vg = vb[bi, gi, sb].reshape(B, G, SLC_Q_BLOCK, n_keys, dh)
        pos = (sb[..., None] * SLC_BLOCK + jnp.arange(SLC_BLOCK)).reshape(B, G, SLC_Q_BLOCK, n_keys)
        dist = t[None, None, :, None] - pos
        bias = tbl[t5_bucket_2(dist), gi].astype(jnp.float32).transpose(0, 1, 4, 2, 3)
        logits = jnp.einsum('bqgrd,bgqkd->bgrqk', qb, kg).astype(jnp.float32) * (dh ** -0.5)
        p = masked_softmax(logits + bias, (dist >= 0)[:, :, None])
        return jnp.einsum('bgrqk,bgqkd->bqgrd', p.astype(vg.dtype), vg)

    out = lax.map(one, (q_blk, sel_blk, jnp.arange(nq)))
    return out.transpose(1, 0, 2, 3, 4, 5).reshape(B, S, H, dh)

def nsa_window(q, k, v, table):
    B, S, H, dh = q.shape
    G, R = NSA_KV_GROUPS, NSA_Q_PER_GROUP
    nq = S // WIN_Q_BLOCK
    span = WIN_SIZE + WIN_Q_BLOCK
    kp = jnp.pad(k, ((0, 0), (WIN_SIZE, 0), (0, 0), (0, 0)))
    vp = jnp.pad(v, ((0, 0), (WIN_SIZE, 0), (0, 0), (0, 0)))
    q_blk = q.reshape(B, nq, WIN_Q_BLOCK, G, R, dh).transpose(1, 0, 2, 3, 4, 5)

    def one(args):
        qb, blk = args
        start = blk * WIN_Q_BLOCK
        kw = lax.dynamic_slice_in_dim(kp, start, span, axis=1)
        vw = lax.dynamic_slice_in_dim(vp, start, span, axis=1)
        t = start + jnp.arange(WIN_Q_BLOCK)
        pos = start - WIN_SIZE + jnp.arange(span)
        dist = t[:, None] - pos[None, :]
        mask = (dist >= 0) & (dist < WIN_SIZE) & (pos[None, :] >= 0)
        bias = table[t5_bucket_2(dist)].astype(jnp.float32)
        bias = bias.reshape(WIN_Q_BLOCK, span, G, R).transpose(2, 3, 0, 1)
        logits = jnp.einsum('bqgrd,bkgd->bgrqk', qb, kw).astype(jnp.float32) * (dh ** -0.5)
        p = masked_softmax(logits + bias, mask)
        return jnp.einsum('bgrqk,bkgd->bqgrd', p.astype(vw.dtype), vw)

    out = lax.map(one, (q_blk, jnp.arange(nq)))
    return out.transpose(1, 0, 2, 3, 4, 5).reshape(B, S, H, dh)

def nsa_mixer(h, w_in, w_out, k_pos, k_w1, k_w2, v_pos, v_w1, v_w2, table):
    B, S, _ = h.shape
    H, dh, G = NSA_HEADS, NSA_HEAD_DIM, NSA_KV_GROUPS
    q, kv, g, z = split_cols(h @ w_in, [NSA_WIDTH, 6 * NSA_KV_WIDTH, 3 * H, 3 * NSA_WIDTH])
    q = q.reshape(B, S, H, dh)
    k_c, v_c, k_s, v_s, k_w, v_w = [a.reshape(B, S, G, dh) for a in jnp.split(kv, 6, axis=-1)]
    gates = jax.nn.sigmoid(g).reshape(B, S, 3, H, 1)
    zs = jax.nn.silu(z).reshape(B, S, 3, H, dh)
    kc = compress_kv(k_c, k_pos, k_w1, k_w2)
    vc = compress_kv(v_c, v_pos, v_w1, v_w2)
    o_cmp, p_cmp = nsa_compressed(q, kc, vc, table)
    sel = select_blocks(p_cmp, S)
    o_slc = nsa_selected(q, k_s, v_s, sel, table)
    o_win = nsa_window(q, k_w, v_w, table)
    o = jnp.stack([o_cmp, o_slc, o_win], axis=2)
    y = jnp.sum(gates * o * zs, axis=2).reshape(B, S, NSA_WIDTH)
    return y @ w_out

def rotary(x):
    S, d = x.shape[1], x.shape[-1]
    inv = 1.0 / (ROPE_BASE ** jnp.linspace(0.0, 1.0, d // 2, dtype=jnp.float32))
    ang = jnp.arange(S, dtype=jnp.float32)[:, None] * inv[None, :]
    cos = jnp.cos(ang)[None, :, None, :].astype(x.dtype)
    sin = jnp.sin(ang)[None, :, None, :].astype(x.dtype)
    x1, x2 = x[..., :d // 2], x[..., d // 2:]
    return jnp.concatenate([x1 * cos - x2 * sin, x1 * sin + x2 * cos], axis=-1)

def chunkwise_retention(q, k, v):
    B, S, H, dk = q.shape
    dv = v.shape[-1]
    C = RET_CHUNK
    nc = S // C
    dt = q.dtype
    log_g = jnp.log(1.0 - 2.0 ** (-5.0 - jnp.arange(H, dtype=jnp.float32)))
    i = jnp.arange(C, dtype=jnp.float32)
    diff = i[:, None] - i[None, :]
    inner = jnp.where(diff >= 0, jnp.exp(diff[None] * log_g[:, None, None]), 0.0).astype(dt)
    xi = jnp.exp((i + 1.0)[None, :] * log_g[:, None]).astype(dt)
    zeta = jnp.exp((C - 1.0 - i)[None, :] * log_g[:, None]).astype(dt)
    chunk_decay = jnp.exp(C * log_g).astype(dt)
    qc = q.reshape(B, nc, C, H, dk).transpose(1, 0, 3, 2, 4)
    kc = k.reshape(B, nc, C, H, dk).transpose(1, 0, 3, 2, 4)
    vc = v.reshape(B, nc, C, H, dv).transpose(1, 0, 3, 2, 4)

    def step(state, inp):
        qi, ki, vi = inp
        attn = jnp.einsum('bhid,bhjd->bhij', qi, ki) * inner[None]
        o = (jnp.einsum('bhij,bhjv->bhiv', attn, vi)
             + jnp.einsum('bhid,bhdv->bhiv', qi, state) * xi[None, :, :, None])
        state = (state * chunk_decay[None, :, None, None]
                 + jnp.einsum('bhjd,bhjv->bhdv', ki * zeta[None, :, :, None], vi))
        return state, o

    state0 = jnp.zeros((B, H, dk, dv), dt)
    _, o = lax.scan(step, state0, (qc, kc, vc))
    return o.transpose(1, 0, 3, 2, 4).reshape(B, S, H, dv)

def retention_mixer(h, w_in, w_out, gn_gain):
    B, S, _ = h.shape
    q, k, v, z = split_cols(h @ w_in, [RET_QK_WIDTH, RET_QK_WIDTH, RET_WIDTH, RET_WIDTH])
    q = rotary(q.reshape(B, S, RET_HEADS, RET_QK_DIM))
    k = rotary(k.reshape(B, S, RET_HEADS, RET_QK_DIM)) * (RET_QK_DIM ** -0.5)
    v = v.reshape(B, S, RET_HEADS, RET_V_DIM)
    o = chunkwise_retention(q, k, v).astype(jnp.float32)
    mu = jnp.mean(o, axis=-1, keepdims=True)
    var = jnp.mean(jnp.square(o - mu), axis=-1, keepdims=True)
    o = (o - mu) * lax.rsqrt(var + GN_EPS) * gn_gain.reshape(RET_HEADS, RET_V_DIM).astype(jnp.float32)
    o = o.astype(h.dtype).reshape(B, S, RET_WIDTH)
    return (o * jax.nn.silu(z)) @ w_out

def second_inputs(seed: int = 0) -> dict:
    key = jax.random.key(seed)
    ks = jax.random.split(key, 16)
    n_nsa = (DEPTH_2 + N_MIXERS - 1) // N_MIXERS
    n_ret = DEPTH_2 // N_MIXERS

    def nrm(k, shape, scale):
        return jax.random.normal(k, shape, jnp.float32) * scale

    return {
        "x": nrm(ks[0], (BATCH, SEQ, D_MODEL), 1.0),
        "pre_norm_gain": 1.0 + nrm(ks[1], (DEPTH_2, D_MODEL), 0.1),
        "post_norm_gain": 1.0 + nrm(ks[2], (DEPTH_2, D_MODEL), 0.1),
        "rel_bias_table": nrm(ks[3], (REL_BUCKETS, NSA_HEADS), 0.5),
        "nsa_w_in": nrm(ks[4], (n_nsa, D_MODEL, NSA_PROJ), D_MODEL ** -0.5),
        "nsa_w_out": nrm(ks[5], (n_nsa, NSA_WIDTH, D_MODEL), NSA_WIDTH ** -0.5),
        "nsa_cmp_k_pos": nrm(ks[6], (n_nsa, CMP_BLOCK, NSA_HEAD_DIM), 0.5),
        "nsa_cmp_k_w1": nrm(ks[7], (n_nsa, CMP_BLOCK * NSA_HEAD_DIM, CMP_HIDDEN), (CMP_BLOCK * NSA_HEAD_DIM) ** -0.5),
        "nsa_cmp_k_w2": nrm(ks[8], (n_nsa, CMP_HIDDEN, NSA_HEAD_DIM), CMP_HIDDEN ** -0.5),
        "nsa_cmp_v_pos": nrm(ks[9], (n_nsa, CMP_BLOCK, NSA_HEAD_DIM), 0.5),
        "nsa_cmp_v_w1": nrm(ks[10], (n_nsa, CMP_BLOCK * NSA_HEAD_DIM, CMP_HIDDEN), (CMP_BLOCK * NSA_HEAD_DIM) ** -0.5),
        "nsa_cmp_v_w2": nrm(ks[11], (n_nsa, CMP_HIDDEN, NSA_HEAD_DIM), CMP_HIDDEN ** -0.5),
        "ret_w_in": nrm(ks[12], (n_ret, D_MODEL, RET_PROJ), D_MODEL ** -0.5),
        "ret_w_out": nrm(ks[13], (n_ret, RET_WIDTH, D_MODEL), RET_WIDTH ** -0.5),
        "ret_gn_gain": 1.0 + nrm(ks[14], (n_ret, RET_WIDTH), 0.1),
    }

def second_block(x, pre_norm_gain, post_norm_gain, rel_bias_table, nsa_w_in, nsa_w_out,
              nsa_cmp_k_pos, nsa_cmp_k_w1, nsa_cmp_k_w2, nsa_cmp_v_pos, nsa_cmp_v_w1, nsa_cmp_v_w2,
              ret_w_in, ret_w_out, ret_gn_gain):
    h = x
    for layer in range(DEPTH_2):
        slot = layer // N_MIXERS
        u = rms_norm(h, pre_norm_gain[layer])
        if layer % N_MIXERS == 0:
            y = nsa_mixer(u, nsa_w_in[slot], nsa_w_out[slot],
                          nsa_cmp_k_pos[slot], nsa_cmp_k_w1[slot], nsa_cmp_k_w2[slot],
                          nsa_cmp_v_pos[slot], nsa_cmp_v_w1[slot], nsa_cmp_v_w2[slot],
                          rel_bias_table)
        else:
            y = retention_mixer(u, ret_w_in[slot], ret_w_out[slot], ret_gn_gain[slot])
        h = h + rms_norm(y, post_norm_gain[layer])
    return h


def setup_inputs(seed=0):
    out = dict(first_inputs(seed))
    for name, value in second_inputs(seed + 1).items():
        if name != "x":
            out[name + "_2"] = value
    return out


def reference(
    x, norm_mix_g, w_in, conv_w, conv_b, b_igate, b_fgate, mlstm_norm_g, attn_sinks, rel_bias,
    w_branch_m, w_branch_a, w_out, norm_mlp_g, w_up, w_down, final_norm_g, pre_norm_gain_2,
    post_norm_gain_2, rel_bias_table_2, nsa_w_in_2, nsa_w_out_2, nsa_cmp_k_pos_2,
    nsa_cmp_k_w1_2, nsa_cmp_k_w2_2, nsa_cmp_v_pos_2, nsa_cmp_v_w1_2, nsa_cmp_v_w2_2, ret_w_in_2,
    ret_w_out_2, ret_gn_gain_2,
):
    x = first_block(
        x, norm_mix_g, w_in, conv_w, conv_b, b_igate, b_fgate, mlstm_norm_g, attn_sinks,
        rel_bias, w_branch_m, w_branch_a, w_out, norm_mlp_g, w_up, w_down, final_norm_g,
    )
    return second_block(
        x, pre_norm_gain_2, post_norm_gain_2, rel_bias_table_2, nsa_w_in_2, nsa_w_out_2,
        nsa_cmp_k_pos_2, nsa_cmp_k_w1_2, nsa_cmp_k_w2_2, nsa_cmp_v_pos_2, nsa_cmp_v_w1_2,
        nsa_cmp_v_w2_2, ret_w_in_2, ret_w_out_2, ret_gn_gain_2,
    )


_drawn_inputs = setup_inputs


def setup_inputs(seed=0):
    import zlib

    import numpy as np

    out = dict(_drawn_inputs(seed))
    spreads = {}
    factors = {'conv_b': 7.61, 'b_igate': 64.0, 'attn_sinks': 5.331}
    for name, (base, spread) in spreads.items():
        noise = np.random.default_rng([zlib.crc32(name.encode()), seed]).standard_normal(out[name].shape)
        drawn = base * np.exp(spread * noise) if base else spread * noise
        out[name] = __import__('jax').numpy.asarray(drawn.astype(out[name].dtype))
    for name, factor in factors.items():
        out[name] = (out[name] * factor).astype(out[name].dtype)
    return out
```

```python
from contextlib import ExitStack, contextmanager

import numpy as np
import concourse.bass as bass
from concourse import mybir

F32, F32R = mybir.dt.float32, mybir.dt.float32r
ALU, ACT, AX = mybir.AluOpType, mybir.ActivationFunctionType, mybir.AxisListType

P = 128
D = 1024
KT = D // P
S = 512
TT = S // P
DEPTH = 2
EPS = 1e-6
HALF = KT // 2 * P
BIG = 1e30
MH, MDV = 4, 256
VP = MDV + 2
DH = 64
GH = 4
NG = 4
BW = 3 * P
BN = 5 * P
NC = 31
CP = 32
SLOPE_CMP = 16
LAYER_UNITS, NSA_UNITS = 140, 52
UNITS = DEPTH * LAYER_UNITS + NSA_UNITS
VIT, VL, VN = 20, 18, 24



def unit(kind, n):
    return [("u0", kind, n), ("u1", kind, n)]


def attend_steps(name, fill, more=None):
    out, n = [], GH * TT
    fill = list(fill)
    for j in range(n + 2):
        if j < n:
            out.append(("S", name, j))
        if 1 <= j <= n:
            out.append(("T", name, j - 1))
        if j >= 2:
            out.append(("V", name, j - 2))
        out += (more or {}).get(j, [])
        if j in fill:
            out.append(("fill",))
    return out


def place_fill(steps, halves):
    halves = list(halves)
    out = [halves.pop(0) if s[0] == "fill" else s for s in steps]
    assert not halves, len(halves)
    return out


PRE = unit("k", 0) + unit("k", 1) + unit("v", 0) + unit("v", 1) + [("TK", 0), ("TK", 1), ("gates",)]
LOOP = (
    unit("conv", 0) + unit("conv", 1) + unit("mv", 0) + unit("mv", 1)
    + [("TV", 0)] + unit("q", 0) + [("TV", 1), ("bc",)] + unit("q", 1)
    + place_fill(
        [("ST", 0), ("ST", 1), ("fill",), ("NUM", 0), ("ST", 2), ("fill",), ("NUM", 1), ("ST", 3), ("fill",),
         ("NUM", 2), ("fill",), ("NUM", 3), ("hnorm", 0)]
        + attend_steps("w", (0, 2, 4, 6, 8, 10, 12), {3: [("hnorm", 1)], 7: [("TH", 0), ("TH", 1)]})
        + [("otail", "w"), ("fill",), ("TA", 0), ("TA", 1)],
        unit("mo", 0) + unit("mo", 1) + unit("ga", 0) + unit("ga", 1) + unit("gb", 0) + unit("gb", 1)))
MIX = unit("pm", 0) + unit("pa", 0) + unit("pm", 1) + unit("pa", 1)
WOUT = unit("res", 0) + unit("res", 1)
MLP = sum((unit("up", n) for n in range(KT)), []) + sum((unit("down", n) for n in range(KT)), [])
NPRE = (sum((unit("x2", n) for n in range(4)), []) + unit("k", 0) + unit("k", 1) + unit("v", 0) + unit("v", 1)
        + [("TK", 0), ("TK", 1)] + unit("k", 2) + unit("k", 3) + unit("v", 2) + unit("v", 3)
        + [("TK", 2), ("TK", 3), ("ngates",), ("cmpbias",), ("compress",)])
NLOOP = (
    unit("q", 0) + unit("q", 1)
    + place_fill(
        [("CS",), ("fill",)] + [("CT", t) for t in range(TT)] + [("otail", "c"), ("fill",)]
        + attend_steps("s", (3, 6, 9, 12)) + [("TO", 0, 0), ("TO", 0, 1), ("otail", "s"), ("fill",)]
        + attend_steps("f", (3, 6, 9, 12)) + [("TO", 1, 0), ("TO", 1, 1), ("otail", "f"), ("fill",)]
        + [("TO", 2, 0), ("TO", 2, 1)],
        sum((unit("z", n) for n in range(6)), [])))
NOUT = unit("y2", 0) + unit("y2", 1)

TAKES = {"u0": ["u"], "TK": ["T"], "gates": ["O1", "T", "T"], "TV": ["T"], "bc": ["O0"], "ST": ["S"], "NUM": ["T"],
         "S": ["S"], "T": ["T"], "TH": ["T"], "otail": ["O0", "O1"], "TA": ["T"], "ngates": ["O1", "T", "T"],
         "cmpbias": ["S", "S", "S", "S"], "compress": ["O0", "O1", "T", "T"], "CS": ["S", "S"],
         "CT": ["T"], "TO": ["T"], "norm_": ["O1"]}
E_KINDS = ("conv", "mo", "ga", "gb", "up", "z")
PAIRED = ("u", "S", "T", "e")


def takes(step):
    out = list(TAKES.get(step[0], []))
    if step[0] == "u1" and step[1] in E_KINDS:
        out.append("e")
    return out


def per(steps):
    out = {}
    for s in steps:
        for r in takes(s):
            out[r] = out.get(r, 0) + 1
    for r in PAIRED:
        assert out.get(r, 0) % 2 == 0, (r, out)
    return out


def add(*counts):
    out = {}
    for times, c in counts:
        for r, n in c.items():
            out[r] = out.get(r, 0) + times * n
    return out


class Use:

    def __init__(self, b, m, n):
        self.b, self.m, self.n = b, m, n


class Walk:

    def __init__(self):
        self.n, self.half, self.seen = {}, {}, {}

    def use(self, r):
        k = self.seen.get(r, 0)
        self.seen[r] = k + 1
        if r in PAIRED:
            return Use(k % 2, self.half.get(r, 0) + k // 2, self.n.get(r, 0) + k)
        return Use(0, self.n.get(r, 0) + k, self.n.get(r, 0) + k)

    def next(self, r, b=0):
        k = self.seen.get(r, 0)
        return self.half.get(r, 0) + (k + 1 - b) // 2 if r in PAIRED else self.n.get(r, 0) + k

    def flush(self):
        for r, k in self.seen.items():
            self.n[r] = self.n.get(r, 0) + k
            self.half[r] = self.half.get(r, 0) + k // 2
        self.seen = {}

    @contextmanager
    def loop(self, eng, count, counts):
        self.flush()
        n0, h0 = dict(self.n), dict(self.half)
        with eng.Fori(0, count) as i:
            for r, c in counts.items():
                self.n[r] = i * c + n0.get(r, 0)
                self.half[r] = i * (c // 2) + h0.get(r, 0)
            yield i
            self.flush()
        self.n = {r: n0.get(r, 0) + count * counts.get(r, 0) for r in {**n0, **counts}}
        self.half = {r: h0.get(r, 0) + count * (counts.get(r, 0) // 2) for r in {**h0, **counts}}
        self.seen = {}


NORM = [("norm_",)]
C_LAYER = add((1, per(NORM)), (1, per(PRE)), (NG, per(LOOP)), (4, per(MIX)), (4, per(WOUT)), (1, per(NORM)), (4, per(MLP)))
assert C_LAYER["u"] == LAYER_UNITS
assert add((1, per(NPRE)), (NG, per(NLOOP)), (4, per(NOUT)))["u"] == NSA_UNITS


def two_layers_and_nsa(nc, w_all, wg_all, vec_it, vec_l, vec_n, ident_in, tri_in, onehot_w, onehot_n, onehot_c,
                       tab_w, tab_n, late_in, x_in, w1_in, w2_in, pos_in, scr_w, scr_n, out):
    ctx = ExitStack()
    with ctx:
        def sem(name):
            return ctx.enter_context(nc.semaphore(name))

        base = 16512
        top = [base]

        def new(name, shape, dt=F32, at=None):
            size = -(-4 * int(np.prod(shape[1:])) // 32) * 32
            off = top[0] if at is None else at[0]
            t = nc.alloc_sbuf_tensor_at(name, shape, dt, offset=off)
            if at is None:
                top[0] += size
            else:
                at[0] += size
            return t

        x = new("x", [P, KT, S])
        hT_at = top[0]
        hT = [new("hT_hi", [P, KT, S], F32R), new("hT_lo", [P, KT, S], F32R)]
        raw = new("w_raw", [P, 2, KT * P])
        w_hi = new("w_hi", [P, 4, HALF], F32R)
        w_lo = new("w_lo", [P, 4, HALF], F32R)
        ident = new("ident", [P, P])
        ones = new("ones", [P, P])
        tri = new("tri", [P, P])
        vit = new("vit", [P, DEPTH * NG, VIT])
        vl = new("vl", [P, DEPTH, VL])
        vn = new("vn", [P, VN])
        vcur = new("vcur", [P, VIT])
        glay = new("glay", [P, VL])
        late = new("late", [P, 1])
        st = new("st", [P, 12, 16])
        e_buf = new("e_buf", [P, 2, S])
        r32_at = top[0]
        top[0] += 32768
        sig_at = top[0]
        top[0] += 32768
        scr_at = top[0]

        hm32 = new("hm32", [P, KT, S], at=[r32_at])
        ha32 = new("ha32", [P, KT, S], at=[r32_at + 16384])
        u_hl = [new("u_hi", [P, KT, S], F32R, at=[r32_at]), new("u_lo", [P, KT, S], F32R, at=[r32_at + 16384])]
        gw_raw = new("gw_raw", [P, KT * P], at=[r32_at])
        gw = [new("gw_hi", [P, KT * P], F32R, at=[r32_at + 4096]), new("gw_lo", [P, KT * P], F32R, at=[r32_at + 8192])]
        sig = new("sig", [P, 2, KT, S], at=[sig_at])
        y_hl = [new("y_hi", [P, KT, S], F32R, at=[sig_at]), new("y_lo", [P, KT, S], F32R, at=[sig_at + 16384])]
        grow = new("grow", [MH, 12, S], at=[sig_at])
        a = [scr_at]
        mqk = new("mqk", [P, 2, S], at=a)
        vbuf = new("vbuf", [P, TT, VP], at=a)
        numsb = new("numsb", [P, TT, VP], at=a)
        aq = new("aq", [P, 2, S], at=a)
        kg = new("kg", [P, S], at=a)
        vg = new("vg", [P, TT, DH], at=a)
        kdup = new("kdup", [P, NG, S], at=a)
        vtok = new("vtok", [P, NG, TT, DH], at=a)
        bias = new("bias", [P, GH, 2 * P], at=a)
        L = new("L", [P, 2, 2 * P], at=a)
        Pb = new("Pb", [P, 2, 2 * P], at=a)
        PT = new("PT", [P, 2, 2 * P], at=a)
        PTm = new("PTm", [P, 2, S], at=a)
        Dm = new("Dm", [P, S], at=a)
        rbuf = Dm
        dg = new("dg", [P, P], at=a)
        sigmo = new("sigmo", [P, 2, S], at=a)
        ao = new("ao", [P, TT, GH * DH], at=a)
        cv = new("cv", [P, S], at=a)
        vtmp = new("vtmp", [P, 2, S], at=a)
        junk = vtmp[:, 0, 0:MDV]
        negM = new("negM", [MH, S], at=a)
        selh = new("selh", [MH, P], at=a)
        gtok = new("gtok", [P, MH, 2 * TT], at=a)
        gcur = new("gcur", [P, 2 * TT], at=a)
        loop_end = a[0]
        hm_hl = [new("hm_hi", [P, KT, S], F32R, at=[hT_at]), new("hm_lo", [P, KT, S], F32R, at=[hT_at + 16384])]
        a = [scr_at]
        ha_hl = [new("ha_hi", [P, KT, S], F32R, at=a), new("ha_lo", [P, KT, S], F32R, at=a)]
        sq = new("sq", [P, 2, S], at=a)
        nt = new("nt", [P, 2, S], at=a)
        rs = new("rs", [P, S], at=a)
        t3 = new("t3", [P, 3, S], at=a)
        a, b = [r32_at], [scr_at]
        kds = [new("kds", [P, NG, S], at=a), new("kdf", [P, NG, S], at=a)]
        vts = [new("vts", [P, NG, TT, DH], at=a), new("vtf", [P, NG, TT, DH], at=a)]
        kcd = new("kcd", [P, NG, CP], at=a)
        vc = new("vc", [NC, NG, DH], at=a)
        gates = new("gates", [P, NG, 3, TT * GH], at=a)
        kcg, vcg = new("kcg", [P, CP], at=a), new("vcg", [NC, DH], at=a)
        gat = new("gat", [P, 3, TT * GH], at=a)
        vgs = [new("vgs", [P, TT, DH], at=a), new("vgf", [P, TT, DH], at=a)]
        assert a[0] <= sig_at
        y2 = new("y2", [P, KT, S], at=[r32_at])
        bcmp = new("bcmp", [P, NG, GH * TT, CP], at=b)
        b_loop = list(b)
        vtmpn = new("vtmpn", [P, 2, S], at=b)
        x2 = [new("x2k", [P, 5, S], at=b), new("x2v", [P, 5, S], at=b)]
        w1 = [new("w1k", [P, 16, 256], at=b), new("w1v", [P, 16, 256], at=[sig_at])]
        gwn_raw = new("gwn_raw", [P, KT * P], at=b)
        gwn = [new("gwn_hi", [P, KT * P], F32R, at=b), new("gwn_lo", [P, KT * P], F32R, at=b)]
        assert b[0] <= 229368, b[0]
        w2 = new("w2", [P, 2, 2, DH], at=[sig_at + 16384])
        hid = new("hid", [P, 4, P], at=[sig_at + 18432])
        ehid = new("ehid", [P, 4, P], at=[sig_at + 20480])
        oh_c = new("oh_c", [33, 1024], at=[sig_at + 22528])
        tabn2 = new("tabn2", [33, 16], at=[sig_at + 26624])
        grow2 = new("grow2", [48, 2, S], at=[sig_at + 26688])
        posb = new("posb", [P, 2, 16], at=[sig_at + 30784])
        b = b_loop
        qn = new("qn", [P, 2, S], at=b)
        kgs = [new("kgs", [P, S], at=b), new("kgf", [P, S], at=b)]
        biasn = new("biasn", [P, GH, S], at=b)
        Ln_ = new("Ln", [P, 2, S], at=b)
        Pn = new("Pn", [P, 2, S], at=b)
        PTn = new("PTn", [P, 2, S], at=b)
        aon = new("aon", [P, TT, GH * DH], at=b)
        sz = new("sz", [P, 6, S], at=b)
        y32 = new("y32", [P, 2, S], at=b)
        tn = new("tn", [P, S], at=b)
        rbufn = new("rbufn", [P, S], at=b)
        assert max(b[0], loop_end) <= 229368, (b[0], loop_end)
        a = [sig_at]
        oh_w, oh_n = new("oh_w", [33, BW], at=a), new("oh_n", [33, BN], at=a)
        tabw, tabn = new("tabw", [33, 16], at=a), new("tabn", [33, 16], at=a)
        bw_sb, bn_sb = new("bw_sb", [16, BW], at=a), new("bn_sb", [16, BN], at=a)

        ps = ctx.enter_context(nc.psum_tensor("ps", [P, 8, S], F32))
        bank = {("u", 0): 0, ("u", 1): 1, ("S", 0): 2, ("S", 1): 3, ("T", 0): 4, ("T", 1): 5, "O0": 6, "O1": 7}

        raw_in = [sem("raw_in0"), sem("raw_in1")]
        hi_done, lo_done = sem("w_hi_done"), sem("w_lo_done")
        used = sem("w_used")
        g_free = [sem("g_free0"), sem("g_free1")]
        s_ready, s_free = [sem("s_ready0"), sem("s_ready1")], [sem("s_free0"), sem("s_free1")]
        t_ready, t_free = [sem("t_ready0"), sem("t_ready1")], [sem("t_free0"), sem("t_free1")]
        o_ready, o_free = [sem("o_ready0"), sem("o_ready1")], [sem("o_free0"), sem("o_free1")]
        e_done = [sem("e_done0"), sem("e_done1")]
        e_conv, e_z = sem("exp_conv"), sem("exp_z")
        cst_in, cst_done = sem("consts_in"), sem("consts_made")
        bw_out, bn_out = sem("bias_window_out"), sem("bias_full_out")
        bw_done, bn_done = sem("bias_window_made"), sem("bias_full_made")
        x_done = sem("x_done")
        sq_ready, sq_used, rs_ready = sem("sq_ready"), sem("sq_used"), sem("rs_ready")
        nt_ready, nhi_done, h_ready = sem("nt_ready"), sem("norm_hi_done"), sem("h_ready")
        gw_in, gwhi_done, gwlo_done = sem("gate_w_in"), sem("gate_w_hi"), sem("gate_w_lo")
        gr_abs, gr_log, grows_done = sem("gate_rows_abs"), sem("gate_rows_log"), sem("gate_rows_done")
        half_a = sem("scalar_half_of_unit")
        staged_v, staged_a = sem("staged_vector"), sem("staged_scalar")
        bias_in = sem("bias_in")
        mqk_done = sem("mqk_done")
        dg_done, d_done = sem("diag_done"), sem("decay_done")
        ss_done, hn_v, hn_a, hm_done = sem("sumsq_done"), sem("hnorm_vector"), sem("hnorm_scalar"), sem("hm_scaled")
        probs = sem("probs")
        t1_done, es_done = sem("sink_logit_done"), sem("sink_exp_done")
        mhi, mlo = sem("mix_in_hi"), sem("mix_in_lo")
        y_v, y_hi_done, y_done = sem("y_sum"), sem("y_hi_done"), sem("y_done")
        u_hi_done, u_done = sem("u_hi_done"), sem("u_done")
        late_in_s, x2_pos = sem("last_layer_in"), sem("x2_pos")
        cmp_pre, cmp_exp, hid_done = sem("cmp_hidden_pre"), sem("cmp_hidden_exp"), sem("cmp_hidden_done")
        cs_sub, cs_exp = sem("cmp_logits_done"), sem("cmp_probs")
        out_s = sem("out_stored")
        chain_v, chain_a = sem("vector_chain"), sem("scalar_chain")

        block = ctx.enter_context(nc.Block())

        @block.sync
        def _(sp):
            with sp.Fori(0, UNITS // 2) as i:
                for p in range(2):
                    sp.wait_ge(lo_done, i * 4 + 2 * p + 2)
                    nc.sync.dma_start(raw[:, p, :], w_all[2 * i + p]).then_inc(raw_in[p], 16)
            for k in range(KT):
                sp.wait_ge(x_done, KT + k + 1)
                nc.sync.dma_start(out[k * P:(k + 1) * P, :], x[:, k, :]).then_inc(out_s, 16)
            sp.wait_ge(out_s, 16 * KT)

        @block.gpsimd
        def _(pool):
            pool.sem_inc(lo_done, 4)
            with pool.Fori(0, UNITS // 2) as i:
                for h in range(4):
                    pool.wait_ge(hi_done, i * 4 + h + 1)
                    nc.gpsimd.tensor_tensor(w_lo[:, h, :], raw[:, h // 2, (h % 2) * HALF:(h % 2 + 1) * HALF],
                                            w_hi[:, h, :].bitcast(F32), ALU.subtract).then_inc(lo_done, 1)

        def step_uses(w, step):
            return [w.use(r) for r in takes(step)]

        @block.tensor
        def _(pe):
            w = Walk()
            cur = {}

            def half_unit(u, h, hi, lo, waits=None):
                p = u.b
                if h == 0:
                    pe.wait_ge(g_free[p], u.m + 1)
                pe.wait_ge(lo_done, u.n * 2 + h + 5)
                for k in range(KT // 2):
                    kk = h * (KT // 2) + k
                    if waits is not None:
                        pe.wait_ge(*waits(kk))
                    wh, wl = w_hi[:, 2 * p + h, k * P:(k + 1) * P], w_lo[:, 2 * p + h, k * P:(k + 1) * P]
                    nc.tensor.matmul(ps[:, p, :], wh, hi[:, kk, :], start=(kk == 0), stop=False)
                    nc.tensor.matmul(ps[:, p, :], wh, lo[:, kk, :], start=False, stop=False)
                    last = nc.tensor.matmul(ps[:, p, :], wl, hi[:, kk, :], start=False, stop=(kk == KT - 1))
                last.then_inc(used, 1)

            def norm_sum(n):
                use = step_uses(w, NORM[0])[0]
                pe.wait_ge(o_free[1], use.m + 1)
                for k in range(KT):
                    pe.wait_ge(sq_ready, n * KT + k + 1)
                    nc.tensor.matmul(ps[:, 7, :], ones[:, :], sq[:, k % 2, :], start=(k == 0), stop=(k == KT - 1))\
                        .then_inc(sq_used if k < KT - 1 else o_ready[1], 1)

            def heads4(dst_bank, src, ready):
                for t in range(TT):
                    last = nc.tensor.transpose(ps[:, dst_bank, t * P:(t + 1) * P], src(t), ident[:, :])
                last.then_inc(ready, 1)

            def gate_gemm(I, use, gw):
                pe.wait_ge(gwlo_done, I + 1)
                pe.wait_ge(o_free[1], use.m + 1)
                for k in range(KT):
                    wh, wl = gw[0][:, k * P:(k + 1) * P], gw[1][:, k * P:(k + 1) * P]
                    nc.tensor.matmul(ps[:, 7, :], wh, hT[0][:, k, :], start=(k == 0), stop=False)
                    nc.tensor.matmul(ps[:, 7, :], wh, hT[1][:, k, :], start=False, stop=False)
                    last = nc.tensor.matmul(ps[:, 7, :], wl, hT[0][:, k, :], start=False, stop=(k == KT - 1))
                last.then_inc(o_ready[1], 1)

            def attend(step, us, q, kk, vv, I, wide, nI):
                kind, name, j = step
                qt, hd = j // GH, j % GH
                k0 = 0 if wide else max(qt - 1, 0)
                nk = qt + 1 - k0
                hp = DH * (hd % 2)
                if kind == "S":
                    pe.wait_ge(s_free[us[0].b], us[0].m + 1)
                    nc.tensor.matmul(ps[:, 2 + us[0].b, 0:nk * P], q[hp:hp + DH, hd // 2, qt * P:(qt + 1) * P],
                                     kk[hp:hp + DH, k0 * P:(qt + 1) * P], start=True, stop=True)\
                        .then_inc(s_ready[us[0].b], 1)
                elif kind == "T":
                    pe.wait_ge(t_free[us[0].b], us[0].m + 1)
                    pe.wait_ge(probs, nI + j + 1)
                    pb = cur["P"]
                    for c in range(nk):
                        last = nc.tensor.transpose(ps[:, 4 + us[0].b, c * P:(c + 1) * P],
                                                   pb[:, j % 2, c * P:(c + 1) * P], ident[:, :])
                    last.then_inc(t_ready[us[0].b], 1)
                    cur["Tuse", j] = us[0]
                else:
                    t = cur["Tuse", j]
                    pe.wait_ge(t_free[t.b], t.m + 2)
                    ob = qt // 2
                    if j % (2 * GH) == 0:
                        pe.wait_ge(o_free[ob], cur["Om"][ob] + 1)
                    pt = cur["PT"]
                    for c in range(nk):
                        last = nc.tensor.matmul(ps[:, 6 + ob, (qt % 2) * 256 + hd * DH:(qt % 2) * 256 + (hd + 1) * DH],
                                                pt[:, j % 2, c * P:(c + 1) * P], vv[:, k0 + c, :],
                                                start=(c == 0), stop=(c == nk - 1))
                    if j % (2 * GH) == 2 * GH - 1:
                        last.then_inc(o_ready[ob], 1)

            pe.wait_ge(cst_in, 16 * 11)
            pe.wait_ge(cst_done, 1)
            nc.tensor.matmul(ps[0:16, 2, 0:BW], tabw[:, :], oh_w[:, :], start=True, stop=True).then_inc(s_ready[0], 1)
            nc.tensor.matmul(ps[0:16, 3, 0:S], tabn[:, :], oh_n[:, 0:S], start=True, stop=True).then_inc(s_ready[1], 1)
            for b_ in range(2):
                nc.tensor.matmul(ps[0:16, 4 + b_, 0:64], tabn[:, :], oh_n[:, S + 64 * b_:S + 64 * (b_ + 1)],
                                 start=True, stop=True).then_inc(t_ready[b_], 1)
            for r in ("S", "S", "T", "T"):
                w.use(r)

            with w.loop(pe, DEPTH, C_LAYER) as l:
                norm_sum(l * 2)
                for s in PRE:
                    us = step_uses(w, s)
                    if s[0] == "u0":
                        cur["u"] = cur[s[1:]] = us[0]
                    if s[0] in ("u0", "u1"):
                        first = s[1:] == ("k", 0)
                        half_unit(cur["u"], int(s[0][1]), *hT,
                                  waits=(lambda k: (h_ready, l * 2 * KT + k + 1)) if first else None)
                    elif s[0] == "TK":
                        pe.wait_ge(t_free[us[0].b], us[0].m + 1)
                        vu = cur["v", s[1]]
                        pe.wait_ge(g_free[vu.b], vu.m + 2)
                        heads4(4 + us[0].b, lambda t: vtmp[:, s[1], t * P:(t + 1) * P], t_ready[us[0].b])
                    elif s[0] == "gates":
                        gate_gemm(l, us[0], gw)
                        pe.wait_ge(grows_done, l + 1)
                        for which in range(2):
                            t_ = us[1 + which]
                            pe.wait_ge(t_free[t_.b], t_.m + 1)
                            for t in range(TT):
                                last = nc.tensor.matmul(ps[:, 4 + t_.b, t * MH:(t + 1) * MH],
                                                        grow[:, 8 + which, t * P:(t + 1) * P], ident[0:MH, 0:MH],
                                                        start=True, stop=True)
                            last.then_inc(t_ready[t_.b], 1)
                w.flush()
                with w.loop(pe, NG, per(LOOP)) as it:
                    I = l * NG + it
                    cur["P"], cur["PT"] = Pb, PT
                    stu, nu = {}, {}
                    for s in LOOP:
                        us = step_uses(w, s)
                        if s[0] == "u0":
                            cur["u"] = cur[s[1:]] = us[0]
                        if s[0] in ("u0", "u1"):
                            half_unit(cur["u"], int(s[0][1]), *hT)
                        elif s[0] == "TV":
                            pe.wait_ge(t_free[us[0].b], us[0].m + 1)
                            vu = cur["mv", s[1]]
                            pe.wait_ge(g_free[vu.b], vu.m + 2)
                            heads4(4 + us[0].b, lambda t: vtmp[:, s[1], t * P:(t + 1) * P], t_ready[us[0].b])
                            cur["TV", s[1]] = us[0]
                        elif s[0] == "bc":
                            pe.wait_ge(o_free[0], us[0].m + 1)
                            pe.wait_ge(staged_v, I + 1)
                            nc.tensor.matmul(ps[:, 6, :], selh[:, :], negM[:, :], start=True, stop=True)\
                                .then_inc(o_ready[0], 1)
                        elif s[0] == "ST":
                            tt = s[1]
                            stu[tt] = us[0]
                            pe.wait_ge(s_free[us[0].b], us[0].m + 1)
                            if tt == 0:
                                pe.wait_ge(mqk_done, I * 2 + 2)
                            for c in range(tt + 1):
                                last = nc.tensor.matmul(ps[:, 2 + us[0].b, c * P:(c + 1) * P],
                                                        mqk[:, 1, c * P:(c + 1) * P], mqk[:, 0, tt * P:(tt + 1) * P],
                                                        start=True, stop=True)
                            last.then_inc(s_ready[us[0].b], 1)
                        elif s[0] == "NUM":
                            tt = s[1]
                            pe.wait_ge(t_free[us[0].b], us[0].m + 1)
                            if tt == 0:
                                for v_ in range(2):
                                    pe.wait_ge(t_free[cur["TV", v_].b], cur["TV", v_].m + 2)
                            pe.wait_ge(s_free[stu[tt].b], stu[tt].m + 2)
                            for c in range(tt + 1):
                                last = nc.tensor.matmul(ps[:, 4 + us[0].b, 0:MDV + 1], PTm[:, tt % 2, c * P:(c + 1) * P],
                                                        vbuf[:, c, 0:MDV + 1], start=(c == 0), stop=(c == tt))
                            last.then_inc(t_ready[us[0].b], 1)
                        elif s[0] in ("S", "T", "V"):
                            if s == ("S", "w", 0):
                                for n in range(2):
                                    pe.wait_ge(g_free[cur["q", n].b], cur["q", n].m + 2)
                                pe.wait_ge(staged_a, I + 1)
                                cur["Om"] = [w.next("O0"), w.next("O1")]
                            attend(s, us, aq, kg, vg, I, False, I * 16)
                        elif s[0] == "TH":
                            pe.wait_ge(t_free[us[0].b], us[0].m + 1)
                            pe.wait_ge(hm_done, I + 1)
                            heads4(4 + us[0].b, lambda t: numsb[:, t, s[1] * P:(s[1] + 1) * P], t_ready[us[0].b])
                        elif s[0] == "otail":
                            cur["tail"] = us
                        elif s[0] == "TA":
                            pe.wait_ge(t_free[us[0].b], us[0].m + 1)
                            if s[1] == 0:
                                for o_ in range(2):
                                    pe.wait_ge(o_free[o_], cur["tail"][o_].m + 2)
                            heads4(4 + us[0].b, lambda t: ao[:, t, s[1] * P:(s[1] + 1) * P], t_ready[us[0].b])
                with w.loop(pe, 4, per(MIX)) as i:
                    for s in MIX:
                        us = step_uses(w, s)
                        if s[0] == "u0":
                            cur["u"] = us[0]
                        second = s[1] == "pa"
                        half_unit(cur["u"], int(s[0][1]), *(ha_hl if second else hm_hl),
                                  waits=(lambda k: (mlo, l * 2 * KT + second * KT + k + 1)) if s[2] == 0 else None)
                with w.loop(pe, 4, per(WOUT)) as i:
                    for s in WOUT:
                        us = step_uses(w, s)
                        if s[0] == "u0":
                            cur["u"] = us[0]
                        half_unit(cur["u"], int(s[0][1]), *y_hl,
                                  waits=(lambda k: (y_done, l * KT + k + 1)) if s[2] == 0 else None)
                norm_sum(l * 2 + 1)
                with w.loop(pe, 4, per(MLP)) as c:
                    for s in MLP:
                        us = step_uses(w, s)
                        if s[0] == "u0":
                            cur["u"] = us[0]
                        if s[1] == "up":
                            half_unit(cur["u"], int(s[0][1]), *hT,
                                      waits=(lambda k: (h_ready, l * 2 * KT + KT + k + 1)) if s[2] == 0 else None)
                        else:
                            half_unit(cur["u"], int(s[0][1]), *u_hl,
                                      waits=(lambda k: (u_done, l * 4 * KT + c * KT + k + 1)) if s[2] == 0 else None)

            norm_sum(DEPTH * 2)
            norm_sum(DEPTH * 2 + 1)
            for s in NPRE:
                us = step_uses(w, s)
                if s[0] == "u0":
                    cur["u"] = cur[s[1:]] = us[0]
                if s[0] in ("u0", "u1"):
                    first = s[1:] == ("x2", 0)
                    half_unit(cur["u"], int(s[0][1]), *hT,
                              waits=(lambda k: (h_ready, DEPTH * 2 * KT + k + 1)) if first else None)
                elif s[0] == "TK":
                    pe.wait_ge(t_free[us[0].b], us[0].m + 1)
                    vu = cur["v", s[1]]
                    pe.wait_ge(g_free[vu.b], vu.m + 2)
                    heads4(4 + us[0].b, lambda t: vtmpn[:, s[1] % 2, t * P:(t + 1) * P], t_ready[us[0].b])
                elif s[0] == "ngates":
                    gate_gemm(DEPTH, us[0], gwn)
                    pe.wait_ge(grows_done, DEPTH + 1)
                    for which in range(2):
                        t_ = us[1 + which]
                        pe.wait_ge(t_free[t_.b], t_.m + 1)
                        for t in range(2):
                            tk = 2 * which + t
                            last = nc.tensor.transpose(ps[:, 4 + t_.b, t * 48:(t + 1) * 48],
                                                       grow2[:, 1, tk * P:(tk + 1) * P], ident[0:48, 0:48])
                        last.then_inc(t_ready[t_.b], 1)
                elif s[0] == "cmpbias":
                    pe.wait_ge(late_in_s, 16 * 6)
                    for qt in range(TT):
                        pe.wait_ge(s_free[us[qt].b], us[qt].m + 1)
                        for c in range(NC):
                            off = P * qt - SLOPE_CMP * c - 31 + 511
                            last = nc.tensor.matmul(ps[:, 2 + us[qt].b, c * 16:(c + 1) * 16], oh_c[:, off:off + P],
                                                    tabn2[:, :], start=True, stop=True)
                        last.then_inc(s_ready[us[qt].b], 1)
                elif s[0] == "compress":
                    pe.wait_ge(x2_pos, 2)
                    for kv in range(2):
                        pe.wait_ge(o_free[kv], us[kv].m + 1)
                        for m in range(2):
                            for pr in range(16):
                                rhs = x2[kv][:, :, 2 * pr:2 * pr + SLOPE_CMP * (NC - 1) + 1:SLOPE_CMP]
                                last = nc.tensor.matmul(ps[:, 6 + kv, m * 256:m * 256 + 5 * NC],
                                                        w1[kv][:, pr, m * P:(m + 1) * P], rhs,
                                                        start=(pr == 0), stop=(pr == 15))
                        last.then_inc(o_ready[kv], 1)
                    pe.wait_ge(hid_done, 1)
                    pe.wait_ge(t_free[0], us[2].m + 1)
                    for m in range(2):
                        last = nc.tensor.matmul(ps[0:DH, 4, 0:NG * NC], w2[:, 0, m, :], hid[:, m, 0:NG * NC],
                                                start=(m == 0), stop=(m == 1))
                    last.then_inc(t_ready[0], 1)
                    pe.wait_ge(t_free[1], us[3].m + 1)
                    for g in range(NG):
                        for m in range(2):
                            last = nc.tensor.matmul(ps[0:NC, 5, g * DH:(g + 1) * DH], hid[:, 2 + m, g * NC:(g + 1) * NC],
                                                    w2[:, 1, m, :], start=(m == 0), stop=(m == 1))
                    last.then_inc(t_ready[1], 1)
            w.flush()
            with w.loop(pe, NG, per(NLOOP)) as it:
                cur["P"], cur["PT"] = Pn, PTn
                ctu = {}
                for s in NLOOP:
                    us = step_uses(w, s)
                    if s[0] == "u0":
                        cur["u"] = cur[s[1:]] = us[0]
                    if s[0] in ("u0", "u1"):
                        half_unit(cur["u"], int(s[0][1]), *hT)
                    elif s[0] == "CS":
                        for n in range(2):
                            pe.wait_ge(g_free[cur["q", n].b], cur["q", n].m + 2)
                        pe.wait_ge(staged_a, DEPTH * NG + it + 1)
                        pe.wait_ge(s_free[0], us[0].m + 1)
                        pe.wait_ge(s_free[1], us[1].m + 1)
                        for j in range(GH * TT):
                            qt, hd = j // GH, j % GH
                            hp = DH * (hd % 2)
                            last = nc.tensor.matmul(ps[:, 2 + j % 2, (j // 2) * CP:(j // 2) * CP + NC],
                                                    qn[hp:hp + DH, hd // 2, qt * P:(qt + 1) * P],
                                                    kcg[hp:hp + DH, 0:NC], start=True, stop=True)
                            if j >= GH * TT - 2:
                                last.then_inc(s_ready[j % 2], 1)
                        cur["Om"] = [w.next("O0"), w.next("O1")]
                    elif s[0] == "CT":
                        qt = s[1]
                        b_ = us[0].b
                        pe.wait_ge(cs_exp, it + 1)
                        pe.wait_ge(t_free[b_], us[0].m + 1)
                        for hd in range(GH):
                            j = qt * GH + hd
                            last = nc.tensor.transpose(ps[0:NC, 4 + b_, hd * P:(hd + 1) * P], Pn[:, 0, j * CP:j * CP + NC],
                                                       ident[:, :])
                        last.then_inc(t_ready[b_], 1)
                        pe.wait_ge(t_free[b_], us[0].m + 2)
                        ob = qt // 2
                        if qt % 2 == 0:
                            pe.wait_ge(o_free[ob], cur["Om"][ob] + 1)
                        for hd in range(GH):
                            last = nc.tensor.matmul(ps[:, 6 + ob, (qt % 2) * 256 + hd * DH:(qt % 2) * 256 + (hd + 1) * DH],
                                                    PTn[0:NC, qt % 2, hd * P:(hd + 1) * P], vcg[:, :], start=True, stop=True)
                        if qt % 2 == 1:
                            last.then_inc(o_ready[ob], 1)
                    elif s[0] in ("S", "T", "V"):
                        br = 0 if s[1] == "s" else 1
                        if s[0] == "S" and s[2] == 0:
                            cur["Om"] = [w.next("O0"), w.next("O1")]
                        attend(s, us, qn, kgs[br], vgs[br], it, True, DEPTH * NG * 16 + it * 32 + br * 16)
                    elif s[0] == "otail":
                        cur["tail"] = us
                    elif s[0] == "TO":
                        pe.wait_ge(t_free[us[0].b], us[0].m + 1)
                        for o_ in range(2):
                            pe.wait_ge(o_free[o_], cur["tail"][o_].m + 2)
                        heads4(4 + us[0].b, lambda t: aon[:, t, s[2] * P:(s[2] + 1) * P], t_ready[us[0].b])
            for i in range(4):
                for s in NOUT:
                    us = step_uses(w, s)
                    if s[0] == "u0":
                        cur["u"] = us[0]
                    first = i == 0 and s[2] == 0
                    half_unit(cur["u"], int(s[0][1]), *y_hl,
                              waits=(lambda k: (y_done, DEPTH * KT + k + 1)) if first else None)
            norm_sum(DEPTH * 2 + 2)

        @block.scalar
        def _(act):
            w = Walk()
            cur = {}
            chain = [0]

            def restart():
                act.sem_clear(chain_a)
                chain[0] = 0

            def link(ins):
                chain[0] += 1
                ins.then_inc(chain_a, 1)
                act.wait_ge(chain_a, chain[0])

            def split(n, half_n, p, h):
                if h == 0:
                    act.wait_ge(raw_in[p], half_n * 16 + 16)
                act.wait_ge(used, n * 2 + h + 1)
                nc.scalar.activation(w_hi[:, 2 * p + h, :], raw[:, p, h * HALF:(h + 1) * HALF], ACT.Copy)\
                    .then_inc(hi_done, 1)

            def product(u):
                act.wait_ge(used, u.n * 2 + 6)

            def gemm_step(s, u):
                if s[0] == "u1":
                    store(s, u)
                if not cur.get("last"):
                    split(u.n + 2, u.m + 1, u.b, int(s[0][1]))

            def store(s, u):
                kind, n = s[1], s[2]
                g = ps[:, u.b, :]
                if kind == "k":
                    dst = kdup if cur["layer"] else kds[n // 2]
                    product(u)
                    for i in range(2):
                        nc.scalar.activation(dst[DH * i:DH * (i + 1), 2 * (n % 2), :], ps[0:DH, u.b, :], ACT.Copy)\
                            .then_inc(half_a, 1)
                elif kind == "x2":
                    product(u)
                    for i in range(2):
                        nc.scalar.activation(x2[n // 2][DH:P, 2 * (n % 2) + i, 0:S - 1],
                                             ps[DH * i:DH * (i + 1), u.b, 1:S], ACT.Copy).then_inc(half_a, 1)
                elif kind in ("v", "mv"):
                    product(u)
                    nc.scalar.activation((vtmp if cur["layer"] else vtmpn)[:, n % 2, :], g, ACT.Copy)\
                        .then_inc(g_free[u.b], 1)
                elif kind == "conv":
                    e = cur["e"]
                    act.wait_ge(g_free[u.b], u.m + 2)
                    act.wait_ge(e_done[e.b], e.m + 1)
                    nc.scalar.activation(e_buf[:, e.b, :], cv[:, :], ACT.Exp, scale=-1.0).then_inc(e_conv, 1)
                elif kind in ("mo", "ga", "gb"):
                    e = cur["e"]
                    product(u)
                    act.wait_ge(e_done[e.b], e.m + 1)
                    nc.scalar.activation(e_buf[:, e.b, :], g, ACT.Exp, scale=-1.0).then_inc(g_free[u.b], 1)
                elif kind == "z":
                    e = cur["e"]
                    product(u)
                    act.wait_ge(e_done[e.b], e.m + 1)
                    nc.scalar.activation(e_buf[:, e.b, :], g, ACT.Exp, scale=-1.0).then_inc(e_z, 1)
                elif kind == "up":
                    e = cur["e"]
                    product(u)
                    act.wait_ge(e_done[e.b], e.m + 1)
                    nc.scalar.activation(e_buf[:, e.b, :], g, ACT.Relu).then_inc(g_free[u.b], 1)
                    act.wait_ge(g_free[u.b], u.m + 2)
                    nc.scalar.activation(u_hl[0][:, n, :], e_buf[:, e.b, :], ACT.Square).then_inc(u_hi_done, 1)
                elif kind == "pa":
                    act.wait_ge(y_v, cur["ny"] + n + 1)
                    nc.scalar.activation(y_hl[0][:, cur["i2"] + n, :], t3[:, n, :], ACT.Copy).then_inc(y_hi_done, 1)
                elif kind == "y2":
                    product(u)
                    nc.scalar.activation(y2[:, cur["i2"] + n, :], g, ACT.Copy).then_inc(g_free[u.b], 1)

            def take(s):
                us = [w.use(r) for r in takes(s)]
                if s[0] == "u0":
                    cur["u"] = cur[s[1:]] = us[0]
                if s[0] == "u1" and us:
                    cur["e"] = us[0]
                return us

            def norm(n, src, ready, split_to):
                use = [w.use(r) for r in takes(NORM[0])][0]
                for k in range(KT):
                    ready(k)
                    if k >= 2:
                        act.wait_ge(sq_used, n * (KT - 1) + k - 1)
                    nc.scalar.activation(sq[:, k % 2, :], src[:, k, :], ACT.Square).then_inc(sq_ready, 1)
                act.wait_ge(o_ready[1], use.m + 1)
                nc.scalar.activation(rs[:, :], ps[:, 7, :], ACT.Ln, scale=1.0 / D, bias=EPS).then_inc(o_free[1], 1)
                act.wait_ge(o_free[1], use.m + 2)
                nc.scalar.activation(rs[:, :], rs[:, :], ACT.Exp, scale=-0.5).then_inc(rs_ready, 1)
                if split_to is not None:
                    for k in range(KT):
                        act.wait_ge(nt_ready, split_to * KT + k + 1)
                        nc.scalar.activation(hT[0][:, k, :], nt[:, k % 2, :], ACT.Copy).then_inc(nhi_done, 1)

            def stored(k=None):
                for b_ in range(2):
                    act.wait_ge(g_free[b_], w.next("u", b_) + 1)

            def gate_weights(I, gw_raw):
                nc.scalar.dma_start(gw_raw[:, :], wg_all[I]).then_inc(gw_in, 16)

            def gate_weights_hi(I, gw_raw, gw):
                act.wait_ge(gw_in, I * 16 + 16)
                nc.scalar.activation(gw[0][:, :], gw_raw[:, :], ACT.Copy).then_inc(gwhi_done, 1)

            def attend_act(s, us, Pbuf, Lbuf, PTbuf, nk, nI, j):
                n = nk * P
                if s[0] == "S":
                    act.wait_ge(s_free[us[0].b], us[0].m + 2)
                    if j >= 2:
                        t = cur["Tuse", j - 2]
                        act.wait_ge(t_ready[t.b], t.m + 1)
                    nc.scalar.activation(Pbuf[:, j % 2, 0:n], Lbuf[:, j % 2, 0:n], ACT.Exp, scale=-1.0,
                                         bias=st[:, 0, j:j + 1], accum_out=st[:, 1, j:j + 1]).then_inc(probs, 1)
                elif s[0] == "T":
                    cur["Tuse", j] = us[0]
                    if j % 2 == 0:
                        act.wait_ge(t_ready[us[0].b], us[0].m + 1)
                        nc.scalar.activation(PTbuf[:, 0, 0:n], ps[:, 4 + us[0].b, 0:n], ACT.Copy)\
                            .then_inc(t_free[us[0].b], 1)

            act.sem_inc(used, 4)
            for f in (*g_free, *s_free, *t_free, *o_free, *e_done):
                act.sem_inc(f, 1)
            for dst, src in ((x[:, :, :], x_in.rearrange("(k p) t -> p k t", p=P)), (ident[:, :], ident_in),
                             (tri[:, :], tri_in), (vit[:, :, :], vec_it), (vl[:, :, :], vec_l), (vn[:, :], vec_n),
                             (oh_w[:, :], onehot_w), (oh_n[:, :], onehot_n), (tabw[:, :], tab_w), (tabn[:, :], tab_n),
                             (late[:, :], late_in)):
                nc.scalar.dma_start(dst, src).then_inc(cst_in, 16)
            act.wait_ge(cst_done, 2)
            link(nc.scalar.activation(st[:, 9, 0:1], ones[:, 0:1], ACT.Ln))
            link(nc.scalar.activation(st[:, 9, 0:1], ones[:, 0:1], ACT.Exp))
            for p in range(2):
                for h in range(2):
                    split(p, 0, p, h)
            for r in ("S", "S", "T", "T"):
                w.use(r)
            act.wait_ge(bw_done, 1)
            nc.scalar.dma_start(scr_w, bw_sb[:, :]).then_inc(bw_out, 16)
            act.wait_ge(bn_done, 3)
            nc.scalar.dma_start(scr_n, bn_sb[:, :]).then_inc(bn_out, 16)
            act.wait_ge(cst_in, 16 * 11)
            act.wait_ge(bw_out, 16)
            act.wait_ge(bn_out, 16)

            with w.loop(act, DEPTH, C_LAYER) as l:
                cur["layer"] = True
                restart()
                stored()
                gate_weights(l, gw_raw)
                norm(l * 2, x, lambda k: None, l * 2)
                gate_weights_hi(l, gw_raw, gw)
                for s in PRE:
                    us = take(s)
                    if s[0] in ("u0", "u1"):
                        gemm_step(s, cur["u"])
                    elif s[0] == "TK":
                        act.wait_ge(t_ready[us[0].b], us[0].m + 1)
                        tk = ps[:, 4 + us[0].b, :].rearrange("p (t d) -> p t d", t=TT)
                        link(nc.scalar.activation(vtok[:, 2 * s[1], :, :], tk[:, :, 0:DH], ACT.Copy))
                        nc.scalar.activation(vtok[:, 2 * s[1] + 1, :, :], tk[:, :, DH:P], ACT.Copy)\
                            .then_inc(t_free[us[0].b], 1)
                    elif s[0] == "gates":
                        act.wait_ge(gr_abs, l + 1)
                        link(nc.scalar.activation(grow[:, 4, :], grow[:, 3, :], ACT.Exp))
                        nc.scalar.activation(grow[:, 5, :], grow[:, 4, :], ACT.Ln, bias=1.0).then_inc(gr_log, 1)
                        t_ = us[2]
                        act.wait_ge(t_ready[t_.b], t_.m + 1)
                        nc.scalar.activation(gtok[:, :, TT:2 * TT],
                                             ps[:, 4 + t_.b, 0:TT * MH].rearrange("p (t h) -> p h t", h=MH),
                                             ACT.Exp, scale=-1.0).then_inc(t_free[t_.b], 1)
                for n in range(2):
                    act.wait_ge(g_free[cur["k", n].b], cur["k", n].m + 2)
                with w.loop(act, NG, per(LOOP)) as it:
                    I = l * NG + it
                    cur["I"] = I
                    restart()
                    nc.scalar.dma_start(bias[:, :, :], bass.AP(scr_w.tensor, scr_w.offset + it * (GH * BW),
                                                               [[1, P], [BW, GH], [1, 2 * P]])).then_inc(bias_in, 16)
                    nc.scalar.activation(kg[:, :], kdup[:, it, :], ACT.Copy)
                    nc.scalar.activation(vg[:, :, :], vtok[:, it, :, :], ACT.Copy).then_inc(staged_a, 1)
                    stu = {}
                    for s in LOOP:
                        us = take(s)
                        if s[0] in ("u0", "u1"):
                            gemm_step(s, cur["u"])
                        elif s[0] == "TV":
                            act.wait_ge(t_ready[us[0].b], us[0].m + 1)
                            nc.scalar.activation(vbuf[:, :, s[1] * P:(s[1] + 1) * P],
                                                 ps[:, 4 + us[0].b, :].rearrange("p (t d) -> p t d", t=TT), ACT.Copy)\
                                .then_inc(t_free[us[0].b], 1)
                        elif s[0] == "bc":
                            cur["bc"] = us[0]
                        elif s[0] == "ST":
                            tt = s[1]
                            stu[tt] = us[0]
                            if tt == 0:
                                act.wait_ge(o_ready[0], cur["bc"].m + 1)
                                act.wait_ge(staged_v, I + 1)
                            else:
                                act.wait_ge(s_free[stu[tt - 1].b], stu[tt - 1].m + 2)
                            act.wait_ge(dg_done, I * 4 + tt + 1)
                            last = nc.scalar.activation(Dm[:, tt * P:(tt + 1) * P], dg[:, :], ACT.Exp)
                            for c in range(tt):
                                last = nc.scalar.activation(Dm[:, c * P:(c + 1) * P], ps[:, 6, tt * P:(tt + 1) * P],
                                                            ACT.Exp, bias=gcur[:, c:c + 1])
                            last.then_inc(d_done if tt < TT - 1 else o_free[0], 1)
                        elif s[0] == "NUM":
                            tt = s[1]
                            act.wait_ge(t_free[us[0].b], us[0].m + 2)
                            nc.scalar.activation(junk, numsb[:, tt, 0:MDV], ACT.Square,
                                                 accum_out=st[:, 6, tt:tt + 1]).then_inc(ss_done, 1)
                        elif s == ("hnorm", 1):
                            act.wait_ge(hn_v, I + 1)
                            link(nc.scalar.activation(st[:, 9, 0:TT], st[:, 8, 0:TT], ACT.Ln, scale=1.0 / MDV, bias=EPS))
                            nc.scalar.activation(st[:, 10, 0:TT], st[:, 9, 0:TT], ACT.Exp, scale=-0.5).then_inc(hn_a, 1)
                        elif s[0] in ("S", "T"):
                            qt = s[2] // GH
                            attend_act(s, us, Pb, L, PT, min(qt + 1, 2), I * 16, s[2])
                        elif s[0] == "otail":
                            act.wait_ge(t1_done, I + 1)
                            nc.scalar.activation(st[:, 3, :], st[:, 2, :], ACT.Exp).then_inc(es_done, 1)
                        elif s[0] == "TA":
                            act.wait_ge(t_ready[us[0].b], us[0].m + 1)
                            nc.scalar.activation(ha32[:, 2 * it + s[1], :], ps[:, 4 + us[0].b, :], ACT.Copy)\
                                .then_inc(t_free[us[0].b], 1)
                stored()
                for b_ in range(2):
                    act.wait_ge(t_free[b_], w.next("T", b_) + 1)
                for src, dst in ((hm32, hm_hl[0]), (ha32, ha_hl[0])):
                    for k in range(KT):
                        nc.scalar.activation(dst[:, k, :], src[:, k, :], ACT.Copy).then_inc(mhi, 1)
                with w.loop(act, 4, per(MIX)) as i:
                    cur["ny"], cur["i2"] = l * KT + i * 2, i * 2
                    for s in MIX:
                        take(s)
                        gemm_step(s, cur["u"])
                with w.loop(act, 4, per(WOUT)) as i:
                    for s in WOUT:
                        take(s)
                        gemm_step(s, cur["u"])
                stored()
                norm(l * 2 + 1, x, lambda k: None, l * 2 + 1)
                with w.loop(act, 4, per(MLP)) as c:
                    for s in MLP:
                        take(s)
                        gemm_step(s, cur["u"])

            stored()
            gate_weights(DEPTH, gwn_raw)
            norm(DEPTH * 2, x, lambda k: None, None)
            cur["layer"] = False
            norm(DEPTH * 2 + 1, x, lambda k: act.wait_ge(x_done, k + 1), DEPTH * 2)
            restart()
            gate_weights_hi(DEPTH, gwn_raw, gwn)
            act.wait_ge(h_ready, (DEPTH * 2 + 1) * KT)
            for dst, src in ((w1[0][:, :, :], w1_in[0]), (w1[1][:, :, :], w1_in[1]), (w2[:, :, :, :], w2_in),
                             (oh_c[:, :], onehot_c), (tabn2[:, :], tab_n), (posb[:, :, :], pos_in)):
                nc.scalar.dma_start(dst, src).then_inc(late_in_s, 16)
            for s in NPRE:
                us = take(s)
                if s[0] in ("u0", "u1"):
                    gemm_step(s, cur["u"])
                elif s[0] == "TK":
                    act.wait_ge(t_ready[us[0].b], us[0].m + 1)
                    tk = ps[:, 4 + us[0].b, :].rearrange("p (t d) -> p t d", t=TT)
                    dst, g0 = vts[s[1] // 2], 2 * (s[1] % 2)
                    link(nc.scalar.activation(dst[:, g0, :, :], tk[:, :, 0:DH], ACT.Copy))
                    nc.scalar.activation(dst[:, g0 + 1, :, :], tk[:, :, DH:P], ACT.Copy).then_inc(t_free[us[0].b], 1)
                elif s[0] == "ngates":
                    act.wait_ge(o_ready[1], us[0].m + 1)
                    nc.scalar.activation(grow2[:, 0, :], ps[0:48, 7, :], ACT.Exp, scale=-1.0).then_inc(o_free[1], 1)
                elif s[0] == "compress":
                    act.wait_ge(cmp_pre, 4)
                    nc.scalar.activation(ehid[:, :, 0:NG * NC], hid[:, :, 0:NG * NC], ACT.Exp, scale=-1.0)\
                        .then_inc(cmp_exp, 1)
                    act.wait_ge(t_ready[0], us[2].m + 1)
                    kc = ps[0:DH, 4, 0:NG * NC].rearrange("p (g c) -> p g c", g=NG)
                    link(nc.scalar.activation(kcd[0:DH, :, 0:NC], kc, ACT.Copy))
                    nc.scalar.activation(kcd[DH:P, :, 0:NC], kc, ACT.Copy).then_inc(t_free[0], 1)
            for n in range(4):
                act.wait_ge(g_free[cur["k", n].b], cur["k", n].m + 2)
            for b_ in range(2):
                act.wait_ge(t_free[b_], w.next("T", b_) + 1)
            w.flush()
            with w.loop(act, NG, per(NLOOP)) as it:
                restart()
                nc.scalar.dma_start(biasn[:, :, :], bass.AP(scr_n.tensor, scr_n.offset + it * (GH * BN),
                                                            [[1, P], [BN, GH], [1, S]])).then_inc(bias_in, 16)
                for dst, src in ((kcg[:, 0:NC], kcd[:, it, 0:NC]), (vcg[:, :], vc[:, it, :]), (kgs[0][:, :], kds[0][:, it, :]),
                                 (kgs[1][:, :], kds[1][:, it, :]), (vgs[0][:, :, :], vts[0][:, it, :, :])):
                    nc.scalar.activation(dst, src, ACT.Copy)
                nc.scalar.activation(vgs[1][:, :, :], vts[1][:, it, :, :], ACT.Copy).then_inc(staged_a, 1)
                for s in NLOOP:
                    us = take(s)
                    if s[0] in ("u0", "u1"):
                        gemm_step(s, cur["u"])
                    elif s[0] == "CS":
                        act.wait_ge(cs_sub, it + 1)
                        nc.scalar.activation(Pn[:, 0, :].rearrange("p (j c) -> p j c", c=CP)[:, :, 0:NC],
                                             Ln_[:, 0, :].rearrange("p (j c) -> p j c", c=CP)[:, :, 0:NC],
                                             ACT.Exp, scale=-1.0).then_inc(cs_exp, 1)
                    elif s[0] == "CT":
                        act.wait_ge(t_ready[us[0].b], us[0].m + 1)
                        nc.scalar.activation(PTn[0:NC, s[1] % 2, :], ps[0:NC, 4 + us[0].b, :], ACT.Copy)\
                            .then_inc(t_free[us[0].b], 1)
                        cur["CT"] = us[0]
                    elif s[0] in ("S", "T"):
                        qt = s[2] // GH
                        attend_act(s, us, Pn, Ln_, PTn, qt + 1, None, s[2])
                    elif s == ("TO", 2, 0) or s == ("TO", 2, 1):
                        act.wait_ge(y_v, DEPTH * KT + it * 2 + s[2] + 1)
                        nc.scalar.activation(y_hl[0][:, 2 * it + s[2], :], y32[:, s[2], :], ACT.Copy).then_inc(y_hi_done, 1)
            for i in range(4):
                cur["i2"] = 2 * i
                cur["last"] = i == 3
                for s in NOUT:
                    take(s)
                    gemm_step(s, cur["u"])
            stored()
            norm(DEPTH * 2 + 2, y2, lambda k: None, None)

        @block.vector
        def _(dve):
            w = Walk()
            cur = {}
            chain = [0]

            def restart():
                dve.sem_clear(chain_v)
                chain[0] = 0

            def link(ins):
                chain[0] += 1
                ins.then_inc(chain_v, 1)
                dve.wait_ge(chain_v, chain[0])

            def settle():
                chain[0] += 1
                dve.sem_inc(chain_v, 1)
                dve.wait_ge(chain_v, chain[0])

            V = nc.vector

            def product(u):
                dve.wait_ge(used, u.n * 2 + 6)

            def take(s):
                us = [w.use(r) for r in takes(s)]
                if s[0] == "u0":
                    cur["u"] = cur[s[1:]] = us[0]
                if s[0] == "u1" and us:
                    cur["e"] = us[0]
                return us

            def sigmoid(e, dst):
                link(V.tensor_scalar(e_buf[:, e.b, :], e_buf[:, e.b, :], 1.0, None, ALU.add))
                V.reciprocal(dst, e_buf[:, e.b, :]).then_inc(e_done[e.b], 1)

            def store(s, u):
                kind, n = s[1], s[2]
                g = ps[:, u.b, :]
                if kind == "k":
                    dst = kdup if cur["layer"] else kds[n // 2]
                    product(u)
                    link(V.tensor_copy(dst[0:DH, 2 * (n % 2) + 1, :], ps[DH:P, u.b, :]))
                    cur["half"] += 2
                    dve.wait_ge(half_a, cur["half0"] + cur["half"])
                    V.tensor_copy(dst[DH:P, 2 * (n % 2) + 1, :], ps[DH:P, u.b, :]).then_inc(g_free[u.b], 1)
                elif kind == "x2":
                    cur["half"] += 2
                    dve.wait_ge(half_a, cur["half0"] + cur["half"])
                    link(V.tensor_copy(x2[n // 2][0:DH, 2 * (n % 2), :], ps[0:DH, u.b, :]))
                    V.tensor_copy(x2[n // 2][0:DH, 2 * (n % 2) + 1, :], ps[DH:P, u.b, :]).then_inc(g_free[u.b], 1)
                elif kind == "q":
                    product(u)
                    V.tensor_scalar((aq if cur["layer"] else qn)[:, n, :], g, -DH ** -0.5, None, ALU.mult)\
                        .then_inc(g_free[u.b], 1)
                elif kind == "conv":
                    if n == 1:
                        dve.wait_ge(mqk_done, cur["I"] * 2 + 1)
                    product(u)
                    c0 = 5 * n
                    link(V.tensor_scalar(cv[:, :], g, vcur[:, c0 + 3:c0 + 4], vcur[:, c0 + 4:c0 + 5], ALU.mult, ALU.add))
                    for back in (1, 2):
                        link(V.scalar_tensor_tensor(cv[:, back:S], ps[:, u.b, 0:S - back], vcur[:, c0 + 3 - back:c0 + 4 - back],
                                                    cv[:, back:S], ALU.mult, ALU.add))
                    V.scalar_tensor_tensor(cv[:, 3:S], ps[:, u.b, 0:S - 3], vcur[:, c0:c0 + 1], cv[:, 3:S],
                                           ALU.mult, ALU.add).then_inc(g_free[u.b], 1)
                    e = cur["e"]
                    dve.wait_ge(e_conv, cur["I"] * 2 + n + 1)
                    sigmoid(e, rbuf[:, :])
                    dve.wait_ge(e_done[e.b], e.m + 2)
                    V.scalar_tensor_tensor(mqk[:, n, :], cv[:, :], P ** -0.5 if n == 0 else 1.0, rbuf[:, :],
                                           ALU.mult, ALU.mult).then_inc(mqk_done, 1)
                elif kind in ("mo", "ga", "gb"):
                    dve.wait_ge(g_free[u.b], u.m + 2)
                    sigmoid(cur["e"], sigmo[:, n, :] if kind == "mo" else sig[:, kind == "gb", 2 * cur["it"] + n, :])
                elif kind == "z":
                    e = cur["e"]
                    dve.wait_ge(e_z, cur["it"] * 6 + n + 1)
                    sigmoid(e, rbufn[:, :])
                    dve.wait_ge(e_done[e.b], e.m + 2)
                    V.tensor_tensor(sz[:, n, :], g, rbufn[:, :], ALU.mult).then_inc(g_free[u.b], 1)
                elif kind == "up":
                    e = cur["e"]
                    dve.wait_ge(g_free[u.b], u.m + 2)
                    V.tensor_tensor(t3[:, n % 2, :], e_buf[:, e.b, :], e_buf[:, e.b, :], ALU.mult)\
                        .then_inc(e_done[e.b], 1)
                    dve.wait_ge(e_done[e.b], e.m + 2)
                    dve.wait_ge(u_hi_done, cur["nu"] + n + 1)
                    V.tensor_tensor(u_hl[1][:, n, :], t3[:, n % 2, :], u_hl[0][:, n, :].bitcast(F32), ALU.subtract)\
                        .then_inc(u_done, 1)
                elif kind == "pm":
                    product(u)
                    V.tensor_tensor(t3[:, n, :], g, sig[:, 0, cur["i2"] + n, :], ALU.mult).then_inc(g_free[u.b], 1)
                elif kind == "pa":
                    product(u)
                    V.tensor_tensor(t3[:, 2, :], g, sig[:, 1, cur["i2"] + n, :], ALU.mult).then_inc(g_free[u.b], 1)
                    dve.wait_ge(g_free[u.b], u.m + 2)
                    V.tensor_tensor(t3[:, n, :], t3[:, n, :], t3[:, 2, :], ALU.add).then_inc(y_v, 1)
                    dve.wait_ge(y_hi_done, cur["ny"] + n + 1)
                    V.tensor_tensor(y_hl[1][:, cur["i2"] + n, :], t3[:, n, :], y_hl[0][:, cur["i2"] + n, :].bitcast(F32),
                                    ALU.subtract).then_inc(y_done, 1)
                elif kind == "res":
                    product(u)
                    V.tensor_tensor(x[:, cur["i2"] + n, :], x[:, cur["i2"] + n, :], g, ALU.add).then_inc(g_free[u.b], 1)
                elif kind == "down":
                    product(u)
                    V.tensor_tensor(x[:, n, :], x[:, n, :], g, ALU.add).then_inc(g_free[u.b], 1)

            def norm(n, src, gain, mode):
                w.use("O1")
                dve.wait_ge(rs_ready, n + 1)
                for k in range(KT):
                    if mode[0] == "split":
                        if k >= 2:
                            dve.wait_ge(h_ready, mode[1] * KT + k - 1)
                        V.scalar_tensor_tensor(nt[:, k % 2, :], src[:, k, :], gain(k), rs[:, :], ALU.mult, ALU.mult)\
                            .then_inc(nt_ready, 1)
                        if k >= 1:
                            norm_lo(mode[1], k - 1)
                    elif mode[0] == "in place":
                        V.scalar_tensor_tensor(src[:, k, :], src[:, k, :], gain(k), rs[:, :], ALU.mult, ALU.mult)\
                            .then_inc(x_done, 1)
                    else:
                        link(V.scalar_tensor_tensor(nt[:, k % 2, :], src[:, k, :], gain(k), rs[:, :], ALU.mult, ALU.mult))
                        V.tensor_tensor(x[:, k, :], x[:, k, :], nt[:, k % 2, :], ALU.add).then_inc(x_done, 1)
                if mode[0] == "split":
                    norm_lo(mode[1], KT - 1)

            def norm_lo(m, k):
                dve.wait_ge(nhi_done, m * KT + k + 1)
                V.tensor_tensor(hT[1][:, k, :], nt[:, k % 2, :], hT[0][:, k, :].bitcast(F32), ALU.subtract)\
                    .then_inc(h_ready, 1)

            def gate_weights_lo(I, gw_raw, gw):
                dve.wait_ge(gwhi_done, I + 1)
                V.tensor_tensor(gw[1][:, :], gw_raw[:, :], gw[0][:, :].bitcast(F32), ALU.subtract).then_inc(gwlo_done, 1)

            def reverse(t, hd, n):
                v = t[:, hd, 0:n]
                return bass.AP(v.tensor, v.offset + n - 1, [v.ap[0], [-1, n]])

            def attend_dve(s, us, bias_t, Lbuf, PTbuf, nk, nP, first, j):
                n = nk * P
                if s[0] == "S":
                    b_ = us[0].b
                    dve.wait_ge(s_ready[b_], us[0].m + 1)
                    if j >= 2:
                        dve.wait_ge(probs, nP + j - 1)
                    settle()
                    V.tensor_tensor_reduce(out=Lbuf[:, j % 2, 0:n], in0=ps[:, 2 + b_, 0:n], in1=reverse(bias_t, j % GH, n),
                                           scale=1.0, scalar=first, op0=ALU.add, op1=ALU.min,
                                           accum_out=st[:, 0, j:j + 1]).then_inc(s_free[b_], 1)
                elif s[0] == "T" and j % 2 == 1:
                    dve.wait_ge(t_ready[us[0].b], us[0].m + 1)
                    V.tensor_copy(PTbuf[:, 1, 0:n], ps[:, 4 + us[0].b, 0:n]).then_inc(t_free[us[0].b], 1)

            def weighted_out(us, dst):
                for ob in range(2):
                    dve.wait_ge(o_ready[ob], us[ob].m + 1)
                    V.tensor_tensor(dst[:, 2 * ob:2 * ob + 2, :].rearrange("p q (h d) -> p (q h) d", d=DH),
                                    ps[:, 6 + ob, :].rearrange("p (j d) -> p j d", d=DH),
                                    st[:, 5, 8 * ob:8 * ob + 8].unsqueeze(2).broadcast_to([P, 8, DH]), ALU.mult)\
                        .then_inc(o_free[ob], 1)

            V.memset(ones[:, :], 1.0).then_inc(cst_done, 2)
            us = [w.use(r) for r in ("S", "S", "T", "T")]
            dve.wait_ge(s_ready[0], 1)
            V.tensor_copy(bw_sb[:, :], ps[0:16, 2, 0:BW]).then_inc(bw_done, 1)
            dve.wait_ge(bw_done, 1)
            dve.sem_inc(s_free[0], 1)
            dve.wait_ge(s_ready[1], 1)
            V.tensor_copy(bn_sb[:, 0:S], ps[0:16, 3, 0:S]).then_inc(bn_done, 1)
            for b_ in range(2):
                dve.wait_ge(t_ready[b_], 1)
                V.tensor_copy(bn_sb[:, S + 64 * b_:S + 64 * (b_ + 1)], ps[0:16, 4 + b_, 0:64]).then_inc(bn_done, 1)
            dve.wait_ge(bn_done, 3)
            for f in (s_free[1], *t_free):
                dve.sem_inc(f, 1)
            dve.wait_ge(cst_in, 16 * 11)

            with w.loop(dve, DEPTH, C_LAYER) as l:
                cur["layer"] = True
                cur["half0"], cur["half"] = l * 4, 0
                restart()
                link(V.tensor_copy(glay[:, :], vl[:, l, :]))
                norm(l * 2, x, lambda k: glay[:, k:k + 1], ("split", l * 2))
                gate_weights_lo(l, gw_raw, gw)
                for s in PRE:
                    us = take(s)
                    if s[0] == "u1":
                        store(s, cur["u"])
                    elif s[0] == "gates":
                        V.memset(grow[:, 10, :], 1.0)
                        V.memset(grow[:, 11, :], 0.0)
                        dve.wait_ge(o_ready[1], us[0].m + 1)
                        link(V.tensor_copy(grow[:, 0, :], ps[32:32 + MH, 7, :]))
                        V.tensor_scalar(grow[:, 1, :], ps[0:MH, 7, :], glay[0:MH, 16:17], None, ALU.add).then_inc(o_free[1], 1)
                        link(V.tensor_scalar(grow[:, 2, :], grow[:, 0, :], glay[0:MH, 17:18], None, ALU.add))
                        V.scalar_tensor_tensor(grow[:, 3, :], grow[:, 2, :], -1.0, grow[:, 2, :], ALU.mult, ALU.min).then_inc(gr_abs, 1)
                        dve.wait_ge(gr_log, l + 1)
                        link(V.scalar_tensor_tensor(grow[:, 6, :], grow[:, 2, :], 0.0, grow[:, 5, :], ALU.min, ALU.subtract))
                        link(V.tensor_tensor_scan(grow[:, 7, :], grow[:, 10, :], grow[:, 6, :], 0.0, ALU.mult, ALU.add))
                        link(V.tensor_tensor(grow[:, 8, :], grow[:, 1, :], grow[:, 7, :], ALU.subtract))
                        link(V.tensor_tensor_scan(grow[:, 0, :], grow[:, 11, :], grow[:, 8, :], 0.0, ALU.add, ALU.max))
                        link(V.tensor_scalar(negM[:, :], grow[:, 0, :], -1.0, None, ALU.mult))
                        V.tensor_tensor(grow[:, 9, :], grow[:, 7, :], grow[:, 0, :], ALU.add).then_inc(grows_done, 1)
                        t_ = us[1]
                        dve.wait_ge(t_ready[t_.b], t_.m + 1)
                        V.tensor_copy(gtok[:, :, 0:TT], ps[:, 4 + t_.b, 0:TT * MH].rearrange("p (t h) -> p h t", h=MH))\
                            .then_inc(t_free[t_.b], 1)
                        for t_ in us[1:]:
                            dve.wait_ge(t_free[t_.b], t_.m + 2)
                        V.memset(vbuf[:, :, MDV:MDV + 1], 1.0)
                with w.loop(dve, NG, per(LOOP)) as it:
                    I = l * NG + it
                    cur["I"], cur["it"] = I, it
                    restart()
                    V.tensor_copy(gcur[:, :], gtok[:, it, :])
                    link(V.tensor_copy(vcur[:, :], vit[:, I, :]))
                    V.tensor_scalar(st[:, 11, 0:GH], vcur[:, 12:16], -1.0, None, ALU.mult)
                    V.tensor_scalar(selh[:, :], ones[0:MH, :], vcur[0:MH, 16:17], None, ALU.mult).then_inc(staged_v, 1)
                    dve.wait_ge(staged_v, I + 1)
                    for s in LOOP:
                        us = take(s)
                        if s[0] == "u1":
                            store(s, cur["u"])
                        elif s[0] == "bc":
                            cur["bc"] = us[0]
                        elif s[0] == "ST":
                            tt, b_ = s[1], us[0].b
                            if tt == 0:
                                dve.wait_ge(o_ready[0], cur["bc"].m + 1)
                            V.scalar_tensor_tensor(dg[:, :], ps[:, 6, tt * P:(tt + 1) * P], gcur[:, tt:tt + 1], tri[:, :],
                                                   ALU.add, ALU.min).then_inc(dg_done, 1)
                            if tt < TT - 1:
                                dve.wait_ge(d_done, I * (TT - 1) + tt + 1)
                            else:
                                dve.wait_ge(o_free[0], cur["bc"].m + 2)
                            dve.wait_ge(s_ready[b_], us[0].m + 1)
                            V.tensor_tensor(PTm[:, tt % 2, 0:(tt + 1) * P], ps[:, 2 + b_, 0:(tt + 1) * P],
                                            Dm[:, 0:(tt + 1) * P], ALU.mult).then_inc(s_free[b_], 1)
                        elif s[0] == "NUM":
                            dve.wait_ge(t_ready[us[0].b], us[0].m + 1)
                            V.tensor_copy(numsb[:, s[1], 0:MDV + 1], ps[:, 4 + us[0].b, 0:MDV + 1])\
                                .then_inc(t_free[us[0].b], 1)
                            cur["num"] = us[0]
                        elif s == ("hnorm", 0):
                            dve.wait_ge(t_free[cur["num"].b], cur["num"].m + 2)
                            den = numsb[:, :, MDV:MDV + 1].rearrange("p t o -> p (t o)")
                            link(V.scalar_tensor_tensor(st[:, 4, 0:TT], den, -1.0, den, ALU.mult, ALU.max))
                            link(V.tensor_tensor(st[:, 4, 0:TT], st[:, 4, 0:TT], gcur[:, TT:2 * TT], ALU.max))
                            link(V.reciprocal(st[:, 7, 0:TT], st[:, 4, 0:TT]))
                            dve.wait_ge(ss_done, I * TT + TT)
                            link(V.tensor_tensor(st[:, 8, 0:TT], st[:, 6, 0:TT], st[:, 7, 0:TT], ALU.mult))
                            V.tensor_tensor(st[:, 8, 0:TT], st[:, 8, 0:TT], st[:, 7, 0:TT], ALU.mult).then_inc(hn_v, 1)
                        elif s == ("hnorm", 1):
                            dve.wait_ge(hn_a, I + 1)
                            link(V.tensor_tensor(st[:, 8, 4:4 + TT], st[:, 7, 0:TT], st[:, 10, 0:TT], ALU.mult))
                            for t in range(TT):
                                last = V.tensor_scalar(numsb[:, t, 0:MDV], numsb[:, t, 0:MDV], st[:, 8, 4 + t:5 + t], None,
                                                       ALU.mult)
                            last.then_inc(hm_done, 1)
                        elif s[0] in ("S", "T"):
                            if s == ("S", "w", 0):
                                dve.wait_ge(bias_in, I * 16 + 16)
                            qt, hd = s[2] // GH, s[2] % GH
                            attend_dve(s, us, bias, L, PT, min(qt + 1, 2), I * 16, st[:, 11, hd:hd + 1], s[2])
                        elif s[0] == "TH":
                            dve.wait_ge(t_ready[us[0].b], us[0].m + 1)
                            V.scalar_tensor_tensor(hm32[:, 2 * it + s[1], :], ps[:, 4 + us[0].b, :], vcur[:, 10 + s[1]:11 + s[1]],
                                                   sigmo[:, s[1], :], ALU.mult, ALU.mult).then_inc(t_free[us[0].b], 1)
                        elif s[0] == "otail":
                            dve.wait_ge(probs, I * 16 + 16)
                            V.tensor_tensor(st[:, 2, :].rearrange("p (q h) -> p q h", h=GH),
                                            st[:, 0, :].rearrange("p (q h) -> p q h", h=GH),
                                            vcur[:, 12:16].unsqueeze(1).broadcast_to([P, TT, GH]), ALU.add)\
                                .then_inc(t1_done, 1)
                            dve.wait_ge(es_done, I + 1)
                            link(V.tensor_tensor(st[:, 4, :], st[:, 1, :], st[:, 3, :], ALU.add))
                            link(V.reciprocal(st[:, 5, :], st[:, 4, :]))
                            weighted_out(us, ao)
                for src, hl, first in ((hm32, hm_hl, 0), (ha32, ha_hl, KT)):
                    for k in range(KT):
                        dve.wait_ge(mhi, l * 2 * KT + first + k + 1)
                        V.tensor_tensor(hl[1][:, k, :], src[:, k, :], hl[0][:, k, :].bitcast(F32), ALU.subtract)\
                            .then_inc(mlo, 1)
                with w.loop(dve, 4, per(MIX)) as i:
                    cur["ny"], cur["i2"] = l * KT + i * 2, i * 2
                    for s in MIX:
                        take(s)
                        if s[0] == "u1":
                            store(s, cur["u"])
                with w.loop(dve, 4, per(WOUT)) as i:
                    cur["i2"] = i * 2
                    for s in WOUT:
                        take(s)
                        if s[0] == "u1":
                            store(s, cur["u"])
                norm(l * 2 + 1, x, lambda k: glay[:, 8 + k:9 + k], ("split", l * 2 + 1))
                with w.loop(dve, 4, per(MLP)) as c:
                    cur["nu"] = l * 4 * KT + c * KT
                    for s in MLP:
                        take(s)
                        if s[0] == "u1":
                            store(s, cur["u"])

            cur["layer"] = False
            cur["half0"], cur["half"] = DEPTH * 4, 0
            restart()
            norm(DEPTH * 2, x, lambda k: vn[:, k:k + 1], ("in place",))
            norm(DEPTH * 2 + 1, x, lambda k: vn[:, 8 + k:9 + k], ("split", DEPTH * 2))
            gate_weights_lo(DEPTH, gwn_raw, gwn)
            V.memset(x2[0][:, 4, :], 0.0)
            V.memset(x2[1][:, 4, :], 0.0)
            V.memset(x2[0][DH:P, 0:4, S - 1:S], 0.0)
            link(V.memset(x2[1][DH:P, 0:4, S - 1:S], 0.0))
            dve.wait_ge(late_in_s, 16 * 6)
            for kv in range(2):
                V.tensor_copy(x2[kv][:, 4, 0:32:2], posb[:, kv, :]).then_inc(x2_pos, 1)
            for s in NPRE:
                us = take(s)
                if s[0] == "u1":
                    store(s, cur["u"])
                elif s[0] == "ngates":
                    dve.wait_ge(o_free[1], us[0].m + 2)
                    link(V.tensor_scalar(grow2[:, 0, :], grow2[:, 0, :], 1.0, None, ALU.add))
                    V.reciprocal(grow2[:, 1, :], grow2[:, 0, :]).then_inc(grows_done, 1)
                    for which in range(2):
                        t_ = us[1 + which]
                        dve.wait_ge(t_ready[t_.b], t_.m + 1)
                        for t in range(2):
                            for b_ in range(3):
                                tk = 2 * which + t
                                last = V.tensor_copy(
                                    gates[:, :, b_, tk * GH:(tk + 1) * GH],
                                    ps[:, 4 + t_.b, t * 48 + b_ * 16:t * 48 + (b_ + 1) * 16].rearrange("p (g d) -> p g d", g=NG))
                        last.then_inc(t_free[t_.b], 1)
                elif s[0] == "cmpbias":
                    for qt in range(TT):
                        b_ = us[qt].b
                        dve.wait_ge(s_ready[b_], us[qt].m + 1)
                        for g in range(NG):
                            last = V.tensor_copy(
                                bcmp[:, g, qt * GH:(qt + 1) * GH, 0:NC],
                                ps[:, 2 + b_, 0:NC * 16].rearrange("p (c h) -> p h c", h=16)[:, g * GH:(g + 1) * GH, :])
                        last.then_inc(s_free[b_], 1)
                elif s[0] == "compress":
                    for kv in range(2):
                        dve.wait_ge(o_ready[kv], us[kv].m + 1)
                        for m in range(2):
                            pre = ps[:, 6 + kv, m * 256:m * 256 + 5 * NC]
                            last = V.tensor_scalar(hid[:, 2 * kv + m, 0:NG * NC], pre[:, 0:NG * NC],
                                                   pre[:, NG * NC:NG * NC + 1], None, ALU.add)
                            last.then_inc(cmp_pre if m == 0 else o_free[kv], 1)
                    dve.wait_ge(o_free[1], us[1].m + 2)
                    dve.sem_inc(cmp_pre, 2)
                    dve.wait_ge(cmp_exp, 1)
                    link(V.tensor_scalar(ehid[:, :, 0:NG * NC], ehid[:, :, 0:NG * NC], 1.0, None, ALU.add))
                    link(V.reciprocal(ehid[:, :, 0:NG * NC], ehid[:, :, 0:NG * NC]))
                    V.tensor_tensor(hid[:, :, 0:NG * NC], hid[:, :, 0:NG * NC], ehid[:, :, 0:NG * NC], ALU.mult)\
                        .then_inc(hid_done, 1)
                    dve.wait_ge(t_ready[1], us[3].m + 1)
                    V.tensor_copy(vc[:, :, :], ps[0:NC, 5, 0:NG * DH].rearrange("p (g d) -> p g d", g=NG))\
                        .then_inc(t_free[1], 1)
                    dve.wait_ge(t_free[1], us[3].m + 2)
            w.flush()
            cj = lambda t: t[:, 0, :].rearrange("p (j c) -> p j c", c=CP)
            with w.loop(dve, NG, per(NLOOP)) as it:
                cur["it"] = it
                restart()
                link(V.tensor_copy(gat[:, :, :], gates[:, it, :, :]))
                for s in NLOOP:
                    us = take(s)
                    if s[0] == "u1":
                        store(s, cur["u"])
                    elif s[0] == "CS":
                        for b_ in range(2):
                            dve.wait_ge(s_ready[b_], us[b_].m + 1)
                            V.tensor_tensor(cj(Ln_)[:, b_::2, 0:NC],
                                            ps[:, 2 + b_, 0:8 * CP].rearrange("p (j c) -> p j c", c=CP)[:, :, 0:NC],
                                            bcmp[:, it, b_::2, 0:NC], ALU.add).then_inc(s_free[b_], 1)
                        dve.wait_ge(s_free[1], us[1].m + 2)
                        link(V.tensor_reduce(st[:, 0, :], cj(Ln_)[:, :, 0:NC], AX.X, ALU.min))
                        V.tensor_tensor(cj(Ln_)[:, :, 0:NC], cj(Ln_)[:, :, 0:NC],
                                        st[:, 0, :].unsqueeze(2).broadcast_to([P, 16, NC]), ALU.subtract).then_inc(cs_sub, 1)
                    elif s[0] in ("S", "T"):
                        if s == ("S", "s", 0):
                            dve.wait_ge(bias_in, (DEPTH * NG + it) * 16 + 16)
                        br = 0 if s[1] == "s" else 1
                        attend_dve(s, us, biasn, Ln_, PTn, s[2] // GH + 1, (DEPTH * NG + it * 2 + br) * 16, 3e38, s[2])
                    elif s[0] == "otail":
                        br = "csf".index(s[1])
                        if br == 0:
                            dve.wait_ge(cs_exp, it + 1)
                            link(V.tensor_reduce(st[:, 1, :], cj(Pn)[:, :, 0:NC], AX.X, ALU.add))
                        else:
                            dve.wait_ge(probs, (DEPTH * NG + it * 2 + br) * 16)
                        link(V.reciprocal(st[:, 4, :], st[:, 1, :]))
                        link(V.tensor_tensor(st[:, 5, :], st[:, 4, :], gat[:, br, :], ALU.mult))
                        if br == 0:
                            link(V.tensor_scalar(st[:, 5, 0:GH], st[:, 5, 0:GH], late[:, :], None, ALU.mult))
                        weighted_out(us, aon)
                    elif s[0] == "TO":
                        br, n = s[1], s[2]
                        t = us[0]
                        dve.wait_ge(t_ready[t.b], t.m + 1)
                        V.tensor_tensor(y32[:, n, :] if br == 0 else tn[:, :], ps[:, 4 + t.b, :], sz[:, 2 * br + n, :],
                                        ALU.mult).then_inc(t_free[t.b], 1)
                        dve.wait_ge(t_free[t.b], t.m + 2)
                        if br == 1:
                            link(V.tensor_tensor(y32[:, n, :], y32[:, n, :], tn[:, :], ALU.add))
                        if br == 2:
                            V.tensor_tensor(y32[:, n, :], y32[:, n, :], tn[:, :], ALU.add).then_inc(y_v, 1)
                            dve.wait_ge(y_hi_done, DEPTH * KT + it * 2 + n + 1)
                            V.tensor_tensor(y_hl[1][:, 2 * it + n, :], y32[:, n, :],
                                            y_hl[0][:, 2 * it + n, :].bitcast(F32), ALU.subtract).then_inc(y_done, 1)
            norm(DEPTH * 2 + 2, y2, lambda k: vn[:, 16 + k:17 + k], ("add",))


def _bucket(n):
    n = np.maximum(n, 0)
    large = 16 + (np.log(np.maximum(n, 1) / 16) / np.log(128 / 16) * 16).astype(np.int32)
    return np.where(n < 16, n, np.minimum(large, 31))


def _onehot(dist, valid):
    a = np.zeros((33, len(dist)), np.float32)
    a[_bucket(dist), np.arange(len(dist))] = np.where(valid, -1.0, 0.0)
    a[32] = np.where(valid, 0.0, BIG)
    return a


def _units(w):
    k, n = w.shape
    a = np.asarray(w).reshape(k // D, KT, P, n // P, P)
    return a.transpose(0, 3, 2, 1, 4).reshape(-1, P, KT * P)


def _pad(cols, width=P):
    return np.concatenate([cols, np.zeros((cols.shape[0], width - cols.shape[1]), np.float32)], 1)


def kernel(**inp):
    import concourse.bacc as bacc
    from concourse.bass_utils import run_bass_kernel_spmd as run

    inp = {k: np.asarray(v) for k, v in inp.items()}
    per_unit, gate_w, v_it, v_l = [], [], [], []
    for l in range(DEPTH):
        wi = inp["w_in"][l]
        o = np.cumsum([0, 1024, 1024, 1024, 4, 4, 1024, 256, 256, 1024, 1024])
        U = {n: _units(wi[:, o[i]:o[i + 1]]) for n, i in (("mqk", 0), ("mv", 1), ("mo", 2), ("aq", 5), ("ak", 6), ("av", 7),
                                                         ("ga", 8), ("gb", 9))}
        gate_w.append(_units(_pad(np.concatenate([_pad(wi[:, o[3]:o[4]], 32), wi[:, o[4]:o[5]]], 1)))[0])
        per_unit += [U["ak"], U["av"]]
        for h in range(NG):
            per_unit += [U["mqk"][[h]], U["mqk"][[4 + h]]] + [U[n][2 * h:2 * h + 2] for n in ("mv", "aq", "mo", "ga", "gb")]
        pm, pa = _units(inp["w_branch_m"][l]), _units(inp["w_branch_a"][l])
        per_unit += [np.stack([pm, pa], 1).reshape(-1, P, KT * P), _units(inp["w_out"][l])]
        up, down = _units(inp["w_up"][l]), _units(inp["w_down"][l])
        for c in range(4):
            per_unit += [up[c * KT:(c + 1) * KT], down[c * KT:(c + 1) * KT]]
        cw, cb = inp["conv_w"][l], inp["conv_b"][l]
        for h in range(NG):
            v = np.zeros((P, VIT), np.float32)
            for n, c in ((0, h), (1, 4 + h)):
                v[:, 5 * n:5 * n + 4] = cw[:, c * P:(c + 1) * P].T
                v[:, 5 * n + 4] = cb[c * P:(c + 1) * P]
            v[:, 10:12] = inp["mlstm_norm_g"][l][2 * h * P:(2 * h + 2) * P].reshape(2, P).T
            v[:, 12:16] = inp["attn_sinks"][l][GH * h:GH * (h + 1)]
            v[h, 16] = 1.0
            v_it.append(v)
        v = np.zeros((P, VL), np.float32)
        v[:, 0:8] = inp["norm_mix_g"][l].reshape(KT, P).T
        v[:, 8:16] = inp["norm_mlp_g"][l].reshape(KT, P).T
        v[0:MH, 16], v[0:MH, 17] = inp["b_igate"][l], inp["b_fgate"][l]
        v_l.append(v)
    wi = inp["nsa_w_in_2"][0]
    kv = _units(wi[:, 1024:2560])
    z = _units(wi[:, 2608:5680]).reshape(3, NG, 2, P, KT * P)
    q = _units(wi[:, 0:1024])
    per_unit += [kv[0:6], kv[6:8], kv[8:10], kv[10:12]]
    for g in range(NG):
        per_unit += [q[2 * g:2 * g + 2], z[:, g].reshape(6, P, KT * P)]
    per_unit.append(_units(inp["nsa_w_out_2"][0]))
    gate_w.append(_units(_pad(wi[:, 2560:2608]))[0])

    dist_w, dist_n, dist_c = np.arange(BW) - 127, np.arange(BN) - 127, np.arange(1024) - 511
    pairs = lambda a: a.reshape(16, P, -1).transpose(1, 0, 2)
    table = lambda a: np.concatenate([a, np.ones((1, 16), np.float32)], 0)
    s_ = np.arange(P)
    data = {
        "w_all": np.concatenate(per_unit, 0),
        "wg_all": np.stack(gate_w),
        "vec_it": np.stack(v_it, 1),
        "vec_l": np.stack(v_l, 1),
        "vec_n": np.concatenate([inp[n].reshape(KT, P).T for n in ("final_norm_g", "pre_norm_gain_2", "post_norm_gain_2")], 1),
        "ident_in": np.eye(P, dtype=np.float32),
        "tri_in": np.where(s_[:, None] <= s_[None, :], 0.0, -BIG),
        "onehot_w": _onehot(dist_w, (dist_w >= 0) & (dist_w < P)),
        "onehot_n": _onehot(dist_n, dist_n >= 0),
        "onehot_c": _onehot(dist_c, dist_c >= 0),
        "tab_w": table(inp["rel_bias"]),
        "tab_n": table(inp["rel_bias_table_2"]),
        "late_in": (s_ >= 31)[:, None],
        "x_in": inp["x"][0].T,
        "w1_in": np.stack([pairs(inp["nsa_cmp_k_w1_2"][0]), pairs(inp["nsa_cmp_v_w1_2"][0])]),
        "w2_in": np.stack([inp[n][0].reshape(2, P, DH).transpose(1, 0, 2) for n in ("nsa_cmp_k_w2_2", "nsa_cmp_v_w2_2")], 1),
        "pos_in": np.stack([inp[n][0].reshape(16, P).T for n in ("nsa_cmp_k_pos_2", "nsa_cmp_v_pos_2")], 1),
    }
    data = {k: np.ascontiguousarray(v, np.float32) for k, v in data.items()}
    assert data["w_all"].shape[0] == UNITS, data["w_all"].shape
    nc = bacc.Bacc("TRN2", target_bir_lowering=False, num_devices=1)
    aps = {k: nc.dram_tensor(k, v.shape, F32, kind="ExternalInput").ap() for k, v in data.items()}
    aps["scr_w"] = nc.dram_tensor("scr_w", [16, BW], F32).ap()
    aps["scr_n"] = nc.dram_tensor("scr_n", [16, BN], F32).ap()
    aps["out"] = nc.dram_tensor("out", [D, S], F32, kind="ExternalOutput").ap()
    two_layers_and_nsa(nc, **aps)
    got = run(nc, [data], core_ids=[0]).results[0]["out"]
    return np.ascontiguousarray(got.T)[None]
```

```python
from contextlib import ExitStack, contextmanager

import numpy as np
import concourse.bass as bass
from concourse import mybir

F32, F32R = mybir.dt.float32, mybir.dt.float32r
ALU, ACT, AX = mybir.AluOpType, mybir.ActivationFunctionType, mybir.AxisListType

P = 128
D = 1024
KT = D // P
S = 512
TT = S // P
DEPTH = 2
EPS = 1e-6
HALF = KT // 2 * P
BIG = 1e30
MH, MDV = 4, 256
VP = MDV + 2
DH = 64
GH = 4
NG = 4
BW = 3 * P
BN = 5 * P
NC = 31
CP = 32
SLOPE_CMP = 16
LAYER_UNITS, NSA_UNITS = 140, 52
UNITS = DEPTH * LAYER_UNITS + NSA_UNITS
VIT, VL, VN = 20, 18, 24



def unit(kind, n):
    return [("u0", kind, n), ("h0", kind, n), ("m1", kind, n), ("u1", kind, n)]


UNIT_STEPS = ("u0", "h0", "m1", "u1")


def attend_steps(name, fill, more=None):
    out, n = [], GH * TT
    more = {n + 1: [("ostat", name)], **(more or {})}
    for j in range(n + 4):
        if j >= 3 and j - 3 < n:
            out.append(("T", name, j - 3))
        if j < n:
            out.append(("S", name, j))
        if j >= 4:
            out.append(("V", name, j - 4))
        out += more.get(j, [])
        out += [("fill",)] * list(fill).count(j)
    return out


F = ("fill",)


def place_fill(steps, quarters):
    quarters = list(quarters)
    out = [quarters.pop(0) if s[0] == "fill" else s for s in steps]
    assert not quarters, len(quarters)
    return out


PRE = (unit("k", 0) + [("gates",)] + unit("k", 1) + unit("v", 0) + unit("v", 1)
       + [("TK", 0), ("TK", 1), ("gatesT",)])
LOOP = (
    unit("conv", 0) + unit("conv", 1) + unit("mv", 0) + unit("mv", 1)
    + [("TV", 0)] + unit("q", 0) + [("TV", 1), ("bc",)] + unit("q", 1)
    + place_fill(
        [("ST", 0), F, ("ST", 1), F, F, ("NUM", 0), ("ST", 2), F, F, ("NUM", 1), ("ST", 3), F, F, ("NUM", 2), F,
         ("NUM", 3), ("hnorm", 0)]
        + attend_steps("w", (0, 1, 1, 2, 2, 4, 5, 7, 8, 9, 11, 12, 14, 18), {3: [("hnorm", 1)], 6: [("hnorm", 2)],
                                                                           10: [("TH", 0), ("TH", 1)]})
        + [("otail", "w"), F, F, ("TA", 0), ("TA", 1)],
        unit("mo", 0) + unit("mo", 1) + unit("ga", 0) + unit("ga", 1) + unit("gb", 0) + unit("gb", 1)))
MIX = unit("pm", 0) + unit("pa", 0) + unit("pm", 1) + unit("pa", 1)
WOUT = unit("res", 0) + unit("res", 1)
MLP = sum((unit("up", n) for n in range(KT)), []) + sum((unit("down", n) for n in range(KT)), [])
NPRE = (unit("x2", 0) + [("ngates",)] + sum((unit("x2", n) for n in range(1, 4)), []) + unit("k", 0) + unit("k", 1) + unit("v", 0) + unit("v", 1)
        + [("TK", 0), ("TK", 1)] + unit("k", 2) + unit("k", 3) + unit("v", 2) + unit("v", 3)
        + [("TK", 2), ("TK", 3), ("ngatesT",), ("cmpbias",), ("compress",)])
NLOOP = (
    unit("q", 0) + unit("q", 1)
    + place_fill(
        [F, F, ("CS",), F, F, ("CT", 0), ("ostat", "c"), ("CT", 1), ("CV", 0), ("CT", 2), ("CV", 1), ("CT", 3), ("CV", 2),
         ("CV", 3), ("otail", "c")]
        + attend_steps("s", (0, 1, 2, 4, 6, 8, 10, 13, 18), {5: [("TO", 0, 0), ("TO", 0, 1)]}) + [("otail", "s")]
        + attend_steps("f", (0, 1, 2, 4, 7, 10, 13, 18), {3: [("TO", 1, 0), ("TO", 1, 1)]}) + [("otail", "f")]
        + [F, F, F, ("TO", 2, 0), ("TO", 2, 1)],
        sum((unit("z", n) for n in range(6)), [])))
NOUT = unit("y2", 0) + unit("y2", 1)

TAKES = {"u0": ["u"], "TK": ["T"], "gates": ["O1"], "gatesT": ["T", "T"], "TV": ["T"], "bc": ["O0"], "ST": ["S"], "NUM": ["T"],
         "S": ["S"], "T": ["T"], "TH": ["T"], "otail": ["O0", "O1"], "TA": ["T"], "ngates": ["O1"], "ngatesT": ["T", "T"],
         "cmpbias": ["O0"], "compress": ["O0", "O1", "T", "T"], "CS": ["S", "S"],
         "CT": ["T"], "TO": ["T"], "norm_": ["O1"]}
E_KINDS = ("conv", "mo", "ga", "gb", "up", "z")
PAIRED = ("u", "S", "T", "e")


def takes(step):
    out = list(TAKES.get(step[0], []))
    if step[0] == "u1" and step[1] in E_KINDS:
        out.append("e")
    return out


def per(steps):
    out = {}
    for s in steps:
        for r in takes(s):
            out[r] = out.get(r, 0) + 1
    for r in PAIRED:
        assert out.get(r, 0) % 2 == 0, (r, out)
    return out


def add(*counts):
    out = {}
    for times, c in counts:
        for r, n in c.items():
            out[r] = out.get(r, 0) + times * n
    return out


class Use:

    def __init__(self, b, m, n):
        self.b, self.m, self.n = b, m, n


class Walk:

    def __init__(self):
        self.n, self.half, self.seen = {}, {}, {}

    def use(self, r):
        k = self.seen.get(r, 0)
        self.seen[r] = k + 1
        if r in PAIRED:
            return Use(k % 2, self.half.get(r, 0) + k // 2, self.n.get(r, 0) + k)
        return Use(0, self.n.get(r, 0) + k, self.n.get(r, 0) + k)

    def next(self, r, b=0):
        k = self.seen.get(r, 0)
        return self.half.get(r, 0) + (k + 1 - b) // 2 if r in PAIRED else self.n.get(r, 0) + k

    def flush(self):
        for r, k in self.seen.items():
            self.n[r] = self.n.get(r, 0) + k
            self.half[r] = self.half.get(r, 0) + k // 2
        self.seen = {}

    @contextmanager
    def loop(self, eng, count, counts):
        self.flush()
        n0, h0 = dict(self.n), dict(self.half)
        with eng.Fori(0, count) as i:
            for r, c in counts.items():
                self.n[r] = i * c + n0.get(r, 0)
                self.half[r] = i * (c // 2) + h0.get(r, 0)
            yield i
            self.flush()
        self.n = {r: n0.get(r, 0) + count * counts.get(r, 0) for r in {**n0, **counts}}
        self.half = {r: h0.get(r, 0) + count * (counts.get(r, 0) // 2) for r in {**h0, **counts}}
        self.seen = {}


NORM = [("norm_",)]
C_LAYER = add((1, per(NORM)), (1, per(PRE)), (NG, per(LOOP)), (4, per(MIX)), (4, per(WOUT)), (1, per(NORM)), (4, per(MLP)))
assert C_LAYER["u"] == LAYER_UNITS
assert add((1, per(NPRE)), (NG, per(NLOOP)), (4, per(NOUT)))["u"] == NSA_UNITS


def two_layers_and_nsa(nc, w_all, wg_all, vec_it, vec_l, vec_n, ident_in, tri_in, onehot_w, onehot_n,
                       tab_w, tab_n, late_in, x_in, w1_in, w2_in, pos_in, scr_w, scr_n, out):
    ctx = ExitStack()
    with ctx:
        def sem(name):
            return ctx.enter_context(nc.semaphore(name))

        base = 16512
        top = [base]

        def new(name, shape, dt=F32, at=None):
            size = -(-4 * int(np.prod(shape[1:])) // 32) * 32
            off = top[0] if at is None else at[0]
            t = nc.alloc_sbuf_tensor_at(name, shape, dt, offset=off)
            if at is None:
                top[0] += size
            else:
                at[0] += size
            return t

        x = new("x", [P, KT, S])
        hT_at = top[0]
        hT = [new("hT_hi", [P, KT, S], F32R), new("hT_lo", [P, KT, S], F32R)]
        raw = new("w_raw", [P, 2, KT * P])
        w_hi = new("w_hi", [P, 4, HALF], F32R)
        w_lo = new("w_lo", [P, 4, HALF], F32R)
        ident = new("ident", [P, P])
        ones = new("ones", [P, P])
        tri = new("tri", [P, P])
        vit = new("vit", [P, DEPTH * NG, VIT])
        vl = new("vl", [P, DEPTH, VL])
        vn = new("vn", [P, VN])
        vcur = new("vcur", [P, VIT])
        glay = new("glay", [P, VL])
        late = new("late", [P, 1])
        st = new("st", [P, 12, 16])
        e_buf = new("e_buf", [P, 2, S])
        r32_at = top[0]
        top[0] += 32768
        sig_at = top[0]
        top[0] += 32768
        scr_at = top[0]

        hm32 = new("hm32", [P, KT, S], at=[r32_at])
        ha32 = new("ha32", [P, KT, S], at=[r32_at + 16384])
        u_hl = [new("u_hi", [P, KT, S], F32R, at=[r32_at]), new("u_lo", [P, KT, S], F32R, at=[r32_at + 16384])]
        gw_raw = new("gw_raw", [P, KT * P], at=[r32_at])
        gw = [new("gw_hi", [P, KT * P], F32R, at=[r32_at + 4096]), new("gw_lo", [P, KT * P], F32R, at=[r32_at + 8192])]
        sig = new("sig", [P, 2, KT, S], at=[sig_at])
        y_hl = [new("y_hi", [P, KT, S], F32R, at=[sig_at]), new("y_lo", [P, KT, S], F32R, at=[sig_at + 16384])]
        grow = new("grow", [MH, 12, S], at=[sig_at])
        a = [scr_at]
        mqk = new("mqk", [P, 2, S], at=a)
        vbuf = new("vbuf", [P, TT, VP], at=a)
        numsb = new("numsb", [P, TT, VP], at=a)
        aq = new("aq", [P, 2, S], at=a)
        kg = new("kg", [P, S], at=a)
        vg = new("vg", [P, TT, DH], at=a)
        kdup = new("kdup", [P, NG, S], at=a)
        vtok = new("vtok", [P, NG, TT, DH], at=a)
        bias = new("bias", [P, GH, 2 * P], at=a)
        L = new("L", [P, 2, 2 * P], at=a)
        PT = new("PT", [P, 2, 2 * P], at=a)
        PTm = new("PTm", [P, 2, S], at=a)
        Pb = new("Pb", [P, 3, 2 * P], at=[a[0] - 4096])
        Dm = new("Dm", [P, S], at=a)
        dg = new("dg", [P, P], at=a)
        sigmo = new("sigmo", [P, 2, S], at=a)
        ao = new("ao", [P, TT, GH * DH], at=a)
        cv = new("cv", [P, S], at=a)
        vtmp = new("vtmp", [P, 2, S], at=a)
        junk = vtmp[:, 0, 0:MDV]
        negM = new("negM", [MH, S], at=a)
        selh = new("selh", [MH, P], at=a)
        gtok = new("gtok", [P, MH, 2 * TT], at=a)
        gcur = new("gcur", [P, 2 * TT], at=a)
        loop_end = a[0]
        hm_hl = [new("hm_hi", [P, KT, S], F32R, at=[hT_at]), new("hm_lo", [P, KT, S], F32R, at=[hT_at + 16384])]
        a = [scr_at]
        ha_hl = [new("ha_hi", [P, KT, S], F32R, at=a), new("ha_lo", [P, KT, S], F32R, at=a)]
        sq = new("sq", [P, 2, S], at=a)
        nt = new("nt", [P, 2, S], at=a)
        rs = new("rs", [P, S], at=a)
        t3 = new("t3", [P, 3, S], at=a)
        ssq = new("ssq", [P, S], at=a)
        scr_after_norm = a[0]
        a, b = [r32_at], [scr_at]
        kds = [new("kds", [P, NG, S], at=a), new("kdf", [P, NG, S], at=a)]
        vts = [new("vts", [P, NG, TT, DH], at=a), new("vtf", [P, NG, TT, DH], at=a)]
        kcd = new("kcd", [P, NG, CP], at=a)
        vc = new("vc", [NC, NG, DH], at=a)
        gates = new("gates", [P, NG, 3, TT * GH], at=a)
        kcg, vcg = new("kcg", [P, CP], at=a), new("vcg", [NC, DH], at=a)
        gat = new("gat", [P, 3, TT * GH], at=a)
        vgs = [new("vgs", [P, TT, DH], at=a), new("vgf", [P, TT, DH], at=a)]
        assert a[0] <= sig_at
        y2 = new("y2", [P, KT, S], at=[r32_at])
        bcmp = new("bcmp", [P, NG, GH * TT, CP], at=b)
        b_loop = list(b)
        vtmpn = new("vtmpn", [P, 2, S], at=b)
        x2 = [new("x2k", [P, 5, S], at=b), new("x2v", [P, 5, S], at=b)]
        w1 = [new("w1k", [P, 16, 256], at=b), new("w1v", [P, 16, 256], at=[sig_at])]
        b[0] = max(b[0], scr_after_norm)
        gwn_raw = new("gwn_raw", [P, KT * P], at=b)
        gwn = [new("gwn_hi", [P, KT * P], F32R, at=b), new("gwn_lo", [P, KT * P], F32R, at=b)]
        assert b[0] <= 229368, b[0]
        w2 = new("w2", [P, 2, 2, DH], at=[sig_at + 16384])
        hid = new("hid", [P, 4, P], at=[sig_at + 18432])
        ehid = new("ehid", [P, 4, P], at=[sig_at + 20480])
        rows_n = new("rows_n", [16, BN], at=[sig_at + 22528])
        grow2 = new("grow2", [48, 2, S], at=[sig_at + 26688])
        posb = new("posb", [P, 2, 16], at=[sig_at + 30784])
        b = b_loop
        qn = new("qn", [P, 2, S], at=b)
        kgs = [new("kgs", [P, S], at=b), new("kgf", [P, S], at=b)]
        biasn = new("biasn", [P, GH, S], at=b)
        Ln_ = new("Ln", [P, 2, S], at=b)
        Pn = new("Pn", [P, 3, S], at=b)
        PTn = new("PTn", [P, 2, S], at=b)
        aon = new("aon", [P, TT, GH * DH], at=b)
        sz = new("sz", [P, 6, S], at=b)
        y32 = new("y32", [P, 2, S], at=b)
        tn = new("tn", [P, S], at=b)
        assert max(b[0], loop_end) <= 229368, (b[0], loop_end)
        a = [sig_at]
        oh_w, oh_n = new("oh_w", [33, BW], at=a), new("oh_n", [33, BN], at=a)
        tabw, tabn = new("tabw", [33, 16], at=a), new("tabn", [33, 16], at=a)
        bw_sb, bn_sb = new("bw_sb", [16, BW], at=a), new("bn_sb", [16, BN], at=a)

        ps = ctx.enter_context(nc.psum_tensor("ps", [P, 8, S], F32))
        bank = {("u", 0): 0, ("u", 1): 1, ("S", 0): 2, ("S", 1): 3, ("T", 0): 4, ("T", 1): 5, "O0": 6, "O1": 7}

        raw_in = [sem("raw_in0"), sem("raw_in1")]
        hi_done, lo_done = sem("w_hi_done"), sem("w_lo_done")
        used = sem("w_used")
        g_free = [sem("g_free0"), sem("g_free1")]
        s_ready, s_free = [sem("s_ready0"), sem("s_ready1")], [sem("s_free0"), sem("s_free1")]
        t_ready, t_free = [sem("t_ready0"), sem("t_ready1")], [sem("t_free0"), sem("t_free1")]
        o_ready, o_free = [sem("o_ready0"), sem("o_ready1")], [sem("o_free0"), sem("o_free1")]
        e_done = [sem("e_done0"), sem("e_done1")]
        e_conv, e_z = sem("tanh_conv"), sem("tanh_z")
        cst_in, cst_done = sem("consts_in"), sem("consts_made")
        bw_out, bn_out = sem("bias_window_out"), sem("bias_full_out")
        bw_done, bn_done = sem("bias_window_made"), sem("bias_full_made")
        x_done = sem("x_done")
        sq_ready, sq_used, rs_ready = sem("sq_ready"), sem("sq_used"), sem("rs_ready")
        nt_ready, nhi_done, h_ready = sem("nt_ready"), sem("norm_hi_done"), sem("h_ready")
        gw_in, gwhi_done, gwlo_done = sem("gate_w_in"), sem("gate_w_hi"), sem("gate_w_lo")
        gr_abs, gr_log, grows_done = sem("gate_rows_abs"), sem("gate_rows_log"), sem("gate_rows_done")
        half_a = sem("scalar_half_of_unit")
        staged_v, staged_a = sem("staged_vector"), sem("staged_scalar")
        bias_in = sem("bias_in")
        dg_done, d_done = sem("diag_done"), sem("decay_done")
        ss_done, hn_v, hn_a, hm_done = sem("sumsq_done"), sem("hnorm_vector"), sem("hnorm_scalar"), sem("hm_scaled")
        probs = sem("probs")
        t1_done, es_done = sem("sink_logit_done"), sem("sink_exp_done")
        mhi, mlo = sem("mix_in_hi"), sem("mix_in_lo")
        y_v, y_hi_done, y_done = sem("y_sum"), sem("y_hi_done"), sem("y_done")
        u_hi_done, u_done = sem("u_hi_done"), sem("u_done")
        late_in_s, x2_pos = sem("last_layer_in"), sem("x2_pos")
        cmp_pre, cmp_exp, hid_done = sem("cmp_hidden_pre"), sem("cmp_hidden_exp"), sem("cmp_hidden_done")
        cs_sub, cs_exp = sem("cmp_logits_done"), sem("cmp_probs")
        out_s = sem("out_stored")
        chain_v, chain_a = sem("vector_chain"), sem("scalar_chain")

        block = ctx.enter_context(nc.Block())

        @block.sync
        def _(sp):
            with sp.Fori(0, UNITS // 2) as i:
                for p in range(2):
                    sp.wait_ge(lo_done, i * 4 + 2 * p + 2)
                    nc.sync.dma_start(raw[:, p, :], w_all[2 * i + p]).then_inc(raw_in[p], 16)
            for k in range(KT):
                sp.wait_ge(x_done, KT + k + 1)
                nc.sync.dma_start(out[k * P:(k + 1) * P, :], x[:, k, :]).then_inc(out_s, 16)
            sp.wait_ge(out_s, 16 * KT)

        @block.gpsimd
        def _(pool):
            pool.sem_inc(lo_done, 4)
            with pool.Fori(0, UNITS // 2) as i:
                for h in range(4):
                    pool.wait_ge(hi_done, i * 4 + h + 1)
                    nc.gpsimd.tensor_tensor(w_lo[:, h, :], raw[:, h // 2, (h % 2) * HALF:(h % 2 + 1) * HALF],
                                            w_hi[:, h, :].bitcast(F32), ALU.subtract).then_inc(lo_done, 1)

        def squares(l):
            return KT + l * 5 * KT

        def step_uses(w, step):
            return [w.use(r) for r in takes(step)]

        @block.tensor
        def _(pe):
            w = Walk()
            cur = {}

            def quarter(s, u, hi, lo, waits=None):
                p, quarter_ = u.b, UNIT_STEPS.index(s[0])
                h = quarter_ // 2
                if quarter_ == 0:
                    pe.wait_ge(g_free[p], u.m + 1)
                if quarter_ % 2 == 0:
                    pe.wait_ge(lo_done, u.n * 2 + h + 5)
                for kk in range(2 * quarter_, 2 * quarter_ + 2):
                    k = kk - h * (KT // 2)
                    if waits is not None:
                        pe.wait_ge(*waits(kk))
                    wh, wl = w_hi[:, 2 * p + h, k * P:(k + 1) * P], w_lo[:, 2 * p + h, k * P:(k + 1) * P]
                    nc.tensor.matmul(ps[:, p, :], wh, hi[:, kk, :], start=(kk == 0), stop=False)
                    nc.tensor.matmul(ps[:, p, :], wh, lo[:, kk, :], start=False, stop=False)
                    last = nc.tensor.matmul(ps[:, p, :], wl, hi[:, kk, :], start=False, stop=(kk == KT - 1))
                if quarter_ % 2 == 1:
                    last.then_inc(used, 1)

            def norm_sum(count):
                use = step_uses(w, NORM[0])[0]
                pe.wait_ge(o_free[1], use.m + 1)
                pe.wait_ge(sq_used, count)
                nc.tensor.matmul(ps[:, 7, :], ones[:, :], ssq[:, :], start=True, stop=True).then_inc(o_ready[1], 1)

            def heads4(dst_bank, src, ready):
                for t in range(TT):
                    last = nc.tensor.transpose(ps[:, dst_bank, t * P:(t + 1) * P], src(t), ident[:, :])
                last.then_inc(ready, 1)

            def gate_gemm(I, use, gw):
                pe.wait_ge(gwlo_done, I + 1)
                pe.wait_ge(o_free[1], use.m + 1)
                for k in range(KT):
                    wh, wl = gw[0][:, k * P:(k + 1) * P], gw[1][:, k * P:(k + 1) * P]
                    nc.tensor.matmul(ps[:, 7, :], wh, hT[0][:, k, :], start=(k == 0), stop=False)
                    nc.tensor.matmul(ps[:, 7, :], wh, hT[1][:, k, :], start=False, stop=False)
                    last = nc.tensor.matmul(ps[:, 7, :], wl, hT[0][:, k, :], start=False, stop=(k == KT - 1))
                last.then_inc(o_ready[1], 1)

            def attend(step, us, q, kk, vv, I, wide, nI):
                kind, name, j = step
                qt, hd = j // GH, j % GH
                k0 = 0 if wide else max(qt - 1, 0)
                nk = qt + 1 - k0
                hp = DH * (hd % 2)
                if kind == "S":
                    pe.wait_ge(s_free[us[0].b], us[0].m + 1)
                    nc.tensor.matmul(ps[:, 2 + us[0].b, 0:nk * P], q[hp:hp + DH, hd // 2, qt * P:(qt + 1) * P],
                                     kk[hp:hp + DH, k0 * P:(qt + 1) * P], start=True, stop=True)\
                        .then_inc(s_ready[us[0].b], 1)
                elif kind == "T":
                    pe.wait_ge(t_free[us[0].b], us[0].m + 1)
                    pe.wait_ge(probs, nI + j + 1)
                    pb = cur["P"]
                    for c in range(nk):
                        last = nc.tensor.transpose(ps[:, 4 + us[0].b, c * P:(c + 1) * P],
                                                   pb[:, j % 3, c * P:(c + 1) * P], ident[:, :])
                    last.then_inc(t_ready[us[0].b], 1)
                    cur["Tuse", j] = us[0]
                else:
                    t = cur["Tuse", j]
                    pe.wait_ge(t_free[t.b], t.m + 2)
                    ob = qt // 2
                    if j % (2 * GH) == 0:
                        pe.wait_ge(o_free[ob], cur["Om"][ob] + 1)
                    pt = cur["PT"]
                    for c in range(nk):
                        last = nc.tensor.matmul(ps[:, 6 + ob, (qt % 2) * 256 + hd * DH:(qt % 2) * 256 + (hd + 1) * DH],
                                                pt[:, j % 2, c * P:(c + 1) * P], vv[:, k0 + c, :],
                                                start=(c == 0), stop=(c == nk - 1))
                    if j % (2 * GH) == 2 * GH - 1:
                        last.then_inc(o_ready[ob], 1)

            pe.wait_ge(cst_in, 16 * 11)
            pe.wait_ge(cst_done, 1)
            nc.tensor.matmul(ps[0:16, 2, 0:BW], tabw[:, :], oh_w[:, :], start=True, stop=True).then_inc(s_ready[0], 1)
            nc.tensor.matmul(ps[0:16, 3, 0:S], tabn[:, :], oh_n[:, 0:S], start=True, stop=True).then_inc(s_ready[1], 1)
            for b_ in range(2):
                nc.tensor.matmul(ps[0:16, 4 + b_, 0:64], tabn[:, :], oh_n[:, S + 64 * b_:S + 64 * (b_ + 1)],
                                 start=True, stop=True).then_inc(t_ready[b_], 1)
            for r in ("S", "S", "T", "T"):
                w.use(r)

            with w.loop(pe, DEPTH, C_LAYER) as l:
                norm_sum(squares(l))
                for s in PRE:
                    us = step_uses(w, s)
                    if s[0] == "u0":
                        cur["u"] = cur[s[1:]] = us[0]
                    if s[0] in UNIT_STEPS:
                        first = s[1:] == ("k", 0)
                        quarter(s, cur["u"], *hT,
                                  waits=(lambda k: (h_ready, l * 2 * KT + k + 1)) if first else None)
                    elif s[0] == "TK":
                        pe.wait_ge(t_free[us[0].b], us[0].m + 1)
                        vu = cur["v", s[1]]
                        pe.wait_ge(g_free[vu.b], vu.m + 2)
                        heads4(4 + us[0].b, lambda t: vtmp[:, s[1], t * P:(t + 1) * P], t_ready[us[0].b])
                    elif s[0] == "gates":
                        gate_gemm(l, us[0], gw)
                    elif s[0] == "gatesT":
                        pe.wait_ge(grows_done, l + 1)
                        for which in range(2):
                            t_ = us[which]
                            pe.wait_ge(t_free[t_.b], t_.m + 1)
                            for t in range(TT):
                                last = nc.tensor.matmul(ps[:, 4 + t_.b, t * MH:(t + 1) * MH],
                                                        grow[:, 8 + which, t * P:(t + 1) * P], ident[0:MH, 0:MH],
                                                        start=True, stop=True)
                            last.then_inc(t_ready[t_.b], 1)
                w.flush()
                with w.loop(pe, NG, per(LOOP)) as it:
                    I = l * NG + it
                    cur["P"], cur["PT"] = Pb, PT
                    stu, nu = {}, {}
                    for s in LOOP:
                        us = step_uses(w, s)
                        if s[0] == "u0":
                            cur["u"] = cur[s[1:]] = us[0]
                        if s[0] in UNIT_STEPS:
                            quarter(s, cur["u"], *hT)
                            if s[0:2] == ("u1", "conv"):
                                cur["conv", s[2], "e"] = us[0]
                        elif s[0] == "TV":
                            pe.wait_ge(t_free[us[0].b], us[0].m + 1)
                            vu = cur["mv", s[1]]
                            pe.wait_ge(g_free[vu.b], vu.m + 2)
                            heads4(4 + us[0].b, lambda t: vtmp[:, s[1], t * P:(t + 1) * P], t_ready[us[0].b])
                            cur["TV", s[1]] = us[0]
                        elif s[0] == "bc":
                            pe.wait_ge(o_free[0], us[0].m + 1)
                            pe.wait_ge(staged_v, I + 1)
                            nc.tensor.matmul(ps[:, 6, :], selh[:, :], negM[:, :], start=True, stop=True)\
                                .then_inc(o_ready[0], 1)
                        elif s[0] == "ST":
                            tt = s[1]
                            stu[tt] = us[0]
                            pe.wait_ge(s_free[us[0].b], us[0].m + 1)
                            if tt == 0:
                                for n in range(2):
                                    pe.wait_ge(e_done[cur["conv", n, "e"].b], cur["conv", n, "e"].m + 2)
                            for c in range(tt + 1):
                                last = nc.tensor.matmul(ps[:, 2 + us[0].b, c * P:(c + 1) * P],
                                                        mqk[:, 1, c * P:(c + 1) * P], mqk[:, 0, tt * P:(tt + 1) * P],
                                                        start=True, stop=True)
                            last.then_inc(s_ready[us[0].b], 1)
                        elif s[0] == "NUM":
                            tt = s[1]
                            pe.wait_ge(t_free[us[0].b], us[0].m + 1)
                            if tt == 0:
                                for v_ in range(2):
                                    pe.wait_ge(t_free[cur["TV", v_].b], cur["TV", v_].m + 2)
                            pe.wait_ge(s_free[stu[tt].b], stu[tt].m + 2)
                            for c in range(tt + 1):
                                last = nc.tensor.matmul(ps[:, 4 + us[0].b, 0:MDV + 1], PTm[:, tt % 2, c * P:(c + 1) * P],
                                                        vbuf[:, c, 0:MDV + 1], start=(c == 0), stop=(c == tt))
                            last.then_inc(t_ready[us[0].b], 1)
                        elif s[0] in ("S", "T", "V"):
                            if s == ("S", "w", 0):
                                for n in range(2):
                                    pe.wait_ge(g_free[cur["q", n].b], cur["q", n].m + 2)
                                pe.wait_ge(staged_a, I + 1)
                                cur["Om"] = [w.next("O0"), w.next("O1")]
                            attend(s, us, aq, kg, vg, I, False, I * 16)
                        elif s[0] == "TH":
                            pe.wait_ge(t_free[us[0].b], us[0].m + 1)
                            pe.wait_ge(hm_done, I + 1)
                            heads4(4 + us[0].b, lambda t: numsb[:, t, s[1] * P:(s[1] + 1) * P], t_ready[us[0].b])
                        elif s[0] == "otail":
                            cur["tail"] = us
                        elif s[0] == "TA":
                            pe.wait_ge(t_free[us[0].b], us[0].m + 1)
                            if s[1] == 0:
                                for o_ in range(2):
                                    pe.wait_ge(o_free[o_], cur["tail"][o_].m + 2)
                            heads4(4 + us[0].b, lambda t: ao[:, t, s[1] * P:(s[1] + 1) * P], t_ready[us[0].b])
                with w.loop(pe, 4, per(MIX)) as i:
                    for s in MIX:
                        us = step_uses(w, s)
                        if s[0] == "u0":
                            cur["u"] = us[0]
                        second = s[1] == "pa"
                        quarter(s, cur["u"], *(ha_hl if second else hm_hl),
                                  waits=(lambda k: (mlo, l * 2 * KT + second * KT + k + 1)) if s[2] == 0 else None)
                with w.loop(pe, 4, per(WOUT)) as i:
                    for s in WOUT:
                        us = step_uses(w, s)
                        if s[0] == "u0":
                            cur["u"] = us[0]
                        quarter(s, cur["u"], *y_hl,
                                  waits=(lambda k: (y_done, l * KT + k + 1)) if s[2] == 0 else None)
                norm_sum(squares(l) + KT)
                with w.loop(pe, 4, per(MLP)) as c:
                    for s in MLP:
                        us = step_uses(w, s)
                        if s[0] == "u0":
                            cur["u"] = us[0]
                        if s[1] == "up":
                            quarter(s, cur["u"], *hT,
                                      waits=(lambda k: (h_ready, l * 2 * KT + KT + k + 1)) if s[2] == 0 else None)
                        else:
                            quarter(s, cur["u"], *u_hl,
                                      waits=(lambda k: (u_done, l * 4 * KT + c * KT + k + 1)) if s[2] == 0 else None)

            norm_sum(squares(DEPTH))
            norm_sum(squares(DEPTH) + KT)
            for s in NPRE:
                us = step_uses(w, s)
                if s[0] == "u0":
                    cur["u"] = cur[s[1:]] = us[0]
                if s[0] in UNIT_STEPS:
                    first = s[1:] == ("x2", 0)
                    quarter(s, cur["u"], *hT,
                              waits=(lambda k: (h_ready, DEPTH * 2 * KT + k + 1)) if first else None)
                elif s[0] == "TK":
                    pe.wait_ge(t_free[us[0].b], us[0].m + 1)
                    vu = cur["v", s[1]]
                    pe.wait_ge(g_free[vu.b], vu.m + 2)
                    heads4(4 + us[0].b, lambda t: vtmpn[:, s[1] % 2, t * P:(t + 1) * P], t_ready[us[0].b])
                elif s[0] == "ngates":
                    gate_gemm(DEPTH, us[0], gwn)
                elif s[0] == "ngatesT":
                    pe.wait_ge(grows_done, DEPTH + 1)
                    for which in range(2):
                        t_ = us[which]
                        pe.wait_ge(t_free[t_.b], t_.m + 1)
                        for t in range(2):
                            tk = 2 * which + t
                            last = nc.tensor.transpose(ps[:, 4 + t_.b, t * 48:(t + 1) * 48],
                                                       grow2[:, 1, tk * P:(tk + 1) * P], ident[0:48, 0:48])
                        last.then_inc(t_ready[t_.b], 1)
                elif s[0] == "cmpbias":
                    pe.wait_ge(late_in_s, 16 * 5)
                    pe.wait_ge(o_free[0], us[0].m + 1)
                    for m in range(NC):
                        last = nc.tensor.transpose(ps[:, 6, m * 16:(m + 1) * 16],
                                                   rows_n[:, SLOPE_CMP * m:SLOPE_CMP * m + P], ident[0:16, 0:16])
                    last.then_inc(o_ready[0], 1)
                elif s[0] == "compress":
                    pe.wait_ge(x2_pos, 2)
                    for kv in range(2):
                        pe.wait_ge(o_free[kv], us[kv].m + 1)
                        for m in range(2):
                            for pr in range(16):
                                rhs = x2[kv][:, :, 2 * pr:2 * pr + SLOPE_CMP * (NC - 1) + 1:SLOPE_CMP]
                                last = nc.tensor.matmul(ps[:, 6 + kv, m * 256:m * 256 + 5 * NC],
                                                        w1[kv][:, pr, m * P:(m + 1) * P], rhs,
                                                        start=(pr == 0), stop=(pr == 15))
                        last.then_inc(o_ready[kv], 1)
                    pe.wait_ge(hid_done, 1)
                    pe.wait_ge(t_free[0], us[2].m + 1)
                    for m in range(2):
                        last = nc.tensor.matmul(ps[0:DH, 4, 0:NG * NC], w2[:, 0, m, :], hid[:, m, 0:NG * NC],
                                                start=(m == 0), stop=(m == 1))
                    last.then_inc(t_ready[0], 1)
                    pe.wait_ge(t_free[1], us[3].m + 1)
                    for g in range(NG):
                        for m in range(2):
                            last = nc.tensor.matmul(ps[0:NC, 5, g * DH:(g + 1) * DH], hid[:, 2 + m, g * NC:(g + 1) * NC],
                                                    w2[:, 1, m, :], start=(m == 0), stop=(m == 1))
                    last.then_inc(t_ready[1], 1)
            w.flush()
            with w.loop(pe, NG, per(NLOOP)) as it:
                cur["P"], cur["PT"] = Pn, PTn
                ctu = {}
                for s in NLOOP:
                    us = step_uses(w, s)
                    if s[0] == "u0":
                        cur["u"] = cur[s[1:]] = us[0]
                    if s[0] in UNIT_STEPS:
                        quarter(s, cur["u"], *hT)
                    elif s[0] == "CS":
                        for n in range(2):
                            pe.wait_ge(g_free[cur["q", n].b], cur["q", n].m + 2)
                        pe.wait_ge(staged_a, DEPTH * NG + it + 1)
                        pe.wait_ge(s_free[0], us[0].m + 1)
                        pe.wait_ge(s_free[1], us[1].m + 1)
                        for j in range(GH * TT):
                            qt, hd = j // GH, j % GH
                            hp = DH * (hd % 2)
                            last = nc.tensor.matmul(ps[:, 2 + j % 2, (j // 2) * CP:(j // 2) * CP + NC],
                                                    qn[hp:hp + DH, hd // 2, qt * P:(qt + 1) * P],
                                                    kcg[hp:hp + DH, 0:NC], start=True, stop=True)
                            if j >= GH * TT - 2:
                                last.then_inc(s_ready[j % 2], 1)
                        cur["Om"] = [w.next("O0"), w.next("O1")]
                    elif s[0] == "CT":
                        qt = s[1]
                        b_ = us[0].b
                        pe.wait_ge(cs_exp, it + 1)
                        pe.wait_ge(t_free[b_], us[0].m + 1)
                        for hd in range(GH):
                            j = qt * GH + hd
                            last = nc.tensor.transpose(ps[0:NC, 4 + b_, hd * P:(hd + 1) * P], Pn[:, 0, j * CP:j * CP + NC],
                                                       ident[:, :])
                        last.then_inc(t_ready[b_], 1)
                        cur["CT", qt] = us[0]
                    elif s[0] == "CV":
                        qt = s[1]
                        pe.wait_ge(t_free[cur["CT", qt].b], cur["CT", qt].m + 2)
                        ob = qt // 2
                        if qt % 2 == 0:
                            pe.wait_ge(o_free[ob], cur["Om"][ob] + 1)
                        for hd in range(GH):
                            last = nc.tensor.matmul(ps[:, 6 + ob, (qt % 2) * 256 + hd * DH:(qt % 2) * 256 + (hd + 1) * DH],
                                                    PTn[0:NC, qt % 2, hd * P:(hd + 1) * P], vcg[:, :], start=True, stop=True)
                        if qt % 2 == 1:
                            last.then_inc(o_ready[ob], 1)
                    elif s[0] in ("S", "T", "V"):
                        br = 0 if s[1] == "s" else 1
                        if s[0] == "S" and s[2] == 0:
                            cur["Om"] = [w.next("O0"), w.next("O1")]
                        attend(s, us, qn, kgs[br], vgs[br], it, True, DEPTH * NG * 16 + it * 32 + br * 16)
                    elif s[0] == "otail":
                        cur["tail"] = us
                    elif s[0] == "TO":
                        pe.wait_ge(t_free[us[0].b], us[0].m + 1)
                        for o_ in range(2):
                            pe.wait_ge(o_free[o_], cur["tail"][o_].m + 2)
                        heads4(4 + us[0].b, lambda t: aon[:, t, s[2] * P:(s[2] + 1) * P], t_ready[us[0].b])
            for i in range(4):
                for s in NOUT:
                    us = step_uses(w, s)
                    if s[0] == "u0":
                        cur["u"] = us[0]
                    first = i == 0 and s[2] == 0
                    quarter(s, cur["u"], *y_hl,
                              waits=(lambda k: (y_done, DEPTH * KT + k + 1)) if first else None)
            norm_sum(squares(DEPTH) + 2 * KT)

        @block.scalar
        def _(act):
            w = Walk()
            cur = {}
            chain = [0]

            def restart():
                act.sem_clear(chain_a)
                chain[0] = 0

            def link(ins):
                chain[0] += 1
                ins.then_inc(chain_a, 1)
                act.wait_ge(chain_a, chain[0])

            def split(n, half_n, p, h):
                if h == 0:
                    act.wait_ge(raw_in[p], half_n * 16 + 16)
                act.wait_ge(used, n * 2 + h + 1)
                nc.scalar.activation(w_hi[:, 2 * p + h, :], raw[:, p, h * HALF:(h + 1) * HALF], ACT.Copy)\
                    .then_inc(hi_done, 1)

            def product(u):
                act.wait_ge(used, u.n * 2 + 6)

            def gemm_step(s, u):
                if s[0] == "u1":
                    store(s, u)
                if s[0] in ("h0", "u1") and not cur.get("last"):
                    split(u.n + 2, u.m + 1, u.b, int(s[0][1]))

            def store(s, u):
                kind, n = s[1], s[2]
                g = ps[:, u.b, :]
                if kind == "k":
                    dst = kdup if cur["layer"] else kds[n // 2]
                    product(u)
                    for i in range(2):
                        nc.scalar.activation(dst[DH * i:DH * (i + 1), 2 * (n % 2), :], ps[0:DH, u.b, :], ACT.Copy)\
                            .then_inc(half_a, 1)
                elif kind == "x2":
                    product(u)
                    for i in range(2):
                        nc.scalar.activation(x2[n // 2][DH:P, 2 * (n % 2) + i, 0:S - 1],
                                             ps[DH * i:DH * (i + 1), u.b, 1:S], ACT.Copy).then_inc(half_a, 1)
                elif kind in ("v", "mv"):
                    product(u)
                    nc.scalar.activation((vtmp if cur["layer"] else vtmpn)[:, n % 2, :], g, ACT.Copy)\
                        .then_inc(g_free[u.b], 1)
                elif kind == "conv":
                    e = cur["e"]
                    act.wait_ge(g_free[u.b], u.m + 2)
                    act.wait_ge(e_done[e.b], e.m + 1)
                    nc.scalar.activation(e_buf[:, e.b, :], cv[:, :], ACT.Tanh, scale=0.5).then_inc(e_conv, 1)
                elif kind in ("mo", "ga", "gb"):
                    e = cur["e"]
                    product(u)
                    act.wait_ge(e_done[e.b], e.m + 1)
                    nc.scalar.activation(e_buf[:, e.b, :], g, ACT.Tanh, scale=0.5).then_inc(g_free[u.b], 1)
                elif kind == "z":
                    e = cur["e"]
                    product(u)
                    act.wait_ge(e_done[e.b], e.m + 1)
                    nc.scalar.activation(e_buf[:, e.b, :], g, ACT.Tanh, scale=0.5).then_inc(e_z, 1)
                elif kind == "up":
                    e = cur["e"]
                    product(u)
                    act.wait_ge(e_done[e.b], e.m + 1)
                    nc.scalar.activation(e_buf[:, e.b, :], g, ACT.Relu).then_inc(g_free[u.b], 1)
                    act.wait_ge(g_free[u.b], u.m + 2)
                    nc.scalar.activation(u_hl[0][:, n, :], e_buf[:, e.b, :], ACT.Square).then_inc(u_hi_done, 1)
                elif kind == "pa":
                    act.wait_ge(y_v, cur["ny"] + n + 1)
                    nc.scalar.activation(y_hl[0][:, cur["i2"] + n, :], t3[:, n, :], ACT.Copy).then_inc(y_hi_done, 1)
                elif kind in ("res", "down"):
                    act.wait_ge(g_free[u.b], u.m + 2)
                    square(x[:, (cur["i2"] if kind == "res" else 0) + n, :], cur["nsq"] + n, n % 2)
                elif kind == "y2":
                    product(u)
                    square(g, cur["nsq"] + n, n % 2)
                    nc.scalar.activation(y2[:, cur["i2"] + n, :], g, ACT.Copy).then_inc(g_free[u.b], 1)

            def take(s):
                us = [w.use(r) for r in takes(s)]
                if s[0] == "u0":
                    cur["u"] = cur[s[1:]] = us[0]
                if s[0] == "u1" and us:
                    cur["e"] = us[0]
                return us

            def ln_exp():
                nc.scalar.preload_act_table_set("natural_log_exp_and_others")

            def square(tile, n, b_, first=False):
                if not first:
                    act.wait_ge(sq_used, n - 1)
                nc.scalar.activation(sq[:, b_, :], tile, ACT.Square, scale=D ** -0.5).then_inc(sq_ready, 1)

            def norm(split_to):
                use = w.use("O1")
                act.wait_ge(o_ready[1], use.m + 1)
                nc.scalar.activation(rs[:, :], ps[:, 7, :], ACT.Ln, bias=EPS).then_inc(o_free[1], 1)
                act.wait_ge(o_free[1], use.m + 2)
                nc.scalar.activation(rs[:, :], rs[:, :], ACT.Exp, scale=-0.5).then_inc(rs_ready, 1)
                if split_to is not None:
                    for k in range(KT):
                        act.wait_ge(nt_ready, split_to * KT + k + 1)
                        nc.scalar.activation(hT[0][:, k, :], nt[:, k % 2, :], ACT.Copy).then_inc(nhi_done, 1)

            def stored(k=None):
                for b_ in range(2):
                    act.wait_ge(g_free[b_], w.next("u", b_) + 1)

            def gate_weights(I, gw_raw):
                nc.scalar.dma_start(gw_raw[:, :], wg_all[I]).then_inc(gw_in, 16)

            def gate_weights_hi(I, gw_raw, gw):
                act.wait_ge(gw_in, I * 16 + 16)
                nc.scalar.activation(gw[0][:, :], gw_raw[:, :], ACT.Copy).then_inc(gwhi_done, 1)

            def attend_act(s, us, Pbuf, Lbuf, PTbuf, nk, nI, j):
                n = nk * P
                if s[0] == "S":
                    act.wait_ge(s_free[us[0].b], us[0].m + 2)
                    if j >= 3:
                        t = cur["Tuse", j - 3]
                        act.wait_ge(t_ready[t.b], t.m + 1)
                    nc.scalar.activation(Pbuf[:, j % 3, 0:n], Lbuf[:, j % 2, 0:n], ACT.Exp, scale=-1.0,
                                         bias=st[:, 0, j:j + 1], accum_out=st[:, 1, j:j + 1]).then_inc(probs, 1)
                elif s[0] == "T":
                    cur["Tuse", j] = us[0]
                    if j % 2 == 0:
                        act.wait_ge(t_ready[us[0].b], us[0].m + 1)
                        nc.scalar.activation(PTbuf[:, 0, 0:n], ps[:, 4 + us[0].b, 0:n], ACT.Copy)\
                            .then_inc(t_free[us[0].b], 1)

            act.sem_inc(used, 4)
            for f in (*g_free, *s_free, *t_free, *o_free, *e_done):
                act.sem_inc(f, 1)
            for dst, src in ((x[:, :, :], x_in.rearrange("(k p) t -> p k t", p=P)), (ident[:, :], ident_in),
                             (tri[:, :], tri_in), (vit[:, :, :], vec_it), (vl[:, :, :], vec_l), (vn[:, :], vec_n),
                             (oh_w[:, :], onehot_w), (oh_n[:, :], onehot_n), (tabw[:, :], tab_w), (tabn[:, :], tab_n),
                             (late[:, :], late_in)):
                nc.scalar.dma_start(dst, src).then_inc(cst_in, 16)
            nc.scalar.preload_act_table(ACT.Exp)
            for p in range(2):
                for h in range(2):
                    split(p, 0, p, h)
            for r in ("S", "S", "T", "T"):
                w.use(r)
            act.wait_ge(bw_done, 1)
            nc.scalar.dma_start(scr_w, bw_sb[:, :]).then_inc(bw_out, 16)
            act.wait_ge(bn_done, 3)
            nc.scalar.dma_start(scr_n, bn_sb[:, :]).then_inc(bn_out, 16)
            act.wait_ge(cst_in, 16 * 11)
            act.wait_ge(bw_out, 16)
            act.wait_ge(bn_out, 16)

            for k in range(KT):
                square(x[:, k, :], k, k % 2, first=k < 2)
            with w.loop(act, DEPTH, C_LAYER) as l:
                cur["layer"] = True
                restart()
                ln_exp()
                stored()
                gate_weights(l, gw_raw)
                norm(l * 2)
                gate_weights_hi(l, gw_raw, gw)
                for s in PRE:
                    us = take(s)
                    if s[0] in UNIT_STEPS:
                        gemm_step(s, cur["u"])
                    elif s[0] == "TK":
                        act.wait_ge(t_ready[us[0].b], us[0].m + 1)
                        tk = ps[:, 4 + us[0].b, :].rearrange("p (t d) -> p t d", t=TT)
                        link(nc.scalar.activation(vtok[:, 2 * s[1], :, :], tk[:, :, 0:DH], ACT.Copy))
                        nc.scalar.activation(vtok[:, 2 * s[1] + 1, :, :], tk[:, :, DH:P], ACT.Copy)\
                            .then_inc(t_free[us[0].b], 1)
                    elif s[0] == "gates":
                        act.wait_ge(gr_abs, l + 1)
                        link(nc.scalar.activation(grow[:, 4, :], grow[:, 3, :], ACT.Exp))
                        nc.scalar.activation(grow[:, 5, :], grow[:, 4, :], ACT.Ln, bias=1.0).then_inc(gr_log, 1)
                    elif s[0] == "gatesT":
                        t_ = us[1]
                        act.wait_ge(t_ready[t_.b], t_.m + 1)
                        nc.scalar.activation(gtok[:, :, TT:2 * TT],
                                             ps[:, 4 + t_.b, 0:TT * MH].rearrange("p (t h) -> p h t", h=MH),
                                             ACT.Exp, scale=-1.0).then_inc(t_free[t_.b], 1)
                for n in range(2):
                    act.wait_ge(g_free[cur["k", n].b], cur["k", n].m + 2)
                with w.loop(act, NG, per(LOOP)) as it:
                    I = l * NG + it
                    cur["I"] = I
                    restart()
                    nc.scalar.dma_start(bias[:, :, :], bass.AP(scr_w.tensor, scr_w.offset + it * (GH * BW),
                                                               [[1, P], [BW, GH], [1, 2 * P]])).then_inc(bias_in, 16)
                    nc.scalar.activation(kg[:, :], kdup[:, it, :], ACT.Copy)
                    nc.scalar.activation(vg[:, :, :], vtok[:, it, :, :], ACT.Copy).then_inc(staged_a, 1)
                    stu = {}
                    for s in LOOP:
                        us = take(s)
                        if s[0] in UNIT_STEPS:
                            gemm_step(s, cur["u"])
                        elif s[0] == "TV":
                            act.wait_ge(t_ready[us[0].b], us[0].m + 1)
                            nc.scalar.activation(vbuf[:, :, s[1] * P:(s[1] + 1) * P],
                                                 ps[:, 4 + us[0].b, :].rearrange("p (t d) -> p t d", t=TT), ACT.Copy)\
                                .then_inc(t_free[us[0].b], 1)
                        elif s[0] == "bc":
                            cur["bc"] = us[0]
                        elif s[0] == "ST":
                            tt = s[1]
                            stu[tt] = us[0]
                            if tt == 0:
                                act.wait_ge(o_ready[0], cur["bc"].m + 1)
                                act.wait_ge(staged_v, I + 1)
                            else:
                                act.wait_ge(s_free[stu[tt - 1].b], stu[tt - 1].m + 2)
                            act.wait_ge(dg_done, I * 4 + tt + 1)
                            last = nc.scalar.activation(Dm[:, tt * P:(tt + 1) * P], dg[:, :], ACT.Exp)
                            for c in range(tt):
                                last = nc.scalar.activation(Dm[:, c * P:(c + 1) * P], ps[:, 6, tt * P:(tt + 1) * P],
                                                            ACT.Exp, bias=gcur[:, c:c + 1])
                            last.then_inc(d_done if tt < TT - 1 else o_free[0], 1)
                        elif s[0] == "NUM":
                            tt = s[1]
                            act.wait_ge(t_free[us[0].b], us[0].m + 2)
                            nc.scalar.activation(junk, numsb[:, tt, 0:MDV], ACT.Square, scale=MDV ** -0.5,
                                                 accum_out=st[:, 6, tt:tt + 1]).then_inc(ss_done, 1)
                        elif s == ("hnorm", 1):
                            ln_exp()
                            act.wait_ge(hn_v, I + 1)
                            link(nc.scalar.activation(st[:, 9, 0:TT], st[:, 8, 0:TT], ACT.Ln, bias=EPS))
                            nc.scalar.activation(st[:, 10, 0:TT], st[:, 9, 0:TT], ACT.Exp, scale=-0.5).then_inc(hn_a, 1)
                        elif s[0] in ("S", "T"):
                            qt = s[2] // GH
                            attend_act(s, us, Pb, L, PT, min(qt + 1, 2), I * 16, s[2])
                        elif s[0] == "ostat":
                            act.wait_ge(t1_done, I + 1)
                            nc.scalar.activation(st[:, 3, :], st[:, 2, :], ACT.Exp).then_inc(es_done, 1)
                        elif s[0] == "TA":
                            act.wait_ge(t_ready[us[0].b], us[0].m + 1)
                            nc.scalar.activation(ha32[:, 2 * it + s[1], :], ps[:, 4 + us[0].b, :], ACT.Copy)\
                                .then_inc(t_free[us[0].b], 1)
                stored()
                for b_ in range(2):
                    act.wait_ge(t_free[b_], w.next("T", b_) + 1)
                for src, dst in ((hm32, hm_hl[0]), (ha32, ha_hl[0])):
                    for k in range(KT):
                        nc.scalar.activation(dst[:, k, :], src[:, k, :], ACT.Copy).then_inc(mhi, 1)
                with w.loop(act, 4, per(MIX)) as i:
                    cur["ny"], cur["i2"] = l * KT + i * 2, i * 2
                    for s in MIX:
                        take(s)
                        gemm_step(s, cur["u"])
                with w.loop(act, 4, per(WOUT)) as i:
                    cur["nsq"], cur["i2"] = squares(l) + i * 2, i * 2
                    for s in WOUT:
                        take(s)
                        gemm_step(s, cur["u"])
                ln_exp()
                stored()
                norm(l * 2 + 1)
                with w.loop(act, 4, per(MLP)) as c:
                    cur["nsq"] = squares(l) + KT + c * KT
                    for s in MLP:
                        take(s)
                        gemm_step(s, cur["u"])

            ln_exp()
            stored()
            gate_weights(DEPTH, gwn_raw)
            norm(None)
            cur["layer"] = False
            for k in range(KT):
                act.wait_ge(x_done, k + 1)
                square(x[:, k, :], squares(DEPTH) + k, k % 2)
            norm(DEPTH * 2)
            restart()
            gate_weights_hi(DEPTH, gwn_raw, gwn)
            act.wait_ge(h_ready, (DEPTH * 2 + 1) * KT)
            for dst, src in ((w1[0][:, :, :], w1_in[0]), (w1[1][:, :, :], w1_in[1]), (w2[:, :, :, :], w2_in),
                             (rows_n[:, :], scr_n), (posb[:, :, :], pos_in)):
                nc.scalar.dma_start(dst, src).then_inc(late_in_s, 16)
            for s in NPRE:
                us = take(s)
                if s[0] in UNIT_STEPS:
                    gemm_step(s, cur["u"])
                elif s[0] == "TK":
                    act.wait_ge(t_ready[us[0].b], us[0].m + 1)
                    tk = ps[:, 4 + us[0].b, :].rearrange("p (t d) -> p t d", t=TT)
                    dst, g0 = vts[s[1] // 2], 2 * (s[1] % 2)
                    link(nc.scalar.activation(dst[:, g0, :, :], tk[:, :, 0:DH], ACT.Copy))
                    nc.scalar.activation(dst[:, g0 + 1, :, :], tk[:, :, DH:P], ACT.Copy).then_inc(t_free[us[0].b], 1)
                elif s[0] == "ngates":
                    act.wait_ge(o_ready[1], us[0].m + 1)
                    nc.scalar.activation(grow2[:, 0, :], ps[0:48, 7, :], ACT.Tanh, scale=0.5).then_inc(o_free[1], 1)
                elif s[0] == "compress":
                    act.wait_ge(cmp_pre, 4)
                    nc.scalar.activation(ehid[:, :, 0:NG * NC], hid[:, :, 0:NG * NC], ACT.Tanh, scale=0.5)\
                        .then_inc(cmp_exp, 1)
                    act.wait_ge(t_ready[0], us[2].m + 1)
                    kc = ps[0:DH, 4, 0:NG * NC].rearrange("p (g c) -> p g c", g=NG)
                    link(nc.scalar.activation(kcd[0:DH, :, 0:NC], kc, ACT.Copy))
                    nc.scalar.activation(kcd[DH:P, :, 0:NC], kc, ACT.Copy).then_inc(t_free[0], 1)
            for n in range(4):
                act.wait_ge(g_free[cur["k", n].b], cur["k", n].m + 2)
            for b_ in range(2):
                act.wait_ge(t_free[b_], w.next("T", b_) + 1)
            w.flush()
            with w.loop(act, NG, per(NLOOP)) as it:
                restart()
                nc.scalar.dma_start(biasn[:, :, :], bass.AP(scr_n.tensor, scr_n.offset + it * (GH * BN),
                                                            [[1, P], [BN, GH], [1, S]])).then_inc(bias_in, 16)
                for dst, src in ((kcg[:, 0:NC], kcd[:, it, 0:NC]), (vcg[:, :], vc[:, it, :]), (kgs[0][:, :], kds[0][:, it, :]),
                                 (kgs[1][:, :], kds[1][:, it, :]), (vgs[0][:, :, :], vts[0][:, it, :, :])):
                    nc.scalar.activation(dst, src, ACT.Copy)
                nc.scalar.activation(vgs[1][:, :, :], vts[1][:, it, :, :], ACT.Copy).then_inc(staged_a, 1)
                for s in NLOOP:
                    us = take(s)
                    if s[0] in UNIT_STEPS:
                        gemm_step(s, cur["u"])
                    elif s[0] == "CS":
                        act.wait_ge(cs_sub, it + 1)
                        nc.scalar.activation(Pn[:, 0, :].rearrange("p (j c) -> p j c", c=CP)[:, :, 0:NC],
                                             Ln_[:, 0, :].rearrange("p (j c) -> p j c", c=CP)[:, :, 0:NC],
                                             ACT.Exp, scale=-1.0).then_inc(cs_exp, 1)
                    elif s[0] == "CT":
                        act.wait_ge(t_ready[us[0].b], us[0].m + 1)
                        nc.scalar.activation(PTn[0:NC, s[1] % 2, :], ps[0:NC, 4 + us[0].b, :], ACT.Copy)\
                            .then_inc(t_free[us[0].b], 1)
                        cur["CT"] = us[0]
                    elif s[0] in ("S", "T"):
                        qt = s[2] // GH
                        attend_act(s, us, Pn, Ln_, PTn, qt + 1, None, s[2])
                    elif s == ("TO", 2, 0) or s == ("TO", 2, 1):
                        act.wait_ge(y_v, DEPTH * KT + it * 2 + s[2] + 1)
                        nc.scalar.activation(y_hl[0][:, 2 * it + s[2], :], y32[:, s[2], :], ACT.Copy).then_inc(y_hi_done, 1)
            for i in range(4):
                cur["i2"], cur["nsq"] = 2 * i, squares(DEPTH) + KT + 2 * i
                cur["last"] = i == 3
                for s in NOUT:
                    take(s)
                    gemm_step(s, cur["u"])
            ln_exp()
            stored()
            norm(None)

        @block.vector
        def _(dve):
            w = Walk()
            cur = {}
            chain = [0]

            def restart():
                dve.sem_clear(chain_v)
                chain[0] = 0

            def link(ins):
                chain[0] += 1
                ins.then_inc(chain_v, 1)
                dve.wait_ge(chain_v, chain[0])

            def settle():
                chain[0] += 1
                dve.sem_inc(chain_v, 1)
                dve.wait_ge(chain_v, chain[0])

            V = nc.vector

            def product(u):
                dve.wait_ge(used, u.n * 2 + 6)

            def take(s):
                us = [w.use(r) for r in takes(s)]
                if s[0] == "u0":
                    cur["u"] = cur[s[1:]] = us[0]
                if s[0] == "u1" and us:
                    cur["e"] = us[0]
                return us

            def sigmoid(e, dst):
                V.tensor_scalar(dst, e_buf[:, e.b, :], 0.5, 0.5, ALU.mult, ALU.add).then_inc(e_done[e.b], 1)

            def store(s, u):
                kind, n = s[1], s[2]
                g = ps[:, u.b, :]
                if kind == "k":
                    dst = kdup if cur["layer"] else kds[n // 2]
                    product(u)
                    link(V.tensor_copy(dst[0:DH, 2 * (n % 2) + 1, :], ps[DH:P, u.b, :]))
                    cur["half"] += 2
                    dve.wait_ge(half_a, cur["half0"] + cur["half"])
                    V.tensor_copy(dst[DH:P, 2 * (n % 2) + 1, :], ps[DH:P, u.b, :]).then_inc(g_free[u.b], 1)
                elif kind == "x2":
                    cur["half"] += 2
                    dve.wait_ge(half_a, cur["half0"] + cur["half"])
                    link(V.tensor_copy(x2[n // 2][0:DH, 2 * (n % 2), :], ps[0:DH, u.b, :]))
                    V.tensor_copy(x2[n // 2][0:DH, 2 * (n % 2) + 1, :], ps[DH:P, u.b, :]).then_inc(g_free[u.b], 1)
                elif kind == "q":
                    product(u)
                    V.tensor_scalar((aq if cur["layer"] else qn)[:, n, :], g, -DH ** -0.5, None, ALU.mult)\
                        .then_inc(g_free[u.b], 1)
                elif kind == "conv":
                    if n == 1:
                        dve.wait_ge(e_done[cur["conv_e"].b], cur["conv_e"].m + 2)
                    cur["conv_e"] = cur["e"]
                    product(u)
                    c0 = 5 * n
                    link(V.tensor_scalar(cv[:, :], g, vcur[:, c0 + 3:c0 + 4], vcur[:, c0 + 4:c0 + 5], ALU.mult, ALU.add))
                    for back in (1, 2):
                        link(V.scalar_tensor_tensor(cv[:, back:S], ps[:, u.b, 0:S - back], vcur[:, c0 + 3 - back:c0 + 4 - back],
                                                    cv[:, back:S], ALU.mult, ALU.add))
                    V.scalar_tensor_tensor(cv[:, 3:S], ps[:, u.b, 0:S - 3], vcur[:, c0:c0 + 1], cv[:, 3:S],
                                           ALU.mult, ALU.add).then_inc(g_free[u.b], 1)
                    e = cur["e"]
                    dve.wait_ge(e_conv, cur["I"] * 2 + n + 1)
                    V.scalar_tensor_tensor(mqk[:, n, :], e_buf[:, e.b, :], 1.0, cv[:, :], ALU.add, ALU.mult)\
                        .then_inc(e_done[e.b], 1)
                elif kind in ("mo", "ga", "gb"):
                    dve.wait_ge(g_free[u.b], u.m + 2)
                    sigmoid(cur["e"], sigmo[:, n, :] if kind == "mo" else sig[:, kind == "gb", 2 * cur["it"] + n, :])
                elif kind == "z":
                    e = cur["e"]
                    dve.wait_ge(e_z, cur["it"] * 6 + n + 1)
                    V.scalar_tensor_tensor(sz[:, n, :], e_buf[:, e.b, :], 1.0, g, ALU.add, ALU.mult).then_inc(g_free[u.b], 1)
                    dve.wait_ge(g_free[u.b], u.m + 2)
                    dve.sem_inc(e_done[e.b], 1)
                elif kind == "up":
                    e = cur["e"]
                    dve.wait_ge(g_free[u.b], u.m + 2)
                    V.tensor_tensor(t3[:, n % 2, :], e_buf[:, e.b, :], e_buf[:, e.b, :], ALU.mult)\
                        .then_inc(e_done[e.b], 1)
                    dve.wait_ge(e_done[e.b], e.m + 2)
                    dve.wait_ge(u_hi_done, cur["nu"] + n + 1)
                    V.tensor_tensor(u_hl[1][:, n, :], t3[:, n % 2, :], u_hl[0][:, n, :].bitcast(F32), ALU.subtract)\
                        .then_inc(u_done, 1)
                elif kind == "pm":
                    product(u)
                    V.tensor_tensor(t3[:, n, :], g, sig[:, 0, cur["i2"] + n, :], ALU.mult).then_inc(g_free[u.b], 1)
                elif kind == "pa":
                    product(u)
                    V.tensor_tensor(t3[:, 2, :], g, sig[:, 1, cur["i2"] + n, :], ALU.mult).then_inc(g_free[u.b], 1)
                    dve.wait_ge(g_free[u.b], u.m + 2)
                    V.tensor_tensor(t3[:, n, :], t3[:, n, :], t3[:, 2, :], ALU.add).then_inc(y_v, 1)
                    dve.wait_ge(y_hi_done, cur["ny"] + n + 1)
                    V.tensor_tensor(y_hl[1][:, cur["i2"] + n, :], t3[:, n, :], y_hl[0][:, cur["i2"] + n, :].bitcast(F32),
                                    ALU.subtract).then_inc(y_done, 1)
                elif kind == "res":
                    product(u)
                    V.tensor_tensor(x[:, cur["i2"] + n, :], x[:, cur["i2"] + n, :], g, ALU.add).then_inc(g_free[u.b], 1)
                    add_square(cur["nsq"] + n, n % 2)
                elif kind == "down":
                    product(u)
                    V.tensor_tensor(x[:, n, :], x[:, n, :], g, ALU.add).then_inc(g_free[u.b], 1)
                    add_square(cur["nsq"] + n, n % 2, first=n == 0)

            def add_square(n, b_, first=False):
                dve.wait_ge(sq_ready, n + 1)
                if first:
                    V.tensor_copy(ssq[:, :], sq[:, b_, :]).then_inc(sq_used, 1)
                else:
                    dve.wait_ge(sq_used, n)
                    V.tensor_tensor(ssq[:, :], ssq[:, :], sq[:, b_, :], ALU.add).then_inc(sq_used, 1)

            def norm(n, src, gain, mode):
                w.use("O1")
                dve.wait_ge(rs_ready, n + 1)
                for k in range(KT):
                    if mode[0] == "split":
                        if k >= 2:
                            dve.wait_ge(h_ready, mode[1] * KT + k - 1)
                        V.scalar_tensor_tensor(nt[:, k % 2, :], src[:, k, :], gain(k), rs[:, :], ALU.mult, ALU.mult)\
                            .then_inc(nt_ready, 1)
                        if k >= 1:
                            norm_lo(mode[1], k - 1)
                    elif mode[0] == "in place":
                        V.scalar_tensor_tensor(src[:, k, :], src[:, k, :], gain(k), rs[:, :], ALU.mult, ALU.mult)\
                            .then_inc(x_done, 1)
                        if k >= 1:
                            add_square(mode[1] + k - 1, (k - 1) % 2, first=k == 1)
                    else:
                        link(V.scalar_tensor_tensor(nt[:, k % 2, :], src[:, k, :], gain(k), rs[:, :], ALU.mult, ALU.mult))
                        V.tensor_tensor(x[:, k, :], x[:, k, :], nt[:, k % 2, :], ALU.add).then_inc(x_done, 1)
                if mode[0] == "split":
                    norm_lo(mode[1], KT - 1)
                elif mode[0] == "in place":
                    add_square(mode[1] + KT - 1, (KT - 1) % 2)

            def norm_lo(m, k):
                dve.wait_ge(nhi_done, m * KT + k + 1)
                V.tensor_tensor(hT[1][:, k, :], nt[:, k % 2, :], hT[0][:, k, :].bitcast(F32), ALU.subtract)\
                    .then_inc(h_ready, 1)

            def gate_weights_lo(I, gw_raw, gw):
                dve.wait_ge(gwhi_done, I + 1)
                V.tensor_tensor(gw[1][:, :], gw_raw[:, :], gw[0][:, :].bitcast(F32), ALU.subtract).then_inc(gwlo_done, 1)

            def reverse(t, hd, n):
                v = t[:, hd, 0:n]
                return bass.AP(v.tensor, v.offset + n - 1, [v.ap[0], [-1, n]])

            def attend_dve(s, us, bias_t, Lbuf, PTbuf, nk, nP, first, j):
                n = nk * P
                if s[0] == "S":
                    b_ = us[0].b
                    dve.wait_ge(s_ready[b_], us[0].m + 1)
                    if j >= 2:
                        dve.wait_ge(probs, nP + j - 1)
                    settle()
                    V.tensor_tensor_reduce(out=Lbuf[:, j % 2, 0:n], in0=ps[:, 2 + b_, 0:n], in1=reverse(bias_t, j % GH, n),
                                           scale=1.0, scalar=first, op0=ALU.add, op1=ALU.min,
                                           accum_out=st[:, 0, j:j + 1]).then_inc(s_free[b_], 1)
                elif s[0] == "T" and j % 2 == 1:
                    dve.wait_ge(t_ready[us[0].b], us[0].m + 1)
                    V.tensor_copy(PTbuf[:, 1, 0:n], ps[:, 4 + us[0].b, 0:n]).then_inc(t_free[us[0].b], 1)

            def weighted_out(us, dst):
                for ob in range(2):
                    dve.wait_ge(o_ready[ob], us[ob].m + 1)
                    V.tensor_tensor(dst[:, 2 * ob:2 * ob + 2, :].rearrange("p q (h d) -> p (q h) d", d=DH),
                                    ps[:, 6 + ob, :].rearrange("p (j d) -> p j d", d=DH),
                                    st[:, 5, 8 * ob:8 * ob + 8].unsqueeze(2).broadcast_to([P, 8, DH]), ALU.mult)\
                        .then_inc(o_free[ob], 1)

            V.memset(ones[:, :], 1.0).then_inc(cst_done, 2)
            us = [w.use(r) for r in ("S", "S", "T", "T")]
            dve.wait_ge(s_ready[0], 1)
            V.tensor_copy(bw_sb[:, :], ps[0:16, 2, 0:BW]).then_inc(bw_done, 1)
            dve.wait_ge(bw_done, 1)
            dve.sem_inc(s_free[0], 1)
            dve.wait_ge(s_ready[1], 1)
            V.tensor_copy(bn_sb[:, 0:S], ps[0:16, 3, 0:S]).then_inc(bn_done, 1)
            for b_ in range(2):
                dve.wait_ge(t_ready[b_], 1)
                V.tensor_copy(bn_sb[:, S + 64 * b_:S + 64 * (b_ + 1)], ps[0:16, 4 + b_, 0:64]).then_inc(bn_done, 1)
            dve.wait_ge(bn_done, 3)
            for f in (s_free[1], *t_free):
                dve.sem_inc(f, 1)
            dve.wait_ge(cst_in, 16 * 11)
            for k in range(KT):
                add_square(k, k % 2, first=k == 0)

            with w.loop(dve, DEPTH, C_LAYER) as l:
                cur["layer"] = True
                cur["half0"], cur["half"] = l * 4, 0
                restart()
                link(V.tensor_copy(glay[:, :], vl[:, l, :]))
                norm(l * 2, x, lambda k: glay[:, k:k + 1], ("split", l * 2))
                gate_weights_lo(l, gw_raw, gw)
                for s in PRE:
                    us = take(s)
                    if s[0] == "u1":
                        store(s, cur["u"])
                    elif s[0] == "gates":
                        V.memset(grow[:, 10, :], 1.0)
                        V.memset(grow[:, 11, :], 0.0)
                        dve.wait_ge(o_ready[1], us[0].m + 1)
                        link(V.tensor_copy(grow[:, 0, :], ps[32:32 + MH, 7, :]))
                        V.tensor_scalar(grow[:, 1, :], ps[0:MH, 7, :], glay[0:MH, 16:17], None, ALU.add).then_inc(o_free[1], 1)
                        link(V.tensor_scalar(grow[:, 2, :], grow[:, 0, :], glay[0:MH, 17:18], None, ALU.add))
                        V.scalar_tensor_tensor(grow[:, 3, :], grow[:, 2, :], -1.0, grow[:, 2, :], ALU.mult, ALU.min).then_inc(gr_abs, 1)
                        dve.wait_ge(gr_log, l + 1)
                        link(V.scalar_tensor_tensor(grow[:, 6, :], grow[:, 2, :], 0.0, grow[:, 5, :], ALU.min, ALU.subtract))
                        link(V.tensor_tensor_scan(grow[:, 7, :], grow[:, 10, :], grow[:, 6, :], 0.0, ALU.mult, ALU.add))
                        link(V.tensor_tensor(grow[:, 8, :], grow[:, 1, :], grow[:, 7, :], ALU.subtract))
                        link(V.tensor_tensor_scan(grow[:, 0, :], grow[:, 11, :], grow[:, 8, :], 0.0, ALU.add, ALU.max))
                        link(V.tensor_scalar(negM[:, :], grow[:, 0, :], -1.0, None, ALU.mult))
                        V.tensor_tensor(grow[:, 9, :], grow[:, 7, :], grow[:, 0, :], ALU.add).then_inc(grows_done, 1)
                    elif s[0] == "gatesT":
                        t_ = us[0]
                        dve.wait_ge(t_ready[t_.b], t_.m + 1)
                        V.tensor_copy(gtok[:, :, 0:TT], ps[:, 4 + t_.b, 0:TT * MH].rearrange("p (t h) -> p h t", h=MH))\
                            .then_inc(t_free[t_.b], 1)
                        for t_ in us:
                            dve.wait_ge(t_free[t_.b], t_.m + 2)
                        V.memset(vbuf[:, :, MDV:MDV + 1], 1.0)
                with w.loop(dve, NG, per(LOOP)) as it:
                    I = l * NG + it
                    cur["I"], cur["it"] = I, it
                    restart()
                    V.tensor_copy(gcur[:, :], gtok[:, it, :])
                    link(V.tensor_copy(vcur[:, :], vit[:, I, :]))
                    V.tensor_scalar(st[:, 11, 0:GH], vcur[:, 12:16], -1.0, None, ALU.mult)
                    V.tensor_scalar(selh[:, :], ones[0:MH, :], vcur[0:MH, 16:17], None, ALU.mult).then_inc(staged_v, 1)
                    dve.wait_ge(staged_v, I + 1)
                    for s in LOOP:
                        us = take(s)
                        if s[0] == "u1":
                            store(s, cur["u"])
                        elif s[0] == "bc":
                            cur["bc"] = us[0]
                        elif s[0] == "ST":
                            tt, b_ = s[1], us[0].b
                            if tt == 0:
                                dve.wait_ge(o_ready[0], cur["bc"].m + 1)
                            V.scalar_tensor_tensor(dg[:, :], ps[:, 6, tt * P:(tt + 1) * P], gcur[:, tt:tt + 1], tri[:, :],
                                                   ALU.add, ALU.min).then_inc(dg_done, 1)
                            if tt < TT - 1:
                                dve.wait_ge(d_done, I * (TT - 1) + tt + 1)
                            else:
                                dve.wait_ge(o_free[0], cur["bc"].m + 2)
                            dve.wait_ge(s_ready[b_], us[0].m + 1)
                            V.scalar_tensor_tensor(PTm[:, tt % 2, 0:(tt + 1) * P], ps[:, 2 + b_, 0:(tt + 1) * P],
                                                   0.25 * P ** -0.5, Dm[:, 0:(tt + 1) * P], ALU.mult, ALU.mult)\
                                .then_inc(s_free[b_], 1)
                        elif s[0] == "NUM":
                            dve.wait_ge(t_ready[us[0].b], us[0].m + 1)
                            V.tensor_copy(numsb[:, s[1], 0:MDV + 1], ps[:, 4 + us[0].b, 0:MDV + 1])\
                                .then_inc(t_free[us[0].b], 1)
                            cur["num"] = us[0]
                        elif s == ("hnorm", 0):
                            dve.wait_ge(t_free[cur["num"].b], cur["num"].m + 2)
                            den = numsb[:, :, MDV:MDV + 1].rearrange("p t o -> p (t o)")
                            link(V.scalar_tensor_tensor(st[:, 4, 0:TT], den, -1.0, den, ALU.mult, ALU.max))
                            link(V.tensor_tensor(st[:, 4, 0:TT], st[:, 4, 0:TT], gcur[:, TT:2 * TT], ALU.max))
                            link(V.reciprocal(st[:, 7, 0:TT], st[:, 4, 0:TT]))
                        elif s == ("hnorm", 1):
                            dve.wait_ge(ss_done, I * TT + TT)
                            link(V.tensor_tensor(st[:, 8, 0:TT], st[:, 6, 0:TT], st[:, 7, 0:TT], ALU.mult))
                            V.tensor_tensor(st[:, 8, 0:TT], st[:, 8, 0:TT], st[:, 7, 0:TT], ALU.mult).then_inc(hn_v, 1)
                        elif s == ("hnorm", 2):
                            dve.wait_ge(hn_a, I + 1)
                            link(V.tensor_tensor(st[:, 8, 4:4 + TT], st[:, 7, 0:TT], st[:, 10, 0:TT], ALU.mult))
                            for t in range(TT):
                                last = V.tensor_scalar(numsb[:, t, 0:MDV], numsb[:, t, 0:MDV], st[:, 8, 4 + t:5 + t], None,
                                                       ALU.mult)
                            last.then_inc(hm_done, 1)
                        elif s[0] in ("S", "T"):
                            if s == ("S", "w", 0):
                                dve.wait_ge(bias_in, I * 16 + 16)
                            qt, hd = s[2] // GH, s[2] % GH
                            attend_dve(s, us, bias, L, PT, min(qt + 1, 2), I * 16, st[:, 11, hd:hd + 1], s[2])
                        elif s[0] == "TH":
                            dve.wait_ge(t_ready[us[0].b], us[0].m + 1)
                            V.scalar_tensor_tensor(hm32[:, 2 * it + s[1], :], ps[:, 4 + us[0].b, :], vcur[:, 10 + s[1]:11 + s[1]],
                                                   sigmo[:, s[1], :], ALU.mult, ALU.mult).then_inc(t_free[us[0].b], 1)
                        elif s[0] == "ostat":
                            dve.wait_ge(probs, I * 16 + 16)
                            V.tensor_tensor(st[:, 2, :].rearrange("p (q h) -> p q h", h=GH),
                                            st[:, 0, :].rearrange("p (q h) -> p q h", h=GH),
                                            vcur[:, 12:16].unsqueeze(1).broadcast_to([P, TT, GH]), ALU.add)\
                                .then_inc(t1_done, 1)
                        elif s[0] == "otail":
                            dve.wait_ge(es_done, I + 1)
                            link(V.tensor_tensor(st[:, 4, :], st[:, 1, :], st[:, 3, :], ALU.add))
                            link(V.reciprocal(st[:, 5, :], st[:, 4, :]))
                            weighted_out(us, ao)
                for src, hl, first in ((hm32, hm_hl, 0), (ha32, ha_hl, KT)):
                    for k in range(KT):
                        dve.wait_ge(mhi, l * 2 * KT + first + k + 1)
                        V.tensor_tensor(hl[1][:, k, :], src[:, k, :], hl[0][:, k, :].bitcast(F32), ALU.subtract)\
                            .then_inc(mlo, 1)
                with w.loop(dve, 4, per(MIX)) as i:
                    cur["ny"], cur["i2"] = l * KT + i * 2, i * 2
                    for s in MIX:
                        take(s)
                        if s[0] == "u1":
                            store(s, cur["u"])
                link(V.memset(ssq[:, :], 0.0))
                with w.loop(dve, 4, per(WOUT)) as i:
                    cur["nsq"], cur["i2"] = squares(l) + i * 2, i * 2
                    for s in WOUT:
                        take(s)
                        if s[0] == "u1":
                            store(s, cur["u"])
                norm(l * 2 + 1, x, lambda k: glay[:, 8 + k:9 + k], ("split", l * 2 + 1))
                with w.loop(dve, 4, per(MLP)) as c:
                    cur["nu"], cur["nsq"] = l * 4 * KT + c * KT, squares(l) + KT + c * KT
                    for s in MLP:
                        take(s)
                        if s[0] == "u1":
                            store(s, cur["u"])

            cur["layer"] = False
            cur["half0"], cur["half"] = DEPTH * 4, 0
            restart()
            norm(DEPTH * 2, x, lambda k: vn[:, k:k + 1], ("in place", squares(DEPTH)))
            norm(DEPTH * 2 + 1, x, lambda k: vn[:, 8 + k:9 + k], ("split", DEPTH * 2))
            gate_weights_lo(DEPTH, gwn_raw, gwn)
            V.memset(x2[0][:, 4, :], 0.0)
            V.memset(x2[1][:, 4, :], 0.0)
            V.memset(x2[0][DH:P, 0:4, S - 1:S], 0.0)
            link(V.memset(x2[1][DH:P, 0:4, S - 1:S], 0.0))
            dve.wait_ge(late_in_s, 16 * 5)
            for kv in range(2):
                V.tensor_copy(x2[kv][:, 4, 0:32:2], posb[:, kv, :]).then_inc(x2_pos, 1)
            for s in NPRE:
                us = take(s)
                if s[0] == "u1":
                    store(s, cur["u"])
                elif s[0] == "ngates":
                    dve.wait_ge(o_free[1], us[0].m + 2)
                    V.tensor_scalar(grow2[:, 1, :], grow2[:, 0, :], 0.25, 0.25, ALU.mult, ALU.add).then_inc(grows_done, 1)
                elif s[0] == "ngatesT":
                    for which in range(2):
                        t_ = us[which]
                        dve.wait_ge(t_ready[t_.b], t_.m + 1)
                        for t in range(2):
                            for b_ in range(3):
                                tk = 2 * which + t
                                last = V.tensor_copy(
                                    gates[:, :, b_, tk * GH:(tk + 1) * GH],
                                    ps[:, 4 + t_.b, t * 48 + b_ * 16:t * 48 + (b_ + 1) * 16].rearrange("p (g d) -> p g d", g=NG))
                        last.then_inc(t_free[t_.b], 1)
                elif s[0] == "cmpbias":
                    link(V.memset(bcmp[:, :, :, :], BIG))
                    dve.wait_ge(o_ready[0], us[0].m + 1)
                    for qt in range(TT):
                        for g in range(NG):
                            n = min(NC, 8 * qt + 7)
                            v = ps[:, 6, (8 * qt + 6) * 16 + g * GH:(8 * qt + 6) * 16 + g * GH + 1]
                            last = V.tensor_copy(bcmp[:, g, qt * GH:(qt + 1) * GH, 0:n],
                                                 bass.AP(v.tensor, v.offset, [v.ap[0], [1, GH], [-16, n]]))
                    last.then_inc(o_free[0], 1)
                elif s[0] == "compress":
                    for kv in range(2):
                        dve.wait_ge(o_ready[kv], us[kv].m + 1)
                        for m in range(2):
                            pre = ps[:, 6 + kv, m * 256:m * 256 + 5 * NC]
                            last = V.tensor_scalar(hid[:, 2 * kv + m, 0:NG * NC], pre[:, 0:NG * NC],
                                                   pre[:, NG * NC:NG * NC + 1], None, ALU.add)
                            last.then_inc(cmp_pre if m == 0 else o_free[kv], 1)
                    dve.wait_ge(o_free[1], us[1].m + 2)
                    dve.sem_inc(cmp_pre, 2)
                    dve.wait_ge(cmp_exp, 1)
                    link(V.tensor_scalar(ehid[:, :, 0:NG * NC], ehid[:, :, 0:NG * NC], 0.5, 0.5, ALU.mult, ALU.add))
                    V.tensor_tensor(hid[:, :, 0:NG * NC], hid[:, :, 0:NG * NC], ehid[:, :, 0:NG * NC], ALU.mult)\
                        .then_inc(hid_done, 1)
                    dve.wait_ge(t_ready[1], us[3].m + 1)
                    V.tensor_copy(vc[:, :, :], ps[0:NC, 5, 0:NG * DH].rearrange("p (g d) -> p g d", g=NG))\
                        .then_inc(t_free[1], 1)
                    dve.wait_ge(t_free[1], us[3].m + 2)
            w.flush()
            cj = lambda t: t[:, 0, :].rearrange("p (j c) -> p j c", c=CP)
            with w.loop(dve, NG, per(NLOOP)) as it:
                cur["it"] = it
                restart()
                link(V.tensor_copy(gat[:, :, :], gates[:, it, :, :]))
                for s in NLOOP:
                    us = take(s)
                    if s[0] == "u1":
                        store(s, cur["u"])
                    elif s[0] == "CS":
                        for b_ in range(2):
                            dve.wait_ge(s_ready[b_], us[b_].m + 1)
                            V.tensor_tensor(cj(Ln_)[:, b_::2, 0:NC],
                                            ps[:, 2 + b_, 0:8 * CP].rearrange("p (j c) -> p j c", c=CP)[:, :, 0:NC],
                                            bcmp[:, it, b_::2, 0:NC], ALU.add).then_inc(s_free[b_], 1)
                        dve.wait_ge(s_free[1], us[1].m + 2)
                        link(V.tensor_reduce(st[:, 0, :], cj(Ln_)[:, :, 0:NC], AX.X, ALU.min))
                        V.tensor_tensor(cj(Ln_)[:, :, 0:NC], cj(Ln_)[:, :, 0:NC],
                                        st[:, 0, :].unsqueeze(2).broadcast_to([P, 16, NC]), ALU.subtract).then_inc(cs_sub, 1)
                    elif s[0] in ("S", "T"):
                        if s == ("S", "s", 0):
                            dve.wait_ge(bias_in, (DEPTH * NG + it) * 16 + 16)
                        br = 0 if s[1] == "s" else 1
                        attend_dve(s, us, biasn, Ln_, PTn, s[2] // GH + 1, (DEPTH * NG + it * 2 + br) * 16, 3e38, s[2])
                    elif s[0] == "ostat":
                        br = "csf".index(s[1])
                        if br == 0:
                            dve.wait_ge(cs_exp, it + 1)
                            link(V.tensor_reduce(st[:, 1, :], cj(Pn)[:, :, 0:NC], AX.X, ALU.add))
                        else:
                            dve.wait_ge(probs, (DEPTH * NG + it * 2 + br) * 16)
                        link(V.reciprocal(st[:, 4, :], st[:, 1, :]))
                        link(V.tensor_tensor(st[:, 5, :], st[:, 4, :], gat[:, br, :], ALU.mult))
                        if br == 0:
                            link(V.tensor_scalar(st[:, 5, 0:GH], st[:, 5, 0:GH], late[:, :], None, ALU.mult))
                    elif s[0] == "otail":
                        weighted_out(us, aon)
                    elif s[0] == "TO":
                        br, n = s[1], s[2]
                        t = us[0]
                        dve.wait_ge(t_ready[t.b], t.m + 1)
                        V.tensor_tensor(y32[:, n, :] if br == 0 else tn[:, :], ps[:, 4 + t.b, :], sz[:, 2 * br + n, :],
                                        ALU.mult).then_inc(t_free[t.b], 1)
                        dve.wait_ge(t_free[t.b], t.m + 2)
                        if br == 1:
                            link(V.tensor_tensor(y32[:, n, :], y32[:, n, :], tn[:, :], ALU.add))
                        if br == 2:
                            V.tensor_tensor(y32[:, n, :], y32[:, n, :], tn[:, :], ALU.add).then_inc(y_v, 1)
                            dve.wait_ge(y_hi_done, DEPTH * KT + it * 2 + n + 1)
                            V.tensor_tensor(y_hl[1][:, 2 * it + n, :], y32[:, n, :],
                                            y_hl[0][:, 2 * it + n, :].bitcast(F32), ALU.subtract).then_inc(y_done, 1)
            for k in range(KT):
                add_square(squares(DEPTH) + KT + k, k % 2, first=k == 0)
            norm(DEPTH * 2 + 2, y2, lambda k: vn[:, 16 + k:17 + k], ("add",))


def _bucket(n):
    n = np.maximum(n, 0)
    large = 16 + (np.log(np.maximum(n, 1) / 16) / np.log(128 / 16) * 16).astype(np.int32)
    return np.where(n < 16, n, np.minimum(large, 31))


def _onehot(dist, valid):
    a = np.zeros((33, len(dist)), np.float32)
    a[_bucket(dist), np.arange(len(dist))] = np.where(valid, -1.0, 0.0)
    a[32] = np.where(valid, 0.0, BIG)
    return a


def _units(w):
    k, n = w.shape
    a = np.asarray(w).reshape(k // D, KT, P, n // P, P)
    return a.transpose(0, 3, 2, 1, 4).reshape(-1, P, KT * P)


def _pad(cols, width=P):
    return np.concatenate([cols, np.zeros((cols.shape[0], width - cols.shape[1]), np.float32)], 1)


def kernel(**inp):
    import concourse.bacc as bacc
    from concourse.bass_utils import run_bass_kernel_spmd as run

    inp = {k: np.asarray(v) for k, v in inp.items()}
    per_unit, gate_w, v_it, v_l = [], [], [], []
    for l in range(DEPTH):
        wi = inp["w_in"][l]
        o = np.cumsum([0, 1024, 1024, 1024, 4, 4, 1024, 256, 256, 1024, 1024])
        U = {n: _units(wi[:, o[i]:o[i + 1]]) for n, i in (("mqk", 0), ("mv", 1), ("mo", 2), ("aq", 5), ("ak", 6), ("av", 7),
                                                         ("ga", 8), ("gb", 9))}
        gate_w.append(_units(_pad(np.concatenate([_pad(wi[:, o[3]:o[4]], 32), wi[:, o[4]:o[5]]], 1)))[0])
        per_unit += [U["ak"], U["av"]]
        for h in range(NG):
            per_unit += [U["mqk"][[h]], U["mqk"][[4 + h]]] + [U[n][2 * h:2 * h + 2] for n in ("mv", "aq", "mo", "ga", "gb")]
        pm, pa = _units(inp["w_branch_m"][l]), _units(inp["w_branch_a"][l])
        per_unit += [np.stack([pm, pa], 1).reshape(-1, P, KT * P), _units(inp["w_out"][l])]
        up, down = _units(inp["w_up"][l]), _units(inp["w_down"][l])
        for c in range(4):
            per_unit += [up[c * KT:(c + 1) * KT], down[c * KT:(c + 1) * KT]]
        cw, cb = inp["conv_w"][l], inp["conv_b"][l]
        for h in range(NG):
            v = np.zeros((P, VIT), np.float32)
            for n, c in ((0, h), (1, 4 + h)):
                v[:, 5 * n:5 * n + 4] = cw[:, c * P:(c + 1) * P].T
                v[:, 5 * n + 4] = cb[c * P:(c + 1) * P]
            v[:, 10:12] = inp["mlstm_norm_g"][l][2 * h * P:(2 * h + 2) * P].reshape(2, P).T
            v[:, 12:16] = inp["attn_sinks"][l][GH * h:GH * (h + 1)]
            v[h, 16] = 1.0
            v_it.append(v)
        v = np.zeros((P, VL), np.float32)
        v[:, 0:8] = inp["norm_mix_g"][l].reshape(KT, P).T
        v[:, 8:16] = inp["norm_mlp_g"][l].reshape(KT, P).T
        v[0:MH, 16], v[0:MH, 17] = inp["b_igate"][l], inp["b_fgate"][l]
        v_l.append(v)
    wi = inp["nsa_w_in_2"][0]
    kv = _units(wi[:, 1024:2560])
    z = _units(wi[:, 2608:5680]).reshape(3, NG, 2, P, KT * P)
    q = _units(wi[:, 0:1024])
    per_unit += [kv[0:6], kv[6:8], kv[8:10], kv[10:12]]
    for g in range(NG):
        per_unit += [q[2 * g:2 * g + 2], z[:, g].reshape(6, P, KT * P)]
    per_unit.append(_units(inp["nsa_w_out_2"][0]))
    gate_w.append(_units(_pad(wi[:, 2560:2608]))[0])

    dist_w, dist_n = np.arange(BW) - 127, np.arange(BN) - 127
    pairs = lambda a: a.reshape(16, P, -1).transpose(1, 0, 2)
    table = lambda a: np.concatenate([a, np.ones((1, 16), np.float32)], 0)
    s_ = np.arange(P)
    data = {
        "w_all": np.concatenate(per_unit, 0),
        "wg_all": np.stack(gate_w),
        "vec_it": np.stack(v_it, 1),
        "vec_l": np.stack(v_l, 1),
        "vec_n": np.concatenate([inp[n].reshape(KT, P).T for n in ("final_norm_g", "pre_norm_gain_2", "post_norm_gain_2")], 1),
        "ident_in": np.eye(P, dtype=np.float32),
        "tri_in": np.where(s_[:, None] <= s_[None, :], 0.0, -BIG),
        "onehot_w": _onehot(dist_w, (dist_w >= 0) & (dist_w < P)),
        "onehot_n": _onehot(dist_n, dist_n >= 0),
        "tab_w": table(inp["rel_bias"]),
        "tab_n": table(inp["rel_bias_table_2"]),
        "late_in": (s_ >= 31)[:, None],
        "x_in": inp["x"][0].T,
        "w1_in": np.stack([pairs(inp["nsa_cmp_k_w1_2"][0]), pairs(inp["nsa_cmp_v_w1_2"][0])]),
        "w2_in": np.stack([inp[n][0].reshape(2, P, DH).transpose(1, 0, 2) for n in ("nsa_cmp_k_w2_2", "nsa_cmp_v_w2_2")], 1),
        "pos_in": np.stack([inp[n][0].reshape(16, P).T for n in ("nsa_cmp_k_pos_2", "nsa_cmp_v_pos_2")], 1),
    }
    data = {k: np.ascontiguousarray(v, np.float32) for k, v in data.items()}
    assert data["w_all"].shape[0] == UNITS, data["w_all"].shape
    nc = bacc.Bacc("TRN2", target_bir_lowering=False, num_devices=1)
    aps = {k: nc.dram_tensor(k, v.shape, F32, kind="ExternalInput").ap() for k, v in data.items()}
    aps["scr_w"] = nc.dram_tensor("scr_w", [16, BW], F32).ap()
    aps["scr_n"] = nc.dram_tensor("scr_n", [16, BN], F32).ap()
    aps["out"] = nc.dram_tensor("out", [D, S], F32, kind="ExternalOutput").ap()
    two_layers_and_nsa(nc, **aps)
    got = run(nc, [data], core_ids=[0]).results[0]["out"]
    return np.ascontiguousarray(got.T)[None]
```

```python
from contextlib import ExitStack, contextmanager

import numpy as np
import concourse.bass as bass
from concourse import mybir

F32, F32R = mybir.dt.float32, mybir.dt.float32r
ALU, ACT, AX = mybir.AluOpType, mybir.ActivationFunctionType, mybir.AxisListType

P = 128
D = 1024
KT = D // P
S = 512
TT = S // P
DEPTH = 2
EPS = 1e-6
HALF = KT // 2 * P
BIG = 1e30
MH, MDV = 4, 256
VP = MDV + 2
DH = 64
GH = 4
NG = 4
BW = 3 * P
BN = 5 * P
NC = 31
CP = 32
STRIDE_CMP = 16
LAYER_UNITS, MIXER_UNITS, NSA_UNITS = 140, 76, 52
UNITS = DEPTH * LAYER_UNITS + NSA_UNITS
VIT, VL, VN = 20, 18, 24



def unit(kind, n):
    return [("u0", kind, n), ("h0", kind, n), ("m1", kind, n), ("u1", kind, n)]


UNIT_STEPS = ("u0", "h0", "m1", "u1")


def attend_steps(name, fill, more=None):
    out, n = [], GH * TT
    more = {n + 1: [("ostat", name)], **(more or {})}
    for j in range(n + 5):
        if j >= 3 and j - 3 < n:
            out.append(("T", name, j - 3))
        if j < n:
            out.append(("S", name, j))
        if j >= 5:
            out.append(("V", name, j - 5))
        out += more.get(j, [])
        out += [("fill",)] * list(fill).count(j)
    return out


F = ("fill",)


def place_fill(steps, quarters):
    quarters = list(quarters)
    out = [quarters.pop(0) if s[0] == "fill" else s for s in steps]
    assert not quarters, len(quarters)
    return out


PRE = (unit("k", 0) + [("gates",)] + unit("k", 1) + unit("v", 0) + unit("v", 1)
       + [("TK", 0), ("TK", 1), ("gatesT",)])
LOOP = (
    unit("conv", 0) + unit("conv", 1) + unit("mv", 0) + unit("mv", 1)
    + [("TV", 0)] + unit("q", 0) + [("TV", 1), ("bc",)] + unit("q", 1)
    + place_fill(
        [("ST", 0), F, ("ST", 1), F, F, ("NUM", 0), ("ST", 2), F, F, ("NUM", 1), ("ST", 3), F, F, ("NUM", 2), F,
         ("NUM", 3), ("hnorm", 0), F]
        + attend_steps("w", (1, 1, 2, 2, 4, 5, 7, 8, 9, 11, 12, 14, 19), {3: [("hnorm", 1)], 6: [("hnorm", 2)],
                                                                           10: [("TH", 0), ("TH", 1)]})
        + [("otail", "w"), F, F, ("TA", 0), ("TA", 1)],
        unit("mo", 0) + unit("mo", 1) + unit("ga", 0) + unit("ga", 1) + unit("gb", 0) + unit("gb", 1)))
MIX = unit("pm", 0) + unit("pa", 0) + unit("pm", 1) + unit("pa", 1)
WOUT = unit("res", 0) + unit("res", 1)
MLP = sum((unit("up", n) for n in range(KT)), []) + sum((unit("down", n) for n in range(KT)), [])
NPRE = (unit("x2", 0) + [("ngates",)] + sum((unit("x2", n) for n in range(1, 4)), [])
        + unit("k", 0) + [("cmpbias",)] + unit("k", 1) + unit("v", 0) + unit("v", 1) + [("TK", 0), ("TK", 1), ("hidden",)]
        + unit("k", 2) + unit("k", 3) + unit("v", 2) + unit("v", 3)
        + [("TK", 2), ("TK", 3), ("ngatesT",), ("compress",)])
NLOOP = (
    unit("q", 0) + [("klo",)] + unit("q", 1)
    + place_fill(
        [F, F, ("CS",), F, F, ("CT", 0), ("ostat", "c"), ("CT", 1), F, ("CV", 0), ("CT", 2), ("CV", 1), ("CT", 3), F, ("CV", 2),
         ("CV", 3), ("otail", "c")]
        + attend_steps("s", (0, 1, 2, 5, 8, 12, 19), {5: [("TO", 0, 0), ("TO", 0, 1)], 16: [("kf",)]}) + [("otail", "s")]
        + attend_steps("f", (0, 1, 2, 4, 7, 10, 13, 19), {3: [("TO", 1, 0), ("TO", 1, 1)]}) + [("otail", "f")]
        + [F, F, F, ("TO", 2, 0), ("TO", 2, 1)],
        sum((unit("z", n) for n in range(6)), [])))
NOUT = unit("y2", 0) + unit("y2", 1)

TAKES = {"u0": ["u"], "TK": ["T"], "gates": ["O1"], "gatesT": ["T", "T"], "TV": ["T"], "bc": ["O0"], "ST": ["S"], "NUM": ["T"],
         "S": ["S"], "T": ["T"], "TH": ["T"], "otail": ["O0", "O1"], "TA": ["T"], "ngates": ["O1"], "ngatesT": ["T", "T"],
         "cmpbias": ["O0"], "hidden": ["O0", "O1"], "compress": ["T", "T"], "CS": ["S", "S"],
         "CT": ["T"], "TO": ["T"], "norm_": ["O1"]}
E_KINDS = ("conv", "mo", "ga", "gb", "up", "z")
PAIRED = ("u", "S", "T", "e")


def takes(step):
    out = list(TAKES.get(step[0], []))
    if step[0] == "u1" and step[1] in E_KINDS:
        out.append("e")
    return out


def per(steps):
    out = {}
    for s in steps:
        for r in takes(s):
            out[r] = out.get(r, 0) + 1
    for r in PAIRED:
        assert out.get(r, 0) % 2 == 0, (r, out)
    return out


def add(*counts):
    out = {}
    for times, c in counts:
        for r, n in c.items():
            out[r] = out.get(r, 0) + times * n
    return out


class Use:

    def __init__(self, b, m, n):
        self.b, self.m, self.n = b, m, n


class Walk:

    def __init__(self):
        self.n, self.half, self.seen = {}, {}, {}

    def use(self, r):
        k = self.seen.get(r, 0)
        self.seen[r] = k + 1
        if r in PAIRED:
            return Use(k % 2, self.half.get(r, 0) + k // 2, self.n.get(r, 0) + k)
        return Use(0, self.n.get(r, 0) + k, self.n.get(r, 0) + k)

    def next(self, r, b=0):
        k = self.seen.get(r, 0)
        return self.half.get(r, 0) + (k + 1 - b) // 2 if r in PAIRED else self.n.get(r, 0) + k

    def flush(self):
        for r, k in self.seen.items():
            self.n[r] = self.n.get(r, 0) + k
            self.half[r] = self.half.get(r, 0) + k // 2
        self.seen = {}

    @contextmanager
    def loop(self, eng, count, counts):
        self.flush()
        n0, h0 = dict(self.n), dict(self.half)
        with eng.Fori(0, count) as i:
            for r, c in counts.items():
                self.n[r] = i * c + n0.get(r, 0)
                self.half[r] = i * (c // 2) + h0.get(r, 0)
            yield i
            self.flush()
        self.n = {r: n0.get(r, 0) + count * counts.get(r, 0) for r in {**n0, **counts}}
        self.half = {r: h0.get(r, 0) + count * (counts.get(r, 0) // 2) for r in {**h0, **counts}}
        self.seen = {}


NORM = [("norm_",)]
C_LAYER = add((1, per(NORM)), (1, per(PRE)), (NG, per(LOOP)), (4, per(MIX)), (4, per(WOUT)), (1, per(NORM)), (4, per(MLP)))
assert C_LAYER["u"] == LAYER_UNITS
assert add((1, per(NPRE)), (NG, per(NLOOP)), (4, per(NOUT)))["u"] == NSA_UNITS


def two_layers_and_nsa(nc, w_all, wg_all, vec_it, vec_l, vec_n, ident_in, tri_in, onehot_w, onehot_n,
                       tab_w, tab_n, late_in, x_in, w1_in, w2_in, pos_in, scr_w, scr_n, out):
    ctx = ExitStack()
    with ctx:
        def sem(name):
            return ctx.enter_context(nc.semaphore(name))

        base = 16512
        top = [base]

        def new(name, shape, dt=F32, at=None):
            size = -(-4 * int(np.prod(shape[1:])) // 32) * 32
            off = top[0] if at is None else at[0]
            t = nc.alloc_sbuf_tensor_at(name, shape, dt, offset=off)
            if at is None:
                top[0] += size
            else:
                at[0] += size
            return t

        x = new("x", [P, KT, S])
        hT_at = top[0]
        hT = [new("hT_hi", [P, KT, S], F32R), new("hT_lo", [P, KT, S], F32R)]
        raw = new("w_raw", [P, 2, KT * P])
        w_hi = new("w_hi", [P, 4, HALF], F32R)
        w_lo = new("w_lo", [P, 4, HALF], F32R)
        ident = new("ident", [P, P])
        ones = new("ones", [P, P])
        tri = new("tri", [P, P])
        vit = new("vit", [P, DEPTH * NG, VIT])
        vl = new("vl", [P, DEPTH, VL])
        vn = new("vn", [P, VN])
        vcur = new("vcur", [P, VIT])
        glay = new("glay", [P, VL])
        late = new("late", [P, 1])
        st = new("st", [P, 12, 16])
        e_buf = new("e_buf", [P, 2, S])
        r32_at = top[0]
        top[0] += 32768
        sig_at = top[0]
        top[0] += 32768
        scr_at = top[0]

        hm32 = new("hm32", [P, KT, S], at=[r32_at])
        ha32 = new("ha32", [P, KT, S], at=[r32_at + 16384])
        u_hl = [new("u_hi", [P, KT, S], F32R, at=[r32_at]), new("u_lo", [P, KT, S], F32R, at=[r32_at + 16384])]
        gw_raw = new("gw_raw", [P, KT * P], at=[r32_at])
        gw = [new("gw_hi", [P, KT * P], F32R, at=[r32_at + 4096]), new("gw_lo", [P, KT * P], F32R, at=[r32_at + 8192])]
        sig = new("sig", [P, 2, KT, S], at=[sig_at])
        y_hl = [new("y_hi", [P, KT, S], F32R, at=[sig_at]), new("y_lo", [P, KT, S], F32R, at=[sig_at + 16384])]
        grow = new("grow", [MH, 12, S], at=[sig_at])
        a = [scr_at]
        mqk = new("mqk", [P, 2, S], at=a)
        vbuf = new("vbuf", [P, TT, VP], at=a)
        numsb = new("numsb", [P, TT, VP], at=a)
        ao = new("ao", [P, TT, GH * DH], at=[a[0]])
        aq = new("aq", [P, GH, S], F32R, at=a)
        kg_hi = new("kg_hi", [P, S], F32R, at=a)
        vg = new("vg", [P, TT, DH], at=a)
        kdup = new("kdup", [P, NG, S], at=a)
        vtok = new("vtok", [P, NG, TT, DH], at=a)
        bias = new("bias", [P, GH, 2 * P], at=a)
        L = new("L", [P, 2, 2 * P], at=a)
        PT = new("PT", [P, 3, 2 * P], at=a)
        PTm = new("PTm", [P, 2, S], at=a)
        Pb = new("Pb", [P, 3, 2 * P], at=[a[0] - 4096])
        kg_lo = new("kg_lo", [P, S], F32R, at=[a[0]])
        Dm = new("Dm", [P, S], at=a)
        dg = new("dg", [P, P], at=a)
        sigmo = new("sigmo", [P, 2, S], at=a)
        cv = new("cv", [P, S], at=a)
        vtmp = new("vtmp", [P, 2, S], at=a)
        junk = vtmp[:, 0, 0:MDV]
        negM = new("negM", [MH, S], at=a)
        selh = new("selh", [MH, P], at=a)
        gtok = new("gtok", [P, MH, 2 * TT], at=a)
        gcur = new("gcur", [P, 2 * TT], at=a)
        loop_end = a[0]
        hm_hl = [new("hm_hi", [P, KT, S], F32R, at=[hT_at]), new("hm_lo", [P, KT, S], F32R, at=[hT_at + 16384])]
        a = [scr_at]
        ha_hl = [new("ha_hi", [P, KT, S], F32R, at=a), new("ha_lo", [P, KT, S], F32R, at=a)]
        sq = new("sq", [P, 2, S], at=a)
        nt = new("nt", [P, 3, S], at=a)
        rs = new("rs", [P, S], at=a)
        t3 = new("t3", [P, 3, S], at=a)
        ssq = new("ssq", [P, S], at=a)
        scr_after_norm = a[0]
        ms2, rs2, gsum = t3[:, 0, :], t3[:, 2, :], t3[:, 1, :]
        rs12 = gsum
        a, b = [r32_at], [scr_at]
        kds = [new("kds", [P, NG, S], at=a), new("kdf", [P, NG, S], at=a)]
        vts = [new("vts", [P, NG, TT, DH], at=a), new("vtf", [P, NG, TT, DH], at=a)]
        kcd = new("kcd", [P, NG, CP], at=a)
        vc = new("vc", [NC, NG, DH], at=a)
        gates = new("gates", [P, NG, 3, TT * GH], at=a)
        kc_hl = [new("kc_hi", [P, CP], F32R, at=a), new("kc_lo", [P, CP], F32R, at=a)]
        vcg = new("vcg", [NC, DH], at=a)
        gat = new("gat", [P, 3, TT * GH], at=a)
        vgs = [new("vgs", [P, TT, DH], at=a), new("vgf", [P, TT, DH], at=a)]
        tn = new("tn", [P, S], at=a)
        assert a[0] <= sig_at
        y2 = new("y2", [P, KT, S], at=[r32_at])
        bcmp = new("bcmp", [P, NG, GH * TT, CP], at=b)
        b_loop = list(b)
        vtmpn = new("vtmpn", [P, 2, S], at=b)
        x2 = [new("x2k", [P, 5, S], at=b), new("x2v", [P, 5, S], at=b)]
        w1 = [new("w1k", [P, 16, 256], at=b), new("w1v", [P, 16, 256], at=[sig_at])]
        b[0] = max(b[0], scr_after_norm)
        gwn_raw = new("gwn_raw", [P, KT * P], at=b)
        gwn = [new("gwn_hi", [P, KT * P], F32R, at=b), new("gwn_lo", [P, KT * P], F32R, at=b)]
        assert b[0] <= 229368, b[0]
        w2 = new("w2", [P, 2, 2, DH], at=[sig_at + 16384])
        hid = new("hid", [P, 4, P], at=[sig_at + 18432])
        ehid = new("ehid", [P, 4, P], at=[sig_at + 20480])
        rows_n = new("rows_n", [16, BN], at=[sig_at + 22528])
        grow2 = new("grow2", [48, 2, S], at=[sig_at + 26688])
        posb = new("posb", [P, 2, 16], at=[sig_at + 30784])
        b = b_loop
        qn = new("qn", [P, GH, S], F32R, at=b)
        kn_hl = [new("kn_hi", [P, S], F32R, at=b), new("kn_lo", [P, S], F32R, at=b)]
        biasn = new("biasn", [P, GH, S], at=b)
        Ln_ = new("Ln", [P, 2, S], at=b)
        Pn = new("Pn", [P, 3, S], at=b)
        PTn = new("PTn", [P, 3, S], at=b)
        aon = new("aon", [P, TT, GH * DH], at=b)
        sz = new("sz", [P, 6, S], at=b)
        y32 = new("y32", [P, 2, S], at=b)
        assert max(b[0], loop_end) <= 229368, (b[0], loop_end)
        a = [sig_at]
        oh_w, oh_n = new("oh_w", [33, BW], at=a), new("oh_n", [33, BN], at=a)
        tabw, tabn = new("tabw", [33, 16], at=a), new("tabn", [33, 16], at=a)
        bw_sb, bn_sb = new("bw_sb", [16, BW], at=a), new("bn_sb", [16, BN], at=a)

        ps = ctx.enter_context(nc.psum_tensor("ps", [P, 8, S], F32))

        raw_in = [sem("raw_in0"), sem("raw_in1")]
        hi_done, lo_done = sem("w_hi_done"), sem("w_lo_done")
        used = sem("w_used")
        g_free = [sem("g_free0"), sem("g_free1")]
        s_ready, s_free = [sem("s_ready0"), sem("s_ready1")], [sem("s_free0"), sem("s_free1")]
        t_ready, t_free = [sem("t_ready0"), sem("t_ready1")], [sem("t_free0"), sem("t_free1")]
        o_ready, o_free = [sem("o_ready0"), sem("o_ready1")], [sem("o_free0"), sem("o_free1")]
        e_done = [sem("e_done0"), sem("e_done1")]
        e_conv, e_z = sem("tanh_conv"), sem("tanh_z")
        cst_in, cst_done, tab_in = sem("consts_in"), sem("consts_made"), sem("tables_in")
        x_landed = [sem(f"x_tile_in{k}") for k in range(KT)]
        bw_out, bn_out = sem("bias_window_out"), sem("bias_full_out")
        bw_done, bn_done = sem("bias_window_made"), sem("bias_full_made")
        x_done, x_pool = sem("x_done"), sem("x_done_pool")
        sq_ready, sq_used, rs_ready = sem("sq_ready"), sem("sq_used"), sem("rs_ready")
        nt_ready, nhi_done = sem("nt_ready"), sem("norm_hi_done")
        h_ready = [sem("h_even_ready"), sem("h_odd_ready")]
        gw_in, gwhi_done, gwlo_done = sem("gate_w_in"), sem("gate_w_hi"), sem("gate_w_lo")
        gr_abs, gr_log, grows_done = sem("gate_rows_abs"), sem("gate_rows_log"), sem("gate_rows_done")
        half_a = sem("scalar_half_of_unit")
        staged_v, staged_a = sem("staged_vector"), sem("staged_scalar")
        bias_in = sem("bias_in")
        dg_done, d_done = sem("diag_done"), sem("decay_done")
        ss_done, hn_v, hn_a, hm_done = sem("sumsq_done"), sem("hnorm_vector"), sem("hnorm_scalar"), sem("hm_scaled")
        q_hi, k_hi, k_lo = sem("queries_hi"), sem("window_keys_hi"), sem("keys_lo")
        probs = sem("probs")
        t1_done, es_done = sem("sink_logit_done"), sem("sink_exp_done")
        mhi, mlo = sem("mix_in_hi"), sem("mix_in_lo")
        y_v, y_hi_done, y_done = sem("y_sum"), sem("y_hi_done"), sem("y_done")
        u_hi_done, u_done = sem("u_hi_done"), sem("u_done")
        late_in_s, x2_pos, pos_in_s, rows_in = sem("last_layer_in"), sem("x2_pos"), sem("pos_in"), sem("bias_rows_in")
        cmp_pre, cmp_exp, hid_done = sem("cmp_hidden_pre"), sem("cmp_hidden_exp"), sem("cmp_hidden_done")
        cs_sub, cs_exp = sem("cmp_logits_done"), sem("cmp_probs")
        ms2_done = sem("second_mean_square")
        out_s = sem("out_stored")
        chain_v, chain_a = sem("vector_chain"), sem("scalar_chain")

        block = ctx.enter_context(nc.Block())

        @block.sync
        def _(sp):
            for k in range(KT):
                nc.sync.dma_start(x[:, k, :], x_in[k * P:(k + 1) * P, :]).then_inc(x_landed[k], 16)
            for dst, src in ((vl[:, :, :], vec_l), (ident[:, :], ident_in), (tri[:, :], tri_in), (vit[:, :, :], vec_it),
                             (vn[:, :], vec_n), (late[:, :], late_in)):
                nc.sync.dma_start(dst, src).then_inc(cst_in, 16)
            with sp.Fori(0, UNITS // 2) as i:
                for p in range(2):
                    sp.wait_ge(lo_done, i * 4 + 2 * p + 2)
                    nc.sync.dma_start(raw[:, p, :], w_all[2 * i + p]).then_inc(raw_in[p], 16)
            for k in range(KT):
                if k % 2 == 0:
                    sp.wait_ge(x_done, KT + k // 2 + 1)
                else:
                    sp.wait_ge(x_pool, k // 2 + 1)
                nc.sync.dma_start(out[k * P:(k + 1) * P, :], x[:, k, :]).then_inc(out_s, 16)
            sp.wait_ge(out_s, 16 * KT)

        @block.gpsimd
        def _(pool):
            def split_pairs(count, before):
                with pool.Fori(0, count) as i:
                    for h in range(4):
                        pool.wait_ge(hi_done, (before + i) * 4 + h + 1)
                        nc.gpsimd.tensor_tensor(w_lo[:, h, :], raw[:, h // 2, (h % 2) * HALF:(h % 2 + 1) * HALF],
                                                w_hi[:, h, :].bitcast(F32), ALU.subtract).then_inc(lo_done, 1)

            def norm_lo(m):
                for k in range(1, KT, 2):
                    pool.wait_ge(nhi_done, m * KT + k + 1)
                    nc.gpsimd.tensor_tensor(hT[1][:, k, :], nt[:, k % 3, :], hT[0][:, k, :].bitcast(F32), ALU.subtract)\
                        .then_inc(h_ready[1], 1)

            pool.sem_inc(lo_done, 4)
            split_pairs(1, 0)
            with pool.Fori(0, DEPTH) as l:
                norm_lo(l * 2)
                split_pairs(MIXER_UNITS // 2, l * (LAYER_UNITS // 2) + 1)
                norm_lo(l * 2 + 1)
                split_pairs((LAYER_UNITS - MIXER_UNITS) // 2, l * (LAYER_UNITS // 2) + MIXER_UNITS // 2 + 1)
            norm_lo(DEPTH * 2)
            split_pairs(NSA_UNITS // 2 - 1, DEPTH * LAYER_UNITS // 2 + 1)
            for k in range(1, KT, 2):
                pool.wait_ge(nt_ready, (DEPTH * 2 + 1) * KT + k + 1)
                nc.gpsimd.tensor_tensor(x[:, k, :], x[:, k, :], nt[:, k % 3, :], ALU.add).then_inc(x_pool, 1)

        def squares(l):
            return KT + l * 5 * KT

        def step_uses(w, step):
            return [w.use(r) for r in takes(step)]

        @block.tensor
        def _(pe):
            w = Walk()
            cur = {}

            def quarter(s, u, hi, lo, waits=None):
                p, quarter_ = u.b, UNIT_STEPS.index(s[0])
                h = quarter_ // 2
                if quarter_ == 0:
                    pe.wait_ge(g_free[p], u.m + 1)
                if quarter_ % 2 == 0:
                    pe.wait_ge(lo_done, u.n * 2 + h + 5)
                for kk in range(2 * quarter_, 2 * quarter_ + 2):
                    k = kk - h * (KT // 2)
                    if waits is not None:
                        pe.wait_ge(*waits(kk))
                    wh, wl = w_hi[:, 2 * p + h, k * P:(k + 1) * P], w_lo[:, 2 * p + h, k * P:(k + 1) * P]
                    nc.tensor.matmul(ps[:, p, :], wh, hi[:, kk, :], start=(kk == 0), stop=False)
                    nc.tensor.matmul(ps[:, p, :], wh, lo[:, kk, :], start=False, stop=False)
                    last = nc.tensor.matmul(ps[:, p, :], wl, hi[:, kk, :], start=False, stop=(kk == KT - 1))
                if quarter_ % 2 == 1:
                    last.then_inc(used, 1)

            def norm_sum(count, total=None):
                use = step_uses(w, NORM[0])[0]
                pe.wait_ge(o_free[1], use.m + 1)
                pe.wait_ge(sq_used, count)
                total = ssq[:, :] if total is None else total
                nc.tensor.matmul(ps[:, 7, :], ones[:, :], total, start=True, stop=True).then_inc(o_ready[1], 1)

            def heads4(dst_bank, src, ready):
                for t in range(TT):
                    last = nc.tensor.transpose(ps[:, dst_bank, t * P:(t + 1) * P], src(t), ident[:, :])
                last.then_inc(ready, 1)

            def gate_gemm(I, use, gw):
                pe.wait_ge(gwlo_done, I + 1)
                pe.wait_ge(o_free[1], use.m + 1)
                for k in range(KT):
                    wh, wl = gw[0][:, k * P:(k + 1) * P], gw[1][:, k * P:(k + 1) * P]
                    nc.tensor.matmul(ps[:, 7, :], wh, hT[0][:, k, :], start=(k == 0), stop=False)
                    nc.tensor.matmul(ps[:, 7, :], wh, hT[1][:, k, :], start=False, stop=False)
                    last = nc.tensor.matmul(ps[:, 7, :], wl, hT[0][:, k, :], start=False, stop=(k == KT - 1))
                last.then_inc(o_ready[1], 1)

            def attend(step, us, q, kk, vv, I, wide, nI):
                kind, name, j = step
                qt, hd = j // GH, j % GH
                k0 = 0 if wide else max(qt - 1, 0)
                nk = qt + 1 - k0
                if kind == "S":
                    pe.wait_ge(s_free[us[0].b], us[0].m + 1)
                    for i in range(2):
                        last = nc.tensor.matmul(ps[:, 2 + us[0].b, 0:nk * P], q[:, hd, qt * P:(qt + 1) * P],
                                                kk[i][:, k0 * P:(qt + 1) * P], start=(i == 0), stop=(i == 1))
                    last.then_inc(s_ready[us[0].b], 1)
                elif kind == "T":
                    pe.wait_ge(t_free[us[0].b], us[0].m + 1)
                    pe.wait_ge(probs, nI + j + 1)
                    pb = cur["P"]
                    for c in range(nk):
                        last = nc.tensor.transpose(ps[:, 4 + us[0].b, c * P:(c + 1) * P],
                                                   pb[:, j % 3, c * P:(c + 1) * P], ident[:, :])
                    last.then_inc(t_ready[us[0].b], 1)
                    cur["Tuse", j] = us[0]
                else:
                    t = cur["Tuse", j]
                    pe.wait_ge(t_free[t.b], t.m + 2)
                    ob = qt // 2
                    if j % (2 * GH) == 0:
                        pe.wait_ge(o_free[ob], cur["Om"][ob] + 1)
                    pt = cur["PT"]
                    for c in range(nk):
                        last = nc.tensor.matmul(ps[:, 6 + ob, (qt % 2) * 256 + hd * DH:(qt % 2) * 256 + (hd + 1) * DH],
                                                pt[:, j % 3, c * P:(c + 1) * P], vv[:, k0 + c, :],
                                                start=(c == 0), stop=(c == nk - 1))
                    if j % (2 * GH) == 2 * GH - 1:
                        last.then_inc(o_ready[ob], 1)

            pe.wait_ge(tab_in, 16 * 4)
            pe.wait_ge(cst_done, 1)
            nc.tensor.matmul(ps[0:16, 2, 0:BW], tabw[:, :], oh_w[:, :], start=True, stop=True).then_inc(s_ready[0], 1)
            nc.tensor.matmul(ps[0:16, 3, 0:S], tabn[:, :], oh_n[:, 0:S], start=True, stop=True).then_inc(s_ready[1], 1)
            for b_ in range(2):
                nc.tensor.matmul(ps[0:16, 4 + b_, 0:64], tabn[:, :], oh_n[:, S + 64 * b_:S + 64 * (b_ + 1)],
                                 start=True, stop=True).then_inc(t_ready[b_], 1)
            for r in ("S", "S", "T", "T"):
                w.use(r)
            pe.wait_ge(cst_in, 16 * 6)

            with w.loop(pe, DEPTH, C_LAYER) as l:
                norm_sum(squares(l))
                for s in PRE:
                    us = step_uses(w, s)
                    if s[0] == "u0":
                        cur["u"] = cur[s[1:]] = us[0]
                    if s[0] in UNIT_STEPS:
                        first = s[1:] == ("k", 0)
                        quarter(s, cur["u"], *hT,
                                  waits=(lambda k: (h_ready[k % 2], l * KT + k // 2 + 1)) if first else None)
                    elif s[0] == "TK":
                        pe.wait_ge(t_free[us[0].b], us[0].m + 1)
                        vu = cur["v", s[1]]
                        pe.wait_ge(g_free[vu.b], vu.m + 2)
                        heads4(4 + us[0].b, lambda t: vtmp[:, s[1], t * P:(t + 1) * P], t_ready[us[0].b])
                    elif s[0] == "gates":
                        gate_gemm(l, us[0], gw)
                    elif s[0] == "gatesT":
                        pe.wait_ge(grows_done, l + 1)
                        for which in range(2):
                            t_ = us[which]
                            pe.wait_ge(t_free[t_.b], t_.m + 1)
                            for t in range(TT):
                                last = nc.tensor.matmul(ps[:, 4 + t_.b, t * MH:(t + 1) * MH],
                                                        grow[:, 8 + which, t * P:(t + 1) * P], ident[0:MH, 0:MH],
                                                        start=True, stop=True)
                            last.then_inc(t_ready[t_.b], 1)
                w.flush()
                with w.loop(pe, NG, per(LOOP)) as it:
                    I = l * NG + it
                    cur["P"], cur["PT"] = Pb, PT
                    stu, nu = {}, {}
                    for s in LOOP:
                        us = step_uses(w, s)
                        if s[0] == "u0":
                            cur["u"] = cur[s[1:]] = us[0]
                        if s[0] in UNIT_STEPS:
                            quarter(s, cur["u"], *hT)
                            if s[0:2] == ("u1", "conv"):
                                cur["conv", s[2], "e"] = us[0]
                        elif s[0] == "TV":
                            pe.wait_ge(t_free[us[0].b], us[0].m + 1)
                            vu = cur["mv", s[1]]
                            pe.wait_ge(g_free[vu.b], vu.m + 2)
                            heads4(4 + us[0].b, lambda t: vtmp[:, s[1], t * P:(t + 1) * P], t_ready[us[0].b])
                            cur["TV", s[1]] = us[0]
                        elif s[0] == "bc":
                            pe.wait_ge(o_free[0], us[0].m + 1)
                            pe.wait_ge(staged_v, I + 1)
                            nc.tensor.matmul(ps[:, 6, :], selh[:, :], negM[:, :], start=True, stop=True)\
                                .then_inc(o_ready[0], 1)
                        elif s[0] == "ST":
                            tt = s[1]
                            stu[tt] = us[0]
                            pe.wait_ge(s_free[us[0].b], us[0].m + 1)
                            if tt == 0:
                                for n in range(2):
                                    pe.wait_ge(e_done[cur["conv", n, "e"].b], cur["conv", n, "e"].m + 2)
                            for c in range(tt + 1):
                                last = nc.tensor.matmul(ps[:, 2 + us[0].b, c * P:(c + 1) * P],
                                                        mqk[:, 1, c * P:(c + 1) * P], mqk[:, 0, tt * P:(tt + 1) * P],
                                                        start=True, stop=True)
                            last.then_inc(s_ready[us[0].b], 1)
                        elif s[0] == "NUM":
                            tt = s[1]
                            pe.wait_ge(t_free[us[0].b], us[0].m + 1)
                            if tt == 0:
                                for v_ in range(2):
                                    pe.wait_ge(t_free[cur["TV", v_].b], cur["TV", v_].m + 2)
                            pe.wait_ge(s_free[stu[tt].b], stu[tt].m + 2)
                            for c in range(tt + 1):
                                last = nc.tensor.matmul(ps[:, 4 + us[0].b, 0:MDV + 1], PTm[:, tt % 2, c * P:(c + 1) * P],
                                                        vbuf[:, c, 0:MDV + 1], start=(c == 0), stop=(c == tt))
                            last.then_inc(t_ready[us[0].b], 1)
                        elif s[0] in ("S", "T", "V"):
                            if s == ("S", "w", 0):
                                for n in range(2):
                                    pe.wait_ge(g_free[cur["q", n].b], cur["q", n].m + 2)
                                pe.wait_ge(staged_a, I + 1)
                                pe.wait_ge(k_lo, I + 1)
                                cur["Om"] = [w.next("O0"), w.next("O1")]
                            attend(s, us, aq, (kg_hi, kg_lo), vg, I, False, I * 16)
                        elif s[0] == "TH":
                            pe.wait_ge(t_free[us[0].b], us[0].m + 1)
                            pe.wait_ge(hm_done, I + 1)
                            heads4(4 + us[0].b, lambda t: numsb[:, t, s[1] * P:(s[1] + 1) * P], t_ready[us[0].b])
                        elif s[0] == "otail":
                            cur["tail"] = us
                        elif s[0] == "TA":
                            pe.wait_ge(t_free[us[0].b], us[0].m + 1)
                            if s[1] == 0:
                                for o_ in range(2):
                                    pe.wait_ge(o_free[o_], cur["tail"][o_].m + 2)
                            heads4(4 + us[0].b, lambda t: ao[:, t, s[1] * P:(s[1] + 1) * P], t_ready[us[0].b])
                with w.loop(pe, 4, per(MIX)) as i:
                    for s in MIX:
                        us = step_uses(w, s)
                        if s[0] == "u0":
                            cur["u"] = us[0]
                        second = s[1] == "pa"
                        quarter(s, cur["u"], *(ha_hl if second else hm_hl),
                                  waits=(lambda k: (mlo, l * 2 * KT + second * KT + k + 1)) if s[2] == 0 else None)
                with w.loop(pe, 4, per(WOUT)) as i:
                    for s in WOUT:
                        us = step_uses(w, s)
                        if s[0] == "u0":
                            cur["u"] = us[0]
                        quarter(s, cur["u"], *y_hl,
                                  waits=(lambda k: (y_done, l * KT + k + 1)) if s[2] == 0 else None)
                norm_sum(squares(l) + KT)
                with w.loop(pe, 4, per(MLP)) as c:
                    for s in MLP:
                        us = step_uses(w, s)
                        if s[0] == "u0":
                            cur["u"] = us[0]
                        if s[1] == "up":
                            quarter(s, cur["u"], *hT,
                                      waits=(lambda k: (h_ready[k % 2], l * KT + KT // 2 + k // 2 + 1)) if s[2] == 0 else None)
                        else:
                            quarter(s, cur["u"], *u_hl,
                                      waits=(lambda k: (u_done, l * 4 * KT + c * KT + k + 1)) if s[2] == 0 else None)

            norm_sum(squares(DEPTH))
            norm_sum(squares(DEPTH) + KT, gsum)
            for s in NPRE:
                us = step_uses(w, s)
                if s[0] == "u0":
                    cur["u"] = cur[s[1:]] = us[0]
                if s[0] in UNIT_STEPS:
                    first = s[1:] == ("x2", 0)
                    quarter(s, cur["u"], *hT,
                              waits=(lambda k: (h_ready[k % 2], DEPTH * KT + k // 2 + 1)) if first else None)
                elif s[0] == "TK":
                    pe.wait_ge(t_free[us[0].b], us[0].m + 1)
                    vu = cur["v", s[1]]
                    pe.wait_ge(g_free[vu.b], vu.m + 2)
                    heads4(4 + us[0].b, lambda t: vtmpn[:, s[1] % 2, t * P:(t + 1) * P], t_ready[us[0].b])
                elif s[0] == "ngates":
                    gate_gemm(DEPTH, us[0], gwn)
                elif s[0] == "ngatesT":
                    pe.wait_ge(grows_done, DEPTH + 1)
                    for which in range(2):
                        t_ = us[which]
                        pe.wait_ge(t_free[t_.b], t_.m + 1)
                        for t in range(2):
                            tk = 2 * which + t
                            last = nc.tensor.transpose(ps[:, 4 + t_.b, t * 48:(t + 1) * 48],
                                                       grow2[:, 1, tk * P:(tk + 1) * P], ident[0:48, 0:48])
                        last.then_inc(t_ready[t_.b], 1)
                elif s[0] == "cmpbias":
                    pe.wait_ge(rows_in, 16)
                    pe.wait_ge(o_free[0], us[0].m + 1)
                    for m in range(NC):
                        last = nc.tensor.transpose(ps[:, 6, m * 16:(m + 1) * 16],
                                                   rows_n[:, STRIDE_CMP * m:STRIDE_CMP * m + P], ident[0:16, 0:16])
                    last.then_inc(o_ready[0], 1)
                elif s[0] == "hidden":
                    pe.wait_ge(late_in_s, 16 * 4)
                    pe.wait_ge(x2_pos, 2)
                    for kv in range(2):
                        pe.wait_ge(o_free[kv], us[kv].m + 1)
                        for m in range(2):
                            for pr in range(16):
                                rhs = x2[kv][:, :, 2 * pr:2 * pr + STRIDE_CMP * (NC - 1) + 1:STRIDE_CMP]
                                last = nc.tensor.matmul(ps[:, 6 + kv, m * 256:m * 256 + 5 * NC],
                                                        w1[kv][:, pr, m * P:(m + 1) * P], rhs,
                                                        start=(pr == 0), stop=(pr == 15))
                        last.then_inc(o_ready[kv], 1)
                elif s[0] == "compress":
                    pe.wait_ge(hid_done, 1)
                    pe.wait_ge(t_free[0], us[0].m + 1)
                    for m in range(2):
                        last = nc.tensor.matmul(ps[0:DH, 4, 0:NG * NC], w2[:, 0, m, :], hid[:, m, 0:NG * NC],
                                                start=(m == 0), stop=(m == 1))
                    last.then_inc(t_ready[0], 1)
                    pe.wait_ge(t_free[1], us[1].m + 1)
                    for g in range(NG):
                        for m in range(2):
                            last = nc.tensor.matmul(ps[0:NC, 5, g * DH:(g + 1) * DH], hid[:, 2 + m, g * NC:(g + 1) * NC],
                                                    w2[:, 1, m, :], start=(m == 0), stop=(m == 1))
                    last.then_inc(t_ready[1], 1)
            w.flush()
            with w.loop(pe, NG, per(NLOOP)) as it:
                cur["P"], cur["PT"] = Pn, PTn
                ctu = {}
                for s in NLOOP:
                    us = step_uses(w, s)
                    if s[0] == "u0":
                        cur["u"] = cur[s[1:]] = us[0]
                    if s[0] in UNIT_STEPS:
                        quarter(s, cur["u"], *hT)
                    elif s[0] == "CS":
                        for n in range(2):
                            pe.wait_ge(g_free[cur["q", n].b], cur["q", n].m + 2)
                        pe.wait_ge(staged_a, DEPTH * NG + it + 1)
                        pe.wait_ge(k_lo, DEPTH * NG + it * 2 + 1)
                        pe.wait_ge(s_free[0], us[0].m + 1)
                        pe.wait_ge(s_free[1], us[1].m + 1)
                        for j in range(GH * TT):
                            qt, hd = j // GH, j % GH
                            for i in range(2):
                                last = nc.tensor.matmul(ps[:, 2 + j % 2, (j // 2) * CP:(j // 2 + 1) * CP],
                                                        qn[:, hd, qt * P:(qt + 1) * P], kc_hl[i][:, :],
                                                        start=(i == 0), stop=(i == 1))
                            if j >= GH * TT - 2:
                                last.then_inc(s_ready[j % 2], 1)
                        cur["Om"] = [w.next("O0"), w.next("O1")]
                    elif s[0] == "CT":
                        qt = s[1]
                        b_ = us[0].b
                        pe.wait_ge(cs_exp, it + 1)
                        pe.wait_ge(t_free[b_], us[0].m + 1)
                        for hd in range(GH):
                            j = qt * GH + hd
                            last = nc.tensor.transpose(ps[0:NC, 4 + b_, hd * P:(hd + 1) * P], Pn[:, 0, j * CP:j * CP + NC],
                                                       ident[:, :])
                        last.then_inc(t_ready[b_], 1)
                        cur["CT", qt] = us[0]
                    elif s[0] == "CV":
                        qt = s[1]
                        pe.wait_ge(t_free[cur["CT", qt].b], cur["CT", qt].m + 2)
                        ob = qt // 2
                        if qt % 2 == 0:
                            pe.wait_ge(o_free[ob], cur["Om"][ob] + 1)
                        for hd in range(GH):
                            last = nc.tensor.matmul(ps[:, 6 + ob, (qt % 2) * 256 + hd * DH:(qt % 2) * 256 + (hd + 1) * DH],
                                                    PTn[0:NC, qt % 2, hd * P:(hd + 1) * P], vcg[:, :], start=True, stop=True)
                        if qt % 2 == 1:
                            last.then_inc(o_ready[ob], 1)
                    elif s[0] in ("S", "T", "V"):
                        br = 0 if s[1] == "s" else 1
                        if s[0] == "S" and s[2] == 0:
                            cur["Om"] = [w.next("O0"), w.next("O1")]
                            pe.wait_ge(k_lo, DEPTH * NG + it * 2 + br + 1)
                        attend(s, us, qn, kn_hl, vgs[br], it, True, DEPTH * NG * 16 + it * 32 + br * 16)
                    elif s[0] == "otail":
                        cur["tail"] = us
                    elif s[0] == "TO":
                        pe.wait_ge(t_free[us[0].b], us[0].m + 1)
                        for o_ in range(2):
                            pe.wait_ge(o_free[o_], cur["tail"][o_].m + 2)
                        heads4(4 + us[0].b, lambda t: aon[:, t, s[2] * P:(s[2] + 1) * P], t_ready[us[0].b])
            for i in range(4):
                for s in NOUT:
                    us = step_uses(w, s)
                    if s[0] == "u0":
                        cur["u"] = us[0]
                    first = i == 0 and s[2] == 0
                    quarter(s, cur["u"], *y_hl,
                              waits=(lambda k: (y_done, DEPTH * KT + k + 1)) if first else None)
            norm_sum(squares(DEPTH) + 2 * KT)

        @block.scalar
        def _(act):
            w = Walk()
            cur = {}
            chain = [0]

            def restart():
                act.sem_clear(chain_a)
                chain[0] = 0

            def link(ins):
                chain[0] += 1
                ins.then_inc(chain_a, 1)
                act.wait_ge(chain_a, chain[0])

            def split(n, half_n, p, h):
                if h == 0:
                    act.wait_ge(raw_in[p], half_n * 16 + 16)
                act.wait_ge(used, n * 2 + h + 1)
                nc.scalar.activation(w_hi[:, 2 * p + h, :], raw[:, p, h * HALF:(h + 1) * HALF], ACT.Copy)\
                    .then_inc(hi_done, 1)

            def product(u):
                act.wait_ge(used, u.n * 2 + 6)

            def gemm_step(s, u):
                if s[0] == "u1":
                    store(s, u)
                if s[0] in ("h0", "u1") and not cur.get("last"):
                    split(u.n + 2, u.m + 1, u.b, int(s[0][1]))

            def store(s, u):
                kind, n = s[1], s[2]
                g = ps[:, u.b, :]
                if kind == "k":
                    dst = kdup if cur["layer"] else kds[n // 2]
                    product(u)
                    for i in range(2):
                        nc.scalar.activation(dst[DH * i:DH * (i + 1), 2 * (n % 2), :], ps[0:DH, u.b, :], ACT.Copy)\
                            .then_inc(half_a, 1)
                elif kind == "x2":
                    product(u)
                    for i in range(2):
                        nc.scalar.activation(x2[n // 2][DH:P, 2 * (n % 2) + i, 0:S - 1],
                                             ps[DH * i:DH * (i + 1), u.b, 1:S], ACT.Copy).then_inc(half_a, 1)
                elif kind == "q":
                    product(u)
                    for i in range(2):
                        half = slice(DH * i, DH * (i + 1))
                        nc.scalar.activation((aq if cur["layer"] else qn)[half, 2 * n + i, :], ps[half, u.b, :], ACT.Copy,
                                             scale=-DH ** -0.5).then_inc(q_hi, 1)
                elif kind in ("v", "mv"):
                    product(u)
                    nc.scalar.activation((vtmp if cur["layer"] else vtmpn)[:, n % 2, :], g, ACT.Copy)\
                        .then_inc(g_free[u.b], 1)
                elif kind == "conv":
                    e = cur["e"]
                    act.wait_ge(g_free[u.b], u.m + 2)
                    act.wait_ge(e_done[e.b], e.m + 1)
                    nc.scalar.activation(e_buf[:, e.b, :], cv[:, :], ACT.Tanh, scale=0.5).then_inc(e_conv, 1)
                elif kind in ("mo", "ga", "gb"):
                    e = cur["e"]
                    product(u)
                    act.wait_ge(e_done[e.b], e.m + 1)
                    nc.scalar.activation(e_buf[:, e.b, :], g, ACT.Tanh, scale=0.5).then_inc(g_free[u.b], 1)
                elif kind == "z":
                    e = cur["e"]
                    product(u)
                    act.wait_ge(e_done[e.b], e.m + 1)
                    nc.scalar.activation(e_buf[:, e.b, :], g, ACT.Tanh, scale=0.5).then_inc(e_z, 1)
                elif kind == "up":
                    e = cur["e"]
                    product(u)
                    act.wait_ge(e_done[e.b], e.m + 1)
                    nc.scalar.activation(e_buf[:, e.b, :], g, ACT.Relu).then_inc(g_free[u.b], 1)
                    act.wait_ge(g_free[u.b], u.m + 2)
                    nc.scalar.activation(u_hl[0][:, n, :], e_buf[:, e.b, :], ACT.Square).then_inc(u_hi_done, 1)
                elif kind == "pa":
                    act.wait_ge(y_v, cur["ny"] + n + 1)
                    nc.scalar.activation(y_hl[0][:, cur["i2"] + n, :], t3[:, n, :], ACT.Copy).then_inc(y_hi_done, 1)
                elif kind in ("res", "down"):
                    act.wait_ge(g_free[u.b], u.m + 2)
                    square(x[:, (cur["i2"] if kind == "res" else 0) + n, :], cur["nsq"] + n, n % 2)
                elif kind == "y2":
                    product(u)
                    square(g, cur["nsq"] + n, n % 2)
                    nc.scalar.activation(y2[:, cur["i2"] + n, :], g, ACT.Copy).then_inc(g_free[u.b], 1)

            def take(s):
                us = [w.use(r) for r in takes(s)]
                if s[0] == "u0":
                    cur["u"] = cur[s[1:]] = us[0]
                if s[0] == "u1" and us:
                    cur["e"] = us[0]
                return us

            def ln_exp():
                nc.scalar.preload_act_table_set("natural_log_exp_and_others")

            def square(tile, n, b_, first=False, scale=D ** -0.5):
                if not first:
                    act.wait_ge(sq_used, n - 1)
                nc.scalar.activation(sq[:, b_, :], tile, ACT.Square, scale=scale).then_inc(sq_ready, 1)

            def norm(split_to):
                use = w.use("O1")
                act.wait_ge(o_ready[1], use.m + 1)
                nc.scalar.activation(rs[:, :], ps[:, 7, :], ACT.Ln, bias=EPS).then_inc(o_free[1], 1)
                act.wait_ge(o_free[1], use.m + 2)
                nc.scalar.activation(rs[:, :], rs[:, :], ACT.Exp, scale=-0.5).then_inc(rs_ready, 1)
                if split_to is not None:
                    hi_parts(split_to)

            def hi_parts(split_to):
                for k in range(KT):
                    act.wait_ge(nt_ready, split_to * KT + k + 1)
                    nc.scalar.activation(hT[0][:, k, :], nt[:, k % 3, :], ACT.Copy).then_inc(nhi_done, 1)

            def stored():
                for b_ in range(2):
                    act.wait_ge(g_free[b_], w.next("u", b_) + 1)

            def gate_weights(I, gw_raw):
                nc.scalar.dma_start(gw_raw[:, :], wg_all[I]).then_inc(gw_in, 16)

            def gate_weights_hi(I, gw_raw, gw):
                act.wait_ge(gw_in, I * 16 + 16)
                nc.scalar.activation(gw[0][:, :], gw_raw[:, :], ACT.Copy).then_inc(gwhi_done, 1)

            def attend_act(s, us, Pbuf, Lbuf, PTbuf, nk, nI, j):
                n = nk * P
                if s[0] == "S":
                    act.wait_ge(s_free[us[0].b], us[0].m + 2)
                    if j >= 3:
                        t = cur["Tuse", j - 3]
                        act.wait_ge(t_ready[t.b], t.m + 1)
                    nc.scalar.activation(Pbuf[:, j % 3, 0:n], Lbuf[:, j % 2, 0:n], ACT.Exp, scale=-1.0,
                                         bias=st[:, 0, j:j + 1], accum_out=st[:, 1, j:j + 1]).then_inc(probs, 1)
                elif s[0] == "T":
                    cur["Tuse", j] = us[0]
                    if j % 2 == 0:
                        act.wait_ge(t_ready[us[0].b], us[0].m + 1)
                        nc.scalar.activation(PTbuf[:, j % 3, 0:n], ps[:, 4 + us[0].b, 0:n], ACT.Copy)\
                            .then_inc(t_free[us[0].b], 1)

            act.sem_inc(used, 4)
            for f in (*g_free, *s_free, *t_free, *o_free, *e_done):
                act.sem_inc(f, 1)
            for dst, src in ((oh_w[:, :], onehot_w), (tabw[:, :], tab_w), (oh_n[:, :], onehot_n), (tabn[:, :], tab_n)):
                nc.scalar.dma_start(dst, src).then_inc(tab_in, 16)
            nc.scalar.preload_act_table(ACT.Exp)
            for r in ("S", "S", "T", "T"):
                w.use(r)
            for k in range(KT):
                act.wait_ge(x_landed[k], 16)
                square(x[:, k, :], k, k % 2, first=k < 2)
            act.wait_ge(bw_done, 1)
            nc.scalar.dma_start(scr_w, bw_sb[:, :]).then_inc(bw_out, 16)
            act.wait_ge(bn_done, 3)
            nc.scalar.dma_start(scr_n, bn_sb[:, :]).then_inc(bn_out, 16)
            for p in range(2):
                for h in range(2):
                    split(p, 0, p, h)
            act.wait_ge(cst_in, 16 * 6)

            with w.loop(act, DEPTH, C_LAYER) as l:
                cur["layer"] = True
                restart()
                ln_exp()
                stored()
                gate_weights(l, gw_raw)
                norm(l * 2)
                gate_weights_hi(l, gw_raw, gw)
                for s in PRE:
                    us = take(s)
                    if s[0] in UNIT_STEPS:
                        gemm_step(s, cur["u"])
                    elif s[0] == "TK":
                        act.wait_ge(t_ready[us[0].b], us[0].m + 1)
                        tk = ps[:, 4 + us[0].b, :].rearrange("p (t d) -> p t d", t=TT)
                        link(nc.scalar.activation(vtok[:, 2 * s[1], :, :], tk[:, :, 0:DH], ACT.Copy))
                        nc.scalar.activation(vtok[:, 2 * s[1] + 1, :, :], tk[:, :, DH:P], ACT.Copy)\
                            .then_inc(t_free[us[0].b], 1)
                    elif s[0] == "gates":
                        act.wait_ge(gr_abs, l + 1)
                        link(nc.scalar.activation(grow[:, 4, :], grow[:, 3, :], ACT.Exp))
                        nc.scalar.activation(grow[:, 5, :], grow[:, 4, :], ACT.Ln, bias=1.0).then_inc(gr_log, 1)
                    elif s[0] == "gatesT":
                        t_ = us[1]
                        act.wait_ge(t_ready[t_.b], t_.m + 1)
                        nc.scalar.activation(gtok[:, :, TT:2 * TT],
                                             ps[:, 4 + t_.b, 0:TT * MH].rearrange("p (t h) -> p h t", h=MH),
                                             ACT.Exp, scale=-1.0).then_inc(t_free[t_.b], 1)
                for n in range(2):
                    act.wait_ge(g_free[cur["k", n].b], cur["k", n].m + 2)
                with w.loop(act, NG, per(LOOP)) as it:
                    I = l * NG + it
                    cur["I"] = I
                    restart()
                    act.wait_ge(bw_out, 16)
                    nc.scalar.dma_start(bias[:, :, :], bass.AP(scr_w.tensor, scr_w.offset + it * (GH * BW),
                                                               [[1, P], [BW, GH], [1, 2 * P]])).then_inc(bias_in, 16)
                    nc.scalar.activation(kg_hi[:, :], kdup[:, it, :], ACT.Copy)
                    nc.scalar.activation(vg[:, :, :], vtok[:, it, :, :], ACT.Copy).then_inc(staged_a, 1)
                    stu = {}
                    for s in LOOP:
                        us = take(s)
                        if s[0] in UNIT_STEPS:
                            gemm_step(s, cur["u"])
                        elif s[0] == "TV":
                            act.wait_ge(t_ready[us[0].b], us[0].m + 1)
                            nc.scalar.activation(vbuf[:, :, s[1] * P:(s[1] + 1) * P],
                                                 ps[:, 4 + us[0].b, :].rearrange("p (t d) -> p t d", t=TT), ACT.Copy)\
                                .then_inc(t_free[us[0].b], 1)
                        elif s[0] == "bc":
                            cur["bc"] = us[0]
                        elif s[0] == "ST":
                            tt = s[1]
                            stu[tt] = us[0]
                            if tt == 0:
                                act.wait_ge(o_ready[0], cur["bc"].m + 1)
                                act.wait_ge(staged_v, I + 1)
                            else:
                                act.wait_ge(s_free[stu[tt - 1].b], stu[tt - 1].m + 2)
                            act.wait_ge(dg_done, I * 4 + tt + 1)
                            last = nc.scalar.activation(Dm[:, tt * P:(tt + 1) * P], dg[:, :], ACT.Exp)
                            for c in range(tt):
                                last = nc.scalar.activation(Dm[:, c * P:(c + 1) * P], ps[:, 6, tt * P:(tt + 1) * P],
                                                            ACT.Exp, bias=gcur[:, c:c + 1])
                            last.then_inc(d_done if tt < TT - 1 else o_free[0], 1)
                        elif s[0] == "NUM":
                            tt = s[1]
                            act.wait_ge(t_free[us[0].b], us[0].m + 2)
                            nc.scalar.activation(junk, numsb[:, tt, 0:MDV], ACT.Square, scale=MDV ** -0.5,
                                                 accum_out=st[:, 6, tt:tt + 1]).then_inc(ss_done, 1)
                        elif s == ("hnorm", 1):
                            ln_exp()
                            act.wait_ge(hn_v, I + 1)
                            link(nc.scalar.activation(st[:, 9, 0:TT], st[:, 8, 0:TT], ACT.Ln, bias=EPS))
                            nc.scalar.activation(st[:, 10, 0:TT], st[:, 9, 0:TT], ACT.Exp, scale=-0.5).then_inc(hn_a, 1)
                        elif s[0] in ("S", "T"):
                            qt = s[2] // GH
                            attend_act(s, us, Pb, L, PT, min(qt + 1, 2), I * 16, s[2])
                        elif s[0] == "ostat":
                            act.wait_ge(t1_done, I + 1)
                            nc.scalar.activation(st[:, 3, :], st[:, 2, :], ACT.Exp).then_inc(es_done, 1)
                        elif s[0] == "TA":
                            act.wait_ge(t_ready[us[0].b], us[0].m + 1)
                            nc.scalar.activation(ha32[:, 2 * it + s[1], :], ps[:, 4 + us[0].b, :], ACT.Copy)\
                                .then_inc(t_free[us[0].b], 1)
                stored()
                for b_ in range(2):
                    act.wait_ge(t_free[b_], w.next("T", b_) + 1)
                for src, dst in ((hm32, hm_hl[0]), (ha32, ha_hl[0])):
                    for k in range(KT):
                        nc.scalar.activation(dst[:, k, :], src[:, k, :], ACT.Copy).then_inc(mhi, 1)
                with w.loop(act, 4, per(MIX)) as i:
                    cur["ny"], cur["i2"] = l * KT + i * 2, i * 2
                    for s in MIX:
                        take(s)
                        gemm_step(s, cur["u"])
                with w.loop(act, 4, per(WOUT)) as i:
                    cur["nsq"], cur["i2"] = squares(l) + i * 2, i * 2
                    for s in WOUT:
                        take(s)
                        gemm_step(s, cur["u"])
                ln_exp()
                stored()
                norm(l * 2 + 1)
                with w.loop(act, 4, per(MLP)) as c:
                    cur["nsq"] = squares(l) + KT + c * KT
                    for s in MLP:
                        take(s)
                        gemm_step(s, cur["u"])

            ln_exp()
            stored()
            gate_weights(DEPTH, gwn_raw)
            cur["layer"] = False
            for k in range(KT):
                square(x[:, k, :], squares(DEPTH) + k, k % 2, scale=vn[:, k:k + 1])
                if k == 3:
                    norm(None)
            w.use("O1")
            act.wait_ge(ms2_done, 1)
            link(nc.scalar.activation(rs2, ms2, ACT.Ln, bias=EPS))
            nc.scalar.activation(rs2, rs2, ACT.Exp, scale=-0.5).then_inc(rs_ready, 1)
            hi_parts(DEPTH * 2)
            restart()
            gate_weights_hi(DEPTH, gwn_raw, gwn)
            for h in h_ready:
                act.wait_ge(h, (DEPTH * 2 + 1) * KT // 2)
            act.wait_ge(bn_out, 16)
            for dst, src, landed in ((posb[:, :, :], pos_in, pos_in_s), (rows_n[:, :], scr_n, rows_in),
                                     (w2[:, :, :, :], w2_in, late_in_s), (w1[0][:, 0:8, :], w1_in[0, :, 0:8], late_in_s),
                                     (w1[0][:, 8:16, :], w1_in[0, :, 8:16], late_in_s), (w1[1][:, :, :], w1_in[1], late_in_s)):
                nc.scalar.dma_start(dst, src).then_inc(landed, 16)
            for s in NPRE:
                us = take(s)
                if s[0] in UNIT_STEPS:
                    gemm_step(s, cur["u"])
                elif s[0] == "TK":
                    act.wait_ge(t_ready[us[0].b], us[0].m + 1)
                    tk = ps[:, 4 + us[0].b, :].rearrange("p (t d) -> p t d", t=TT)
                    dst, g0 = vts[s[1] // 2], 2 * (s[1] % 2)
                    link(nc.scalar.activation(dst[:, g0, :, :], tk[:, :, 0:DH], ACT.Copy))
                    nc.scalar.activation(dst[:, g0 + 1, :, :], tk[:, :, DH:P], ACT.Copy).then_inc(t_free[us[0].b], 1)
                elif s[0] == "ngates":
                    act.wait_ge(o_ready[1], us[0].m + 1)
                    nc.scalar.activation(grow2[:, 0, :], ps[0:48, 7, :], ACT.Tanh, scale=0.5).then_inc(o_free[1], 1)
                elif s[0] == "hidden":
                    act.wait_ge(cmp_pre, 4)
                    nc.scalar.activation(ehid[:, :, 0:NG * NC], hid[:, :, 0:NG * NC], ACT.Tanh, scale=0.5)\
                        .then_inc(cmp_exp, 1)
                elif s[0] == "compress":
                    act.wait_ge(t_ready[0], us[0].m + 1)
                    kc = ps[0:DH, 4, 0:NG * NC].rearrange("p (g c) -> p g c", g=NG)
                    link(nc.scalar.activation(kcd[0:DH, :, 0:NC], kc, ACT.Copy))
                    nc.scalar.activation(kcd[DH:P, :, 0:NC], kc, ACT.Copy).then_inc(t_free[0], 1)
            for n in range(4):
                act.wait_ge(g_free[cur["k", n].b], cur["k", n].m + 2)
            for b_ in range(2):
                act.wait_ge(t_free[b_], w.next("T", b_) + 1)
            w.flush()
            with w.loop(act, NG, per(NLOOP)) as it:
                restart()
                act.wait_ge(bn_out, 16)
                nc.scalar.dma_start(biasn[:, :, :], bass.AP(scr_n.tensor, scr_n.offset + it * (GH * BN),
                                                            [[1, P], [BN, GH], [1, S]])).then_inc(bias_in, 16)
                for dst, src in ((kc_hl[0][:, :], kcd[:, it, :]), (vcg[:, :], vc[:, it, :]), (kn_hl[0][:, :], kds[0][:, it, :]),
                                 (vgs[0][:, :, :], vts[0][:, it, :, :])):
                    nc.scalar.activation(dst, src, ACT.Copy)
                nc.scalar.activation(vgs[1][:, :, :], vts[1][:, it, :, :], ACT.Copy).then_inc(staged_a, 1)
                for s in NLOOP:
                    us = take(s)
                    if s[0] in UNIT_STEPS:
                        gemm_step(s, cur["u"])
                    elif s[0] == "kf":
                        nc.scalar.activation(kn_hl[0][:, :], kds[1][:, it, :], ACT.Copy).then_inc(k_hi, 1)
                    elif s[0] == "CS":
                        act.wait_ge(cs_sub, it + 1)
                        nc.scalar.activation(Pn[:, 0, :].rearrange("p (j c) -> p j c", c=CP)[:, :, 0:NC],
                                             Ln_[:, 0, :].rearrange("p (j c) -> p j c", c=CP)[:, :, 0:NC],
                                             ACT.Exp, scale=-1.0).then_inc(cs_exp, 1)
                    elif s[0] == "CT":
                        act.wait_ge(t_ready[us[0].b], us[0].m + 1)
                        nc.scalar.activation(PTn[0:NC, s[1] % 2, :], ps[0:NC, 4 + us[0].b, :], ACT.Copy)\
                            .then_inc(t_free[us[0].b], 1)
                        cur["CT"] = us[0]
                    elif s[0] in ("S", "T"):
                        qt = s[2] // GH
                        attend_act(s, us, Pn, Ln_, PTn, qt + 1, None, s[2])
                    elif s == ("TO", 2, 0) or s == ("TO", 2, 1):
                        act.wait_ge(y_v, DEPTH * KT + it * 2 + s[2] + 1)
                        nc.scalar.activation(y_hl[0][:, 2 * it + s[2], :], y32[:, s[2], :], ACT.Copy).then_inc(y_hi_done, 1)
            for i in range(4):
                cur["i2"], cur["nsq"] = 2 * i, squares(DEPTH) + KT + 2 * i
                cur["last"] = i == 3
                for s in NOUT:
                    take(s)
                    gemm_step(s, cur["u"])
            ln_exp()
            stored()
            norm(None)

        @block.vector
        def _(dve):
            w = Walk()
            cur = {}
            chain = [0]

            def restart():
                dve.sem_clear(chain_v)
                chain[0] = 0

            def link(ins):
                chain[0] += 1
                ins.then_inc(chain_v, 1)
                dve.wait_ge(chain_v, chain[0])

            def settle():
                chain[0] += 1
                dve.sem_inc(chain_v, 1)
                dve.wait_ge(chain_v, chain[0])

            V = nc.vector

            def product(u):
                dve.wait_ge(used, u.n * 2 + 6)

            def take(s):
                us = [w.use(r) for r in takes(s)]
                if s[0] == "u0":
                    cur["u"] = cur[s[1:]] = us[0]
                if s[0] == "u1" and us:
                    cur["e"] = us[0]
                return us

            def sigmoid(e, dst):
                V.tensor_scalar(dst, e_buf[:, e.b, :], 0.5, 0.5, ALU.mult, ALU.add).then_inc(e_done[e.b], 1)

            def store(s, u):
                kind, n = s[1], s[2]
                g = ps[:, u.b, :]
                if kind == "k":
                    dst = kdup if cur["layer"] else kds[n // 2]
                    product(u)
                    link(V.tensor_copy(dst[0:DH, 2 * (n % 2) + 1, :], ps[DH:P, u.b, :]))
                    cur["half"] += 2
                    dve.wait_ge(half_a, cur["half0"] + cur["half"])
                    V.tensor_copy(dst[DH:P, 2 * (n % 2) + 1, :], ps[DH:P, u.b, :]).then_inc(g_free[u.b], 1)
                elif kind == "x2":
                    cur["half"] += 2
                    dve.wait_ge(half_a, cur["half0"] + cur["half"])
                    link(V.tensor_copy(x2[n // 2][0:DH, 2 * (n % 2), :], ps[0:DH, u.b, :]))
                    V.tensor_copy(x2[n // 2][0:DH, 2 * (n % 2) + 1, :], ps[DH:P, u.b, :]).then_inc(g_free[u.b], 1)
                elif kind == "q":
                    product(u)
                    qs = aq if cur["layer"] else qn
                    dve.wait_ge(q_hi, cur["Iq"] * 4 + 2 * n + 2)
                    for i in range(2):
                        half, other = slice(DH * i, DH * (i + 1)), slice(DH * (1 - i), DH * (2 - i))
                        lo = V.scalar_tensor_tensor(qs[other, 2 * n + i, :], ps[half, u.b, :], -DH ** -0.5,
                                                    qs[half, 2 * n + i, :].bitcast(F32), ALU.mult, ALU.subtract)
                        if i == 0:
                            link(lo)
                    lo.then_inc(g_free[u.b], 1)
                elif kind == "conv":
                    if n == 1:
                        dve.wait_ge(e_done[cur["conv_e"].b], cur["conv_e"].m + 2)
                    cur["conv_e"] = cur["e"]
                    product(u)
                    c0 = 5 * n
                    link(V.tensor_scalar(cv[:, :], g, vcur[:, c0 + 3:c0 + 4], vcur[:, c0 + 4:c0 + 5], ALU.mult, ALU.add))
                    for back in (1, 2):
                        link(V.scalar_tensor_tensor(cv[:, back:S], ps[:, u.b, 0:S - back], vcur[:, c0 + 3 - back:c0 + 4 - back],
                                                    cv[:, back:S], ALU.mult, ALU.add))
                    V.scalar_tensor_tensor(cv[:, 3:S], ps[:, u.b, 0:S - 3], vcur[:, c0:c0 + 1], cv[:, 3:S],
                                           ALU.mult, ALU.add).then_inc(g_free[u.b], 1)
                    e = cur["e"]
                    dve.wait_ge(e_conv, cur["I"] * 2 + n + 1)
                    V.scalar_tensor_tensor(mqk[:, n, :], e_buf[:, e.b, :], 1.0, cv[:, :], ALU.add, ALU.mult)\
                        .then_inc(e_done[e.b], 1)
                elif kind in ("mo", "ga", "gb"):
                    dve.wait_ge(g_free[u.b], u.m + 2)
                    sigmoid(cur["e"], sigmo[:, n, :] if kind == "mo" else sig[:, kind == "gb", 2 * cur["it"] + n, :])
                elif kind == "z":
                    e = cur["e"]
                    dve.wait_ge(e_z, cur["it"] * 6 + n + 1)
                    V.scalar_tensor_tensor(sz[:, n, :], e_buf[:, e.b, :], 1.0, g, ALU.add, ALU.mult).then_inc(g_free[u.b], 1)
                    dve.wait_ge(g_free[u.b], u.m + 2)
                    dve.sem_inc(e_done[e.b], 1)
                elif kind == "up":
                    e = cur["e"]
                    dve.wait_ge(g_free[u.b], u.m + 2)
                    V.tensor_tensor(t3[:, n % 2, :], e_buf[:, e.b, :], e_buf[:, e.b, :], ALU.mult)\
                        .then_inc(e_done[e.b], 1)
                    dve.wait_ge(e_done[e.b], e.m + 2)
                    dve.wait_ge(u_hi_done, cur["nu"] + n + 1)
                    V.tensor_tensor(u_hl[1][:, n, :], t3[:, n % 2, :], u_hl[0][:, n, :].bitcast(F32), ALU.subtract)\
                        .then_inc(u_done, 1)
                elif kind == "pm":
                    product(u)
                    V.tensor_tensor(t3[:, n, :], g, sig[:, 0, cur["i2"] + n, :], ALU.mult).then_inc(g_free[u.b], 1)
                elif kind == "pa":
                    product(u)
                    V.tensor_tensor(t3[:, 2, :], g, sig[:, 1, cur["i2"] + n, :], ALU.mult).then_inc(g_free[u.b], 1)
                    dve.wait_ge(g_free[u.b], u.m + 2)
                    V.tensor_tensor(t3[:, n, :], t3[:, n, :], t3[:, 2, :], ALU.add).then_inc(y_v, 1)
                    dve.wait_ge(y_hi_done, cur["ny"] + n + 1)
                    V.tensor_tensor(y_hl[1][:, cur["i2"] + n, :], t3[:, n, :], y_hl[0][:, cur["i2"] + n, :].bitcast(F32),
                                    ALU.subtract).then_inc(y_done, 1)
                elif kind == "res":
                    product(u)
                    V.tensor_tensor(x[:, cur["i2"] + n, :], x[:, cur["i2"] + n, :], g, ALU.add).then_inc(g_free[u.b], 1)
                    add_square(cur["nsq"] + n, n % 2)
                elif kind == "down":
                    product(u)
                    V.tensor_tensor(x[:, n, :], x[:, n, :], g, ALU.add).then_inc(g_free[u.b], 1)
                    add_square(cur["nsq"] + n, n % 2, first=n == 0)

            def add_square(n, b_, first=False, total=ssq[:, :]):
                dve.wait_ge(sq_ready, n + 1)
                if first:
                    V.tensor_copy(total, sq[:, b_, :]).then_inc(sq_used, 1)
                else:
                    dve.wait_ge(sq_used, n)
                    V.tensor_tensor(total, total, sq[:, b_, :], ALU.add).then_inc(sq_used, 1)

            def norm(n, src, gain, mode, factor=None):
                if factor is None:
                    w.use("O1")
                    dve.wait_ge(rs_ready, n + 1)
                    factor = rs[:, :]
                for k in range(KT):
                    if mode[0] == "split":
                        if k >= 3:
                            dve.wait_ge(h_ready[(k - 3) % 2], mode[1] * (KT // 2) + (k - 3) // 2 + 1)
                        V.scalar_tensor_tensor(nt[:, k % 3, :], src[:, k, :], gain(k), factor, ALU.mult, ALU.mult)\
                            .then_inc(nt_ready, 1)
                        if k % 2 == 1:
                            norm_lo(mode[1], k - 1)
                    else:
                        if k >= 3:
                            if k % 2 == 1:
                                dve.wait_ge(x_done, KT + (k - 3) // 2 + 1)
                            else:
                                dve.wait_ge(x_pool, (k - 3) // 2 + 1)
                        V.scalar_tensor_tensor(nt[:, k % 3, :], src[:, k, :], gain(k), factor, ALU.mult, ALU.mult)\
                            .then_inc(nt_ready, 1)
                        if k % 2 == 0:
                            dve.wait_ge(nt_ready, (DEPTH * 2 + 1) * KT + k + 1)
                            V.tensor_tensor(x[:, k, :], x[:, k, :], nt[:, k % 3, :], ALU.add).then_inc(x_done, 1)

            def norm_lo(m, k):
                dve.wait_ge(nhi_done, m * KT + k + 1)
                V.tensor_tensor(hT[1][:, k, :], nt[:, k % 3, :], hT[0][:, k, :].bitcast(F32), ALU.subtract)\
                    .then_inc(h_ready[0], 1)

            def gate_weights_lo(I, gw_raw, gw):
                dve.wait_ge(gwhi_done, I + 1)
                V.tensor_tensor(gw[1][:, :], gw_raw[:, :], gw[0][:, :].bitcast(F32), ALU.subtract).then_inc(gwlo_done, 1)

            def reverse(t, hd, n):
                v = t[:, hd, 0:n]
                return bass.AP(v.tensor, v.offset + n - 1, [v.ap[0], [-1, n]])

            def attend_dve(s, us, bias_t, Lbuf, PTbuf, nk, nP, first, j):
                n = nk * P
                if s[0] == "S":
                    b_ = us[0].b
                    dve.wait_ge(s_ready[b_], us[0].m + 1)
                    if j >= 2:
                        dve.wait_ge(probs, nP + j - 1)
                    settle()
                    V.tensor_tensor_reduce(out=Lbuf[:, j % 2, 0:n], in0=ps[:, 2 + b_, 0:n], in1=reverse(bias_t, j % GH, n),
                                           scale=1.0, scalar=first, op0=ALU.add, op1=ALU.min,
                                           accum_out=st[:, 0, j:j + 1]).then_inc(s_free[b_], 1)
                elif s[0] == "T" and j % 2 == 1:
                    dve.wait_ge(t_ready[us[0].b], us[0].m + 1)
                    V.tensor_copy(PTbuf[:, j % 3, 0:n], ps[:, 4 + us[0].b, 0:n]).then_inc(t_free[us[0].b], 1)

            def weighted_out(us, dst):
                for ob in range(2):
                    dve.wait_ge(o_ready[ob], us[ob].m + 1)
                    V.tensor_tensor(dst[:, 2 * ob:2 * ob + 2, :].rearrange("p q (h d) -> p (q h) d", d=DH),
                                    ps[:, 6 + ob, :].rearrange("p (j d) -> p j d", d=DH),
                                    st[:, 5, 8 * ob:8 * ob + 8].unsqueeze(2).broadcast_to([P, 8, DH]), ALU.mult)\
                        .then_inc(o_free[ob], 1)

            V.memset(ones[:, :], 1.0).then_inc(cst_done, 2)
            us = [w.use(r) for r in ("S", "S", "T", "T")]
            for k in range(4):
                add_square(k, k % 2, first=k == 0)
            dve.wait_ge(s_ready[0], 1)
            V.tensor_copy(bw_sb[:, :], ps[0:16, 2, 0:BW]).then_inc(bw_done, 1)
            add_square(4, 0)
            add_square(5, 1)
            dve.wait_ge(s_ready[1], 1)
            V.tensor_copy(bn_sb[:, 0:S], ps[0:16, 3, 0:S]).then_inc(bn_done, 1)
            for b_ in range(2):
                dve.wait_ge(t_ready[b_], 1)
                V.tensor_copy(bn_sb[:, S + 64 * b_:S + 64 * (b_ + 1)], ps[0:16, 4 + b_, 0:64]).then_inc(bn_done, 1)
            add_square(6, 0)
            add_square(7, 1)
            dve.wait_ge(bw_done, 1)
            dve.wait_ge(bn_done, 3)
            for f in (*s_free, *t_free):
                dve.sem_inc(f, 1)
            dve.wait_ge(cst_in, 16 * 6)

            with w.loop(dve, DEPTH, C_LAYER) as l:
                cur["layer"] = True
                cur["half0"], cur["half"] = l * 4, 0
                restart()
                link(V.tensor_copy(glay[:, :], vl[:, l, :]))
                norm(l * 2, x, lambda k: glay[:, k:k + 1], ("split", l * 2))
                gate_weights_lo(l, gw_raw, gw)
                for s in PRE:
                    us = take(s)
                    if s[0] == "u1":
                        store(s, cur["u"])
                    elif s[0] == "gates":
                        V.memset(grow[:, 10, :], 1.0)
                        V.memset(grow[:, 11, :], 0.0)
                        dve.wait_ge(o_ready[1], us[0].m + 1)
                        link(V.tensor_copy(grow[:, 0, :], ps[32:32 + MH, 7, :]))
                        V.tensor_scalar(grow[:, 1, :], ps[0:MH, 7, :], glay[0:MH, 16:17], None, ALU.add).then_inc(o_free[1], 1)
                        link(V.tensor_scalar(grow[:, 2, :], grow[:, 0, :], glay[0:MH, 17:18], None, ALU.add))
                        V.scalar_tensor_tensor(grow[:, 3, :], grow[:, 2, :], -1.0, grow[:, 2, :], ALU.mult, ALU.min).then_inc(gr_abs, 1)
                        dve.wait_ge(gr_log, l + 1)
                        link(V.scalar_tensor_tensor(grow[:, 6, :], grow[:, 2, :], 0.0, grow[:, 5, :], ALU.min, ALU.subtract))
                        link(V.tensor_tensor_scan(grow[:, 7, :], grow[:, 10, :], grow[:, 6, :], 0.0, ALU.mult, ALU.add))
                        link(V.tensor_tensor(grow[:, 8, :], grow[:, 1, :], grow[:, 7, :], ALU.subtract))
                        link(V.tensor_tensor_scan(grow[:, 0, :], grow[:, 11, :], grow[:, 8, :], 0.0, ALU.add, ALU.max))
                        link(V.tensor_scalar(negM[:, :], grow[:, 0, :], -1.0, None, ALU.mult))
                        V.tensor_tensor(grow[:, 9, :], grow[:, 7, :], grow[:, 0, :], ALU.add).then_inc(grows_done, 1)
                    elif s[0] == "gatesT":
                        t_ = us[0]
                        dve.wait_ge(t_ready[t_.b], t_.m + 1)
                        V.tensor_copy(gtok[:, :, 0:TT], ps[:, 4 + t_.b, 0:TT * MH].rearrange("p (t h) -> p h t", h=MH))\
                            .then_inc(t_free[t_.b], 1)
                        for t_ in us:
                            dve.wait_ge(t_free[t_.b], t_.m + 2)
                        V.memset(vbuf[:, :, MDV:MDV + 1], 1.0)
                with w.loop(dve, NG, per(LOOP)) as it:
                    I = l * NG + it
                    cur["I"], cur["it"], cur["Iq"] = I, it, I
                    restart()
                    V.tensor_copy(gcur[:, :], gtok[:, it, :])
                    link(V.tensor_copy(vcur[:, :], vit[:, I, :]))
                    V.tensor_scalar(st[:, 11, 0:GH], vcur[:, 12:16], -1.0, None, ALU.mult)
                    V.tensor_scalar(selh[:, :], ones[0:MH, :], vcur[0:MH, 16:17], None, ALU.mult).then_inc(staged_v, 1)
                    dve.wait_ge(staged_v, I + 1)
                    for s in LOOP:
                        us = take(s)
                        if s[0] == "u1":
                            store(s, cur["u"])
                        elif s[0] == "bc":
                            cur["bc"] = us[0]
                        elif s[0] == "ST":
                            tt, b_ = s[1], us[0].b
                            cur["ST"] = us[0]
                            if tt == 0:
                                dve.wait_ge(o_ready[0], cur["bc"].m + 1)
                            V.scalar_tensor_tensor(dg[:, :], ps[:, 6, tt * P:(tt + 1) * P], gcur[:, tt:tt + 1], tri[:, :],
                                                   ALU.add, ALU.min).then_inc(dg_done, 1)
                            if tt < TT - 1:
                                dve.wait_ge(d_done, I * (TT - 1) + tt + 1)
                            else:
                                dve.wait_ge(o_free[0], cur["bc"].m + 2)
                            dve.wait_ge(s_ready[b_], us[0].m + 1)
                            V.scalar_tensor_tensor(PTm[:, tt % 2, 0:(tt + 1) * P], ps[:, 2 + b_, 0:(tt + 1) * P],
                                                   0.25 * P ** -0.5, Dm[:, 0:(tt + 1) * P], ALU.mult, ALU.mult)\
                                .then_inc(s_free[b_], 1)
                        elif s[0] == "NUM":
                            dve.wait_ge(t_ready[us[0].b], us[0].m + 1)
                            V.tensor_copy(numsb[:, s[1], 0:MDV + 1], ps[:, 4 + us[0].b, 0:MDV + 1])\
                                .then_inc(t_free[us[0].b], 1)
                            cur["num"] = us[0]
                        elif s == ("hnorm", 0):
                            dve.wait_ge(staged_a, I + 1)
                            dve.wait_ge(s_free[cur["ST"].b], cur["ST"].m + 2)
                            V.tensor_tensor(kg_lo[:, :], kdup[:, it, :], kg_hi[:, :].bitcast(F32), ALU.subtract)\
                                .then_inc(k_lo, 1)
                            dve.wait_ge(t_free[cur["num"].b], cur["num"].m + 2)
                            den = numsb[:, :, MDV:MDV + 1].rearrange("p t o -> p (t o)")
                            link(V.scalar_tensor_tensor(st[:, 4, 0:TT], den, -1.0, den, ALU.mult, ALU.max))
                            link(V.tensor_tensor(st[:, 4, 0:TT], st[:, 4, 0:TT], gcur[:, TT:2 * TT], ALU.max))
                            link(V.reciprocal(st[:, 7, 0:TT], st[:, 4, 0:TT]))
                        elif s == ("hnorm", 1):
                            dve.wait_ge(ss_done, I * TT + TT)
                            link(V.tensor_tensor(st[:, 8, 0:TT], st[:, 6, 0:TT], st[:, 7, 0:TT], ALU.mult))
                            V.tensor_tensor(st[:, 8, 0:TT], st[:, 8, 0:TT], st[:, 7, 0:TT], ALU.mult).then_inc(hn_v, 1)
                        elif s == ("hnorm", 2):
                            dve.wait_ge(hn_a, I + 1)
                            link(V.tensor_tensor(st[:, 8, 4:4 + TT], st[:, 7, 0:TT], st[:, 10, 0:TT], ALU.mult))
                            for t in range(TT):
                                last = V.tensor_scalar(numsb[:, t, 0:MDV], numsb[:, t, 0:MDV], st[:, 8, 4 + t:5 + t], None,
                                                       ALU.mult)
                            last.then_inc(hm_done, 1)
                        elif s[0] in ("S", "T"):
                            if s == ("S", "w", 0):
                                dve.wait_ge(bias_in, I * 16 + 16)
                            qt, hd = s[2] // GH, s[2] % GH
                            attend_dve(s, us, bias, L, PT, min(qt + 1, 2), I * 16, st[:, 11, hd:hd + 1], s[2])
                        elif s[0] == "TH":
                            dve.wait_ge(t_ready[us[0].b], us[0].m + 1)
                            V.scalar_tensor_tensor(hm32[:, 2 * it + s[1], :], ps[:, 4 + us[0].b, :], vcur[:, 10 + s[1]:11 + s[1]],
                                                   sigmo[:, s[1], :], ALU.mult, ALU.mult).then_inc(t_free[us[0].b], 1)
                        elif s[0] == "ostat":
                            dve.wait_ge(probs, I * 16 + 16)
                            V.tensor_tensor(st[:, 2, :].rearrange("p (q h) -> p q h", h=GH),
                                            st[:, 0, :].rearrange("p (q h) -> p q h", h=GH),
                                            vcur[:, 12:16].unsqueeze(1).broadcast_to([P, TT, GH]), ALU.add)\
                                .then_inc(t1_done, 1)
                        elif s[0] == "otail":
                            dve.wait_ge(es_done, I + 1)
                            link(V.tensor_tensor(st[:, 4, :], st[:, 1, :], st[:, 3, :], ALU.add))
                            link(V.reciprocal(st[:, 5, :], st[:, 4, :]))
                            weighted_out(us, ao)
                for src, hl, first in ((hm32, hm_hl, 0), (ha32, ha_hl, KT)):
                    for k in range(KT):
                        dve.wait_ge(mhi, l * 2 * KT + first + k + 1)
                        V.tensor_tensor(hl[1][:, k, :], src[:, k, :], hl[0][:, k, :].bitcast(F32), ALU.subtract)\
                            .then_inc(mlo, 1)
                with w.loop(dve, 4, per(MIX)) as i:
                    cur["ny"], cur["i2"] = l * KT + i * 2, i * 2
                    for s in MIX:
                        take(s)
                        if s[0] == "u1":
                            store(s, cur["u"])
                link(V.memset(ssq[:, :], 0.0))
                with w.loop(dve, 4, per(WOUT)) as i:
                    cur["nsq"], cur["i2"] = squares(l) + i * 2, i * 2
                    for s in WOUT:
                        take(s)
                        if s[0] == "u1":
                            store(s, cur["u"])
                norm(l * 2 + 1, x, lambda k: glay[:, 8 + k:9 + k], ("split", l * 2 + 1))
                with w.loop(dve, 4, per(MLP)) as c:
                    cur["nu"], cur["nsq"] = l * 4 * KT + c * KT, squares(l) + KT + c * KT
                    for s in MLP:
                        take(s)
                        if s[0] == "u1":
                            store(s, cur["u"])

            cur["layer"] = False
            cur["half0"], cur["half"] = DEPTH * 4, 0
            restart()
            for k in range(KT):
                add_square(squares(DEPTH) + k, k % 2, first=k == 0, total=gsum)
            w.use("O1")
            use = w.use("O1")
            link(V.tensor_tensor(glay[:, 0:8], vn[:, 0:8], vn[:, 8:16], ALU.mult))
            dve.wait_ge(rs_ready, DEPTH * 2 + 1)
            dve.wait_ge(o_ready[1], use.m + 1)
            V.scalar_tensor_tensor(ms2, ps[:, 7, :], 1.0 / D, rs[:, :], ALU.mult, ALU.mult).then_inc(o_free[1], 1)
            dve.wait_ge(o_free[1], use.m + 2)
            V.tensor_tensor(ms2, ms2, rs[:, :], ALU.mult).then_inc(ms2_done, 1)
            link(V.tensor_copy(tn[:, :], rs[:, :]))
            dve.wait_ge(rs_ready, DEPTH * 2 + 2)
            link(V.tensor_tensor(rs12, rs[:, :], rs2, ALU.mult))
            norm(DEPTH * 2 + 1, x, lambda k: glay[:, k:k + 1], ("split", DEPTH * 2), factor=rs12)
            gate_weights_lo(DEPTH, gwn_raw, gwn)
            V.memset(kcd[:, :, NC:CP], 0.0)
            V.memset(x2[0][:, 4, :], 0.0)
            V.memset(x2[1][:, 4, :], 0.0)
            V.memset(x2[0][DH:P, 0:4, S - 1:S], 0.0)
            link(V.memset(x2[1][DH:P, 0:4, S - 1:S], 0.0))
            dve.wait_ge(pos_in_s, 16)
            for kv in range(2):
                V.tensor_copy(x2[kv][:, 4, 0:32:2], posb[:, kv, :]).then_inc(x2_pos, 1)
            for s in NPRE:
                us = take(s)
                if s[0] == "u1":
                    store(s, cur["u"])
                elif s[0] == "ngates":
                    dve.wait_ge(o_free[1], us[0].m + 2)
                    V.tensor_scalar(grow2[:, 1, :], grow2[:, 0, :], 0.25, 0.25, ALU.mult, ALU.add).then_inc(grows_done, 1)
                elif s[0] == "ngatesT":
                    for which in range(2):
                        t_ = us[which]
                        dve.wait_ge(t_ready[t_.b], t_.m + 1)
                        for t in range(2):
                            for b_ in range(3):
                                tk = 2 * which + t
                                last = V.tensor_copy(
                                    gates[:, :, b_, tk * GH:(tk + 1) * GH],
                                    ps[:, 4 + t_.b, t * 48 + b_ * 16:t * 48 + (b_ + 1) * 16].rearrange("p (g d) -> p g d", g=NG))
                        last.then_inc(t_free[t_.b], 1)
                elif s[0] == "cmpbias":
                    link(V.memset(bcmp[:, :, :, :], BIG))
                    dve.wait_ge(o_ready[0], us[0].m + 1)
                    for qt in range(TT):
                        for g in range(NG):
                            n = min(NC, 8 * qt + 7)
                            v = ps[:, 6, (8 * qt + 6) * 16 + g * GH:(8 * qt + 6) * 16 + g * GH + 1]
                            last = V.tensor_copy(bcmp[:, g, qt * GH:(qt + 1) * GH, 0:n],
                                                 bass.AP(v.tensor, v.offset, [v.ap[0], [1, GH], [-16, n]]))
                    last.then_inc(o_free[0], 1)
                elif s[0] == "hidden":
                    for k in range(KT):
                        V.scalar_tensor_tensor(x[:, k, :], x[:, k, :], vn[:, k:k + 1], tn[:, :], ALU.mult, ALU.mult)\
                            .then_inc(x_done, 1)
                    for kv in range(2):
                        dve.wait_ge(o_ready[kv], us[kv].m + 1)
                        for m in range(2):
                            pre = ps[:, 6 + kv, m * 256:m * 256 + 5 * NC]
                            last = V.tensor_scalar(hid[:, 2 * kv + m, 0:NG * NC], pre[:, 0:NG * NC],
                                                   pre[:, NG * NC:NG * NC + 1], None, ALU.add)
                            last.then_inc(cmp_pre if m == 0 else o_free[kv], 1)
                    dve.wait_ge(o_free[1], us[1].m + 2)
                    dve.sem_inc(cmp_pre, 2)
                    dve.wait_ge(cmp_exp, 1)
                    link(V.tensor_scalar(ehid[:, :, 0:NG * NC], ehid[:, :, 0:NG * NC], 0.5, 0.5, ALU.mult, ALU.add))
                    V.tensor_tensor(hid[:, :, 0:NG * NC], hid[:, :, 0:NG * NC], ehid[:, :, 0:NG * NC], ALU.mult)\
                        .then_inc(hid_done, 1)
                elif s[0] == "compress":
                    dve.wait_ge(t_ready[1], us[1].m + 1)
                    V.tensor_copy(vc[:, :, :], ps[0:NC, 5, 0:NG * DH].rearrange("p (g d) -> p g d", g=NG))\
                        .then_inc(t_free[1], 1)
                    dve.wait_ge(t_free[1], us[1].m + 2)
            w.flush()
            cj = lambda t: t[:, 0, :].rearrange("p (j c) -> p j c", c=CP)
            with w.loop(dve, NG, per(NLOOP)) as it:
                cur["it"], cur["Iq"] = it, DEPTH * NG + it
                restart()
                link(V.tensor_copy(gat[:, :, :], gates[:, it, :, :]))
                for s in NLOOP:
                    us = take(s)
                    if s[0] == "u1":
                        store(s, cur["u"])
                    elif s[0] == "klo":
                        dve.wait_ge(staged_a, DEPTH * NG + it + 1)
                        link(V.tensor_tensor(kc_hl[1][:, :], kcd[:, it, :], kc_hl[0][:, :].bitcast(F32), ALU.subtract))
                        V.tensor_tensor(kn_hl[1][:, :], kds[0][:, it, :], kn_hl[0][:, :].bitcast(F32), ALU.subtract)\
                            .then_inc(k_lo, 1)
                    elif s[0] == "kf":
                        dve.wait_ge(k_hi, it + 1)
                        V.tensor_tensor(kn_hl[1][:, :], kds[1][:, it, :], kn_hl[0][:, :].bitcast(F32), ALU.subtract)\
                            .then_inc(k_lo, 1)
                    elif s[0] == "CS":
                        for b_ in range(2):
                            dve.wait_ge(s_ready[b_], us[b_].m + 1)
                            V.tensor_tensor(cj(Ln_)[:, b_::2, 0:NC],
                                            ps[:, 2 + b_, 0:8 * CP].rearrange("p (j c) -> p j c", c=CP)[:, :, 0:NC],
                                            bcmp[:, it, b_::2, 0:NC], ALU.add).then_inc(s_free[b_], 1)
                        dve.wait_ge(s_free[1], us[1].m + 2)
                        link(V.tensor_reduce(st[:, 0, :], cj(Ln_)[:, :, 0:NC], AX.X, ALU.min))
                        V.tensor_tensor(cj(Ln_)[:, :, 0:NC], cj(Ln_)[:, :, 0:NC],
                                        st[:, 0, :].unsqueeze(2).broadcast_to([P, 16, NC]), ALU.subtract).then_inc(cs_sub, 1)
                    elif s[0] in ("S", "T"):
                        if s == ("S", "s", 0):
                            dve.wait_ge(bias_in, (DEPTH * NG + it) * 16 + 16)
                        br = 0 if s[1] == "s" else 1
                        attend_dve(s, us, biasn, Ln_, PTn, s[2] // GH + 1, (DEPTH * NG + it * 2 + br) * 16, 3e38, s[2])
                    elif s[0] == "ostat":
                        br = "csf".index(s[1])
                        if br == 0:
                            dve.wait_ge(cs_exp, it + 1)
                            link(V.tensor_reduce(st[:, 1, :], cj(Pn)[:, :, 0:NC], AX.X, ALU.add))
                        else:
                            dve.wait_ge(probs, (DEPTH * NG + it * 2 + br) * 16)
                        link(V.reciprocal(st[:, 4, :], st[:, 1, :]))
                        link(V.tensor_tensor(st[:, 5, :], st[:, 4, :], gat[:, br, :], ALU.mult))
                        if br == 0:
                            link(V.tensor_scalar(st[:, 5, 0:GH], st[:, 5, 0:GH], late[:, :], None, ALU.mult))
                    elif s[0] == "otail":
                        weighted_out(us, aon)
                    elif s[0] == "TO":
                        br, n = s[1], s[2]
                        t = us[0]
                        dve.wait_ge(t_ready[t.b], t.m + 1)
                        V.tensor_tensor(y32[:, n, :] if br == 0 else tn[:, :], ps[:, 4 + t.b, :], sz[:, 2 * br + n, :],
                                        ALU.mult).then_inc(t_free[t.b], 1)
                        dve.wait_ge(t_free[t.b], t.m + 2)
                        if br == 1:
                            link(V.tensor_tensor(y32[:, n, :], y32[:, n, :], tn[:, :], ALU.add))
                        if br == 2:
                            V.tensor_tensor(y32[:, n, :], y32[:, n, :], tn[:, :], ALU.add).then_inc(y_v, 1)
                            dve.wait_ge(y_hi_done, DEPTH * KT + it * 2 + n + 1)
                            V.tensor_tensor(y_hl[1][:, 2 * it + n, :], y32[:, n, :],
                                            y_hl[0][:, 2 * it + n, :].bitcast(F32), ALU.subtract).then_inc(y_done, 1)
            for k in range(KT):
                add_square(squares(DEPTH) + KT + k, k % 2, first=k == 0)
            norm(DEPTH * 2 + 2, y2, lambda k: vn[:, 16 + k:17 + k], ("add",))


def _bucket(n):
    n = np.maximum(n, 0)
    large = 16 + (np.log(np.maximum(n, 1) / 16) / np.log(128 / 16) * 16).astype(np.int32)
    return np.where(n < 16, n, np.minimum(large, 31))


def _onehot(dist, valid):
    a = np.zeros((33, len(dist)), np.float32)
    a[_bucket(dist), np.arange(len(dist))] = np.where(valid, -1.0, 0.0)
    a[32] = np.where(valid, 0.0, BIG)
    return a


def _units(w):
    k, n = w.shape
    a = np.asarray(w).reshape(k // D, KT, P, n // P, P)
    return a.transpose(0, 3, 2, 1, 4).reshape(-1, P, KT * P)


def _pad(cols, width=P):
    return np.concatenate([cols, np.zeros((cols.shape[0], width - cols.shape[1]), np.float32)], 1)


def kernel(**inp):
    import concourse.bacc as bacc
    from concourse.bass_utils import run_bass_kernel_spmd as run

    inp = {k: np.asarray(v) for k, v in inp.items()}
    per_unit, gate_w, v_it, v_l = [], [], [], []
    for l in range(DEPTH):
        wi = inp["w_in"][l]
        o = np.cumsum([0, 1024, 1024, 1024, 4, 4, 1024, 256, 256, 1024, 1024])
        U = {n: _units(wi[:, o[i]:o[i + 1]]) for n, i in (("mqk", 0), ("mv", 1), ("mo", 2), ("aq", 5), ("ak", 6), ("av", 7),
                                                         ("ga", 8), ("gb", 9))}
        gate_w.append(_units(_pad(np.concatenate([_pad(wi[:, o[3]:o[4]], 32), wi[:, o[4]:o[5]]], 1)))[0])
        per_unit += [U["ak"], U["av"]]
        for h in range(NG):
            per_unit += [U["mqk"][[h]], U["mqk"][[4 + h]]] + [U[n][2 * h:2 * h + 2] for n in ("mv", "aq", "mo", "ga", "gb")]
        pm, pa = _units(inp["w_branch_m"][l]), _units(inp["w_branch_a"][l])
        per_unit += [np.stack([pm, pa], 1).reshape(-1, P, KT * P), _units(inp["w_out"][l])]
        up, down = _units(inp["w_up"][l]), _units(inp["w_down"][l])
        for c in range(4):
            per_unit += [up[c * KT:(c + 1) * KT], down[c * KT:(c + 1) * KT]]
        cw, cb = inp["conv_w"][l], inp["conv_b"][l]
        for h in range(NG):
            v = np.zeros((P, VIT), np.float32)
            for n, c in ((0, h), (1, 4 + h)):
                v[:, 5 * n:5 * n + 4] = cw[:, c * P:(c + 1) * P].T
                v[:, 5 * n + 4] = cb[c * P:(c + 1) * P]
            v[:, 10:12] = inp["mlstm_norm_g"][l][2 * h * P:(2 * h + 2) * P].reshape(2, P).T
            v[:, 12:16] = inp["attn_sinks"][l][GH * h:GH * (h + 1)]
            v[h, 16] = 1.0
            v_it.append(v)
        v = np.zeros((P, VL), np.float32)
        v[:, 0:8] = inp["norm_mix_g"][l].reshape(KT, P).T
        v[:, 8:16] = inp["norm_mlp_g"][l].reshape(KT, P).T
        v[0:MH, 16], v[0:MH, 17] = inp["b_igate"][l], inp["b_fgate"][l]
        v_l.append(v)
    wi = inp["nsa_w_in_2"][0]
    kv = _units(wi[:, 1024:2560])
    z = _units(wi[:, 2608:5680]).reshape(3, NG, 2, P, KT * P)
    q = _units(wi[:, 0:1024])
    per_unit += [kv[0:6], kv[6:8], kv[8:10], kv[10:12]]
    for g in range(NG):
        per_unit += [q[2 * g:2 * g + 2], z[:, g].reshape(6, P, KT * P)]
    per_unit.append(_units(inp["nsa_w_out_2"][0]))
    gate_w.append(_units(_pad(wi[:, 2560:2608]))[0])

    dist_w, dist_n = np.arange(BW) - 127, np.arange(BN) - 127
    pairs = lambda a: a.reshape(16, P, -1).transpose(1, 0, 2)
    table = lambda a: np.concatenate([a, np.ones((1, 16), np.float32)], 0)
    s_ = np.arange(P)
    data = {
        "w_all": np.concatenate(per_unit, 0),
        "wg_all": np.stack(gate_w),
        "vec_it": np.stack(v_it, 1),
        "vec_l": np.stack(v_l, 1),
        "vec_n": np.concatenate([inp[n].reshape(KT, P).T for n in ("final_norm_g", "pre_norm_gain_2", "post_norm_gain_2")], 1),
        "ident_in": np.eye(P, dtype=np.float32),
        "tri_in": np.where(s_[:, None] <= s_[None, :], 0.0, -BIG),
        "onehot_w": _onehot(dist_w, (dist_w >= 0) & (dist_w < P)),
        "onehot_n": _onehot(dist_n, dist_n >= 0),
        "tab_w": table(inp["rel_bias"]),
        "tab_n": table(inp["rel_bias_table_2"]),
        "late_in": (s_ >= 31)[:, None],
        "x_in": inp["x"][0].T,
        "w1_in": np.stack([pairs(inp["nsa_cmp_k_w1_2"][0]), pairs(inp["nsa_cmp_v_w1_2"][0])]),
        "w2_in": np.stack([inp[n][0].reshape(2, P, DH).transpose(1, 0, 2) for n in ("nsa_cmp_k_w2_2", "nsa_cmp_v_w2_2")], 1),
        "pos_in": np.stack([inp[n][0].reshape(16, P).T for n in ("nsa_cmp_k_pos_2", "nsa_cmp_v_pos_2")], 1),
    }
    data = {k: np.ascontiguousarray(v, np.float32) for k, v in data.items()}
    assert data["w_all"].shape[0] == UNITS, data["w_all"].shape
    nc = bacc.Bacc("TRN2", target_bir_lowering=False, num_devices=1)
    aps = {k: nc.dram_tensor(k, v.shape, F32, kind="ExternalInput").ap() for k, v in data.items()}
    aps["scr_w"] = nc.dram_tensor("scr_w", [16, BW], F32).ap()
    aps["scr_n"] = nc.dram_tensor("scr_n", [16, BN], F32).ap()
    aps["out"] = nc.dram_tensor("out", [D, S], F32, kind="ExternalOutput").ap()
    two_layers_and_nsa(nc, **aps)
    got = run(nc, [data], core_ids=[0]).results[0]["out"]
    return np.ascontiguousarray(got.T)[None]
```
